# Optimizing a Trainium2 kernel written in Bass

```python
import math
import numpy as np
import jax
import jax.numpy as jnp
from jax import lax

D_MODEL = 2048
BATCH = 1
SEQ = 256
DEPTH = 2

PLE_DIM = 256
EPS = 1e-6
QBLK = 128
NEG_INF = -1e30
BIG = 1e6

NSA_HEADS = 8
NSA_KV = 2
NSA_GROUP = NSA_HEADS // NSA_KV
NSA_HD = 128
CMP_STRIDE = 16
CMP_LEN = 2 * CMP_STRIDE
SEL_LEN = 64
SEL_TOPK = 16
WIN = 512
N_BRANCH = 3

DIFF_HEADS = 8
DIFF_QK = 64
DIFF_V = 2 * DIFF_QK

A_Q = NSA_HEADS * NSA_HD
A_KV = NSA_KV * NSA_HD
A_GATE = NSA_HEADS * N_BRANCH
B_QK = DIFF_HEADS * 2 * DIFF_QK
B_V = DIFF_HEADS * DIFF_V
ATTN_IN = A_Q + 6 * A_KV + A_GATE + 2 * B_QK + B_V
MIX_OUT = A_Q + B_V

LRU_W = D_MODEL
LRU_BLOCKS = 8
LRU_BW = LRU_W // LRU_BLOCKS
CONV_W = 4
LRU_C = 8.0

D_FF = -(-8 * D_MODEL // (3 * 256)) * 256

N_ATTN = (DEPTH + 1) // 2
N_REC = DEPTH // 2

kernel_name = "hybrid_nsa_diff_rglru_trunk"

def rmsnorm(x, g):
    x32 = x.astype(jnp.float32)
    y = x32 * lax.rsqrt(jnp.mean(x32 * x32, axis=-1, keepdims=True) + EPS)
    return (y * g.astype(jnp.float32)).astype(x.dtype)

def masked_softmax(s, valid):
    s = jnp.where(valid, s.astype(jnp.float32), NEG_INF)
    return jax.nn.softmax(s, axis=-1) * valid

def compress(kv, pe, w1, w2):
    b, s, h, d = kv.shape
    ch = kv.reshape(b, s // CMP_STRIDE, CMP_STRIDE, h, d)
    lo = ch[:, :-1] + pe[:CMP_STRIDE, None, :]
    hi = ch[:, 1:] + pe[CMP_STRIDE:, None, :]
    z = (jnp.einsum('bnlhd,lde->bnhe', lo, w1[:CMP_STRIDE])
         + jnp.einsum('bnlhd,lde->bnhe', hi, w1[CMP_STRIDE:]))
    return jnp.einsum('bnhe,ef->bnhf', jax.nn.gelu(z), w2)

def cmp_to_sel_matrix(n_cmp, n_sel):
    c0 = np.arange(n_cmp)[:, None] * CMP_STRIDE
    s0 = np.arange(n_sel)[None, :] * SEL_LEN
    ov = np.minimum(c0 + CMP_LEN, s0 + SEL_LEN) - np.maximum(c0, s0)
    return jnp.asarray(np.clip(ov, 0, None) / CMP_LEN, dtype=jnp.float32)

def nsa_attention(q, kc, vc, ks, vs, kw, vw, gates):
    b, s = q.shape[:2]
    n_cmp = kc.shape[1]
    n_sel = s // SEL_LEN
    topk = min(SEL_TOPK, n_sel)
    scale = NSA_HD ** -0.5
    sel_map = cmp_to_sel_matrix(n_cmp, n_sel)
    cmp_end = jnp.arange(n_cmp) * CMP_STRIDE + CMP_LEN - 1
    blk = jnp.arange(n_sel)
    ks_b = ks.reshape(b, n_sel, SEL_LEN, NSA_KV, NSA_HD).transpose(0, 3, 1, 2, 4)
    vs_b = vs.reshape(b, n_sel, SEL_LEN, NSA_KV, NSA_HD).transpose(0, 3, 1, 2, 4)
    kw_p = jnp.pad(kw, ((0, 0), (WIN, 0), (0, 0), (0, 0)))
    vw_p = jnp.pad(vw, ((0, 0), (WIN, 0), (0, 0), (0, 0)))
    bi = jnp.arange(b)[:, None, None, None]
    hi = jnp.arange(NSA_KV)[None, :, None, None]

    def block(qb):
        start = qb * QBLK
        t = start + jnp.arange(QBLK)
        qq = lax.dynamic_slice_in_dim(q, start, QBLK, 1) * scale
        gg = jax.nn.sigmoid(lax.dynamic_slice_in_dim(gates, start, QBLK, 1).astype(jnp.float32))
        s_c = jnp.einsum('bqhgd,bnhd->bhgqn', qq, kc)
        p_c = masked_softmax(s_c, cmp_end[None, :] <= t[:, None])
        o_c = jnp.einsum('bhgqn,bnhd->bqhgd', p_c, vc)
        imp = jnp.einsum('bhgqn,nj->bhqj', p_c, sel_map)
        cur = (t // SEL_LEN)[:, None]
        forced = (blk == 0) | (blk == cur) | (blk == cur - 1)
        imp = jnp.where(blk > cur, -BIG, jnp.where(forced, BIG, imp))
        _, idx = lax.top_k(imp, topk)
        kg = ks_b[bi, hi, idx]
        vg = vs_b[bi, hi, idx]
        pos = idx[..., None] * SEL_LEN + jnp.arange(SEL_LEN)
        valid_s = (pos <= t[:, None, None]).reshape(b, NSA_KV, 1, QBLK, topk * SEL_LEN)
        s_s = jnp.einsum('bqhgd,bhqkld->bhgqkl', qq, kg).reshape(b, NSA_KV, NSA_GROUP, QBLK, topk * SEL_LEN)
        p_s = masked_softmax(s_s, valid_s).reshape(b, NSA_KV, NSA_GROUP, QBLK, topk, SEL_LEN)
        o_s = jnp.einsum('bhgqkl,bhqkld->bqhgd', p_s, vg)
        kwb = lax.dynamic_slice_in_dim(kw_p, start, QBLK + WIN, 1)
        vwb = lax.dynamic_slice_in_dim(vw_p, start, QBLK + WIN, 1)
        kpos = start - WIN + jnp.arange(QBLK + WIN)
        dlt = t[:, None] - kpos[None, :]
        valid_w = (dlt >= 0) & (dlt < WIN) & (kpos[None, :] >= 0)
        s_w = jnp.einsum('bqhgd,bkhd->bhgqk', qq, kwb)
        p_w = masked_softmax(s_w, valid_w)
        o_w = jnp.einsum('bhgqk,bkhd->bqhgd', p_w, vwb)
        o = gg[..., 0:1] * o_c + gg[..., 1:2] * o_s + gg[..., 2:3] * o_w
        return o.reshape(b, QBLK, A_Q).astype(q.dtype)

    out = lax.map(block, jnp.arange(s // QBLK))
    return out.transpose(1, 0, 2, 3).reshape(b, s, A_Q)

def diff_attention(q, k, v, lam):
    b, s = q.shape[:2]
    scale = DIFF_QK ** -0.5
    kpos = jnp.arange(s)

    def block(qb):
        start = qb * QBLK
        t = start + jnp.arange(QBLK)
        qq = lax.dynamic_slice_in_dim(q, start, QBLK, 1) * scale
        sc = jnp.einsum('bqhcd,bkhcd->cbhqk', qq, k)
        pr = masked_softmax(sc, kpos[None, :] <= t[:, None])
        a = pr[0] - lam * pr[1]
        return jnp.einsum('bhqk,bkhd->bqhd', a, v).astype(v.dtype)

    out = lax.map(block, jnp.arange(s // QBLK))
    return out.transpose(1, 0, 2, 3, 4).reshape(b, s, DIFF_HEADS, DIFF_V)

def attn_mixer(xn, layer_idx, w_in, pe_k, w1_k, w2_k, pe_v, w1_v, w2_v,
               lq1, lk1, lq2, lk2, subln, w_out):
    b, s, _ = xn.shape
    proj = xn @ w_in
    o1 = A_Q
    o2 = o1 + 6 * A_KV
    o3 = o2 + A_GATE
    o4 = o3 + B_QK
    o5 = o4 + B_QK
    q_a, kv_a, g_a, q_b, k_b, v_b = jnp.split(proj, [o1, o2, o3, o4, o5], axis=-1)
    kv_a = kv_a.reshape(b, s, 6, NSA_KV, NSA_HD)
    kc = compress(kv_a[:, :, 0], pe_k, w1_k, w2_k)
    vc = compress(kv_a[:, :, 1], pe_v, w1_v, w2_v)
    o_a = nsa_attention(q_a.reshape(b, s, NSA_KV, NSA_GROUP, NSA_HD), kc, vc,
                        kv_a[:, :, 2], kv_a[:, :, 3], kv_a[:, :, 4], kv_a[:, :, 5],
                        g_a.reshape(b, s, NSA_KV, NSA_GROUP, N_BRANCH))
    lam_init = 0.8 - 0.6 * math.exp(-0.3 * layer_idx)
    f32 = jnp.float32
    lam = (jnp.exp(jnp.sum(lq1.astype(f32) * lk1.astype(f32)))
           - jnp.exp(jnp.sum(lq2.astype(f32) * lk2.astype(f32))) + lam_init)
    o_b = diff_attention(q_b.reshape(b, s, DIFF_HEADS, 2, DIFF_QK),
                         k_b.reshape(b, s, DIFF_HEADS, 2, DIFF_QK),
                         v_b.reshape(b, s, DIFF_HEADS, DIFF_V), lam)
    o_b = rmsnorm(o_b, subln) * (1.0 - lam_init)
    o = jnp.concatenate([o_a, o_b.reshape(b, s, B_V)], axis=-1)
    return o @ w_out

def rglru_mixer(xn, w_in, conv_w, conv_b, wa, ba, wx, bx, lam_p, w_out):
    b, s, _ = xn.shape
    xb, yb = jnp.split(xn @ w_in, 2, axis=-1)
    y = jax.nn.gelu(yb)
    xc = lax.conv_general_dilated(xb, conv_w[:, None, :], window_strides=(1,),
                                  padding=[(CONV_W - 1, 0)],
                                  dimension_numbers=('NWC', 'WIO', 'NWC'),
                                  feature_group_count=LRU_W) + conv_b
    xg = xc.reshape(b, s, LRU_BLOCKS, LRU_BW)
    r = jax.nn.sigmoid(jnp.einsum('bsnd,nde->bsne', xg, wa).reshape(b, s, LRU_W) + ba)
    i = jax.nn.sigmoid(jnp.einsum('bsnd,nde->bsne', xg, wx).reshape(b, s, LRU_W) + bx)
    log_a = -LRU_C * r.astype(jnp.float32) * jax.nn.softplus(-lam_p.astype(jnp.float32))
    a = jnp.exp(log_a)
    u = jnp.sqrt(-jnp.expm1(2.0 * log_a)) * (i * xc).astype(jnp.float32)

    def comb(e1, e2):
        a1, b1 = e1
        a2, b2 = e2
        return a1 * a2, a2 * b1 + b2

    _, h = lax.associative_scan(comb, (a, u), axis=1)
    return (h.astype(xn.dtype) * y) @ w_out

def swiglu(xn, wg, wu, wd):
    return (jax.nn.silu(xn @ wg) * (xn @ wu)) @ wd

def _normal(key, shape, scale):
    return jax.random.normal(key, shape, jnp.float32) * scale

def setup_inputs(seed: int = 0) -> dict:
    key = jax.random.key(seed)
    ks = jax.random.split(key, 33)
    na, nr = N_ATTN, N_REC
    out_scale = (2 * DEPTH) ** -0.5
    a0 = jax.random.uniform(ks[26], (nr, LRU_W), jnp.float32, 0.9, 0.999)
    return {
        "x": _normal(ks[0], (BATCH, SEQ, D_MODEL), 1.0),
        "p": _normal(ks[1], (DEPTH, BATCH, SEQ, PLE_DIM), 1.0),
        "g_mix": 1.0 + _normal(ks[2], (DEPTH, D_MODEL), 0.02),
        "g_ffn": 1.0 + _normal(ks[3], (DEPTH, D_MODEL), 0.02),
        "g_ple": 1.0 + _normal(ks[4], (DEPTH, D_MODEL), 0.02),
        "g_final": 1.0 + _normal(ks[5], (D_MODEL,), 0.02),
        "w_in_attn": _normal(ks[6], (na, D_MODEL, ATTN_IN), D_MODEL ** -0.5),
        "cmp_pe_k": _normal(ks[7], (na, CMP_LEN, NSA_HD), 0.5),
        "cmp_w1_k": _normal(ks[8], (na, CMP_LEN, NSA_HD, NSA_HD), (CMP_LEN * NSA_HD) ** -0.5),
        "cmp_w2_k": _normal(ks[9], (na, NSA_HD, NSA_HD), NSA_HD ** -0.5),
        "cmp_pe_v": _normal(ks[10], (na, CMP_LEN, NSA_HD), 0.5),
        "cmp_w1_v": _normal(ks[11], (na, CMP_LEN, NSA_HD, NSA_HD), (CMP_LEN * NSA_HD) ** -0.5),
        "cmp_w2_v": _normal(ks[12], (na, NSA_HD, NSA_HD), NSA_HD ** -0.5),
        "diff_lq1": _normal(ks[13], (na, DIFF_QK), 0.1),
        "diff_lk1": _normal(ks[14], (na, DIFF_QK), 0.1),
        "diff_lq2": _normal(ks[15], (na, DIFF_QK), 0.1),
        "diff_lk2": _normal(ks[16], (na, DIFF_QK), 0.1),
        "diff_subln": 1.0 + _normal(ks[17], (na, DIFF_HEADS, DIFF_V), 0.02),
        "w_out_attn": _normal(ks[18], (na, MIX_OUT, D_MODEL), MIX_OUT ** -0.5 * out_scale),
        "w_in_rec": _normal(ks[19], (nr, D_MODEL, 2 * LRU_W), D_MODEL ** -0.5),
        "conv_w": _normal(ks[20], (nr, CONV_W, LRU_W), CONV_W ** -0.5),
        "conv_b": _normal(ks[21], (nr, LRU_W), 0.01),
        "lru_wa": _normal(ks[22], (nr, LRU_BLOCKS, LRU_BW, LRU_BW), LRU_BW ** -0.5),
        "lru_ba": _normal(ks[23], (nr, LRU_W), 0.01),
        "lru_wx": _normal(ks[24], (nr, LRU_BLOCKS, LRU_BW, LRU_BW), LRU_BW ** -0.5),
        "lru_bx": _normal(ks[25], (nr, LRU_W), 0.01),
        "lru_lambda": jnp.log(a0) - jnp.log1p(-a0),
        "w_out_rec": _normal(ks[27], (nr, LRU_W, D_MODEL), LRU_W ** -0.5 * out_scale),
        "w_ffn_gate": _normal(ks[28], (DEPTH, D_MODEL, D_FF), D_MODEL ** -0.5),
        "w_ffn_up": _normal(ks[29], (DEPTH, D_MODEL, D_FF), D_MODEL ** -0.5),
        "w_ffn_down": _normal(ks[30], (DEPTH, D_FF, D_MODEL), D_FF ** -0.5 * out_scale),
        "w_ple_proj": _normal(ks[31], (DEPTH, PLE_DIM, D_MODEL), PLE_DIM ** -0.5),
        "w_ple_gate": _normal(ks[32], (DEPTH, D_MODEL, D_MODEL), D_MODEL ** -0.5),
    }

def reference(x, p, g_mix, g_ffn, g_ple, g_final, w_in_attn, cmp_pe_k, cmp_w1_k, cmp_w2_k,
              cmp_pe_v, cmp_w1_v, cmp_w2_v, diff_lq1, diff_lk1, diff_lq2, diff_lk2, diff_subln,
              w_out_attn, w_in_rec, conv_w, conv_b, lru_wa, lru_ba, lru_wx, lru_bx, lru_lambda,
              w_out_rec, w_ffn_gate, w_ffn_up, w_ffn_down, w_ple_proj, w_ple_gate):
    h = x
    for i in range(DEPTH):
        xn = rmsnorm(h, g_mix[i])
        j = i // 2
        if i % 2 == 0:
            mix = attn_mixer(xn, i, w_in_attn[j], cmp_pe_k[j], cmp_w1_k[j], cmp_w2_k[j],
                             cmp_pe_v[j], cmp_w1_v[j], cmp_w2_v[j], diff_lq1[j], diff_lk1[j],
                             diff_lq2[j], diff_lk2[j], diff_subln[j], w_out_attn[j])
        else:
            mix = rglru_mixer(xn, w_in_rec[j], conv_w[j], conv_b[j], lru_wa[j], lru_ba[j],
                              lru_wx[j], lru_bx[j], lru_lambda[j], w_out_rec[j])
        h = h + mix
        h = h + swiglu(rmsnorm(h, g_ffn[i]), w_ffn_gate[i], w_ffn_up[i], w_ffn_down[i])
        gate = jax.nn.sigmoid(rmsnorm(h, g_ple[i]) @ w_ple_gate[i])
        h = h + gate * (p[i] @ w_ple_proj[i])
    return rmsnorm(h, g_final)


_drawn_inputs = setup_inputs


def setup_inputs(seed=0):
    import zlib

    import numpy as np

    out = dict(_drawn_inputs(seed))
    spreads = {}
    factors = {'g_mix': 5.509,
     'g_ffn': 6.037,
     'g_ple': 64.0,
     'g_final': 7.513,
     'cmp_pe_k': 7.301,
     'cmp_w1_k': 2.74,
     'diff_lq1': 3.912,
     'diff_lk1': 5.932,
     'diff_lq2': 3.854,
     'diff_lk2': 5.339,
     'diff_subln': 8.0,
     'conv_b': 8.0,
     'lru_ba': 64.0,
     'lru_bx': 56.828}
    for name, (base, spread) in spreads.items():
        noise = np.random.default_rng([zlib.crc32(name.encode()), seed]).standard_normal(out[name].shape)
        drawn = base * np.exp(spread * noise) if base else spread * noise
        out[name] = jnp.asarray(drawn.astype(out[name].dtype))
    for name, factor in factors.items():
        out[name] = (out[name] * factor).astype(out[name].dtype)
    return out
```

```python
from contextlib import ExitStack
import math

import numpy as np

import concourse.bass as bass
from concourse import mybir

F32 = mybir.dt.float32
F32R = mybir.dt.float32r
BF16 = mybir.dt.bfloat16
ALU = mybir.AluOpType
ACT = mybir.ActivationFunctionType
AX_X = mybir.AxisListType.X

P = 128
NT = 2
S = NT * P
D = 2048
KD = D // P
DFF = 5632
KF = DFF // P
CW = 512
EPS = 1e-6
PLE = 256
NRING = 4

HEADS = 8
KVG = 4
HD = 128
NCMP = 15
CSTR = 16
DQK = 64
Q_A, KV_A, G_A = 0, 1024, 2560
Q_B, K_B, V_B = 2584, 3608, 4632
NGATE = 24
NEG = -1e30
BIGF = 3e38
LAM_INIT = 0.8 - 0.6 * math.exp(-0.3 * 0)
LRU_C = 8.0
NBLK = 8
XPAD = 260


class Kind:

    def __init__(self, name, evac, banks=0, split=False):
        self.name, self.evac, self.banks, self.split = name, evac, banks, split


class Phase:

    def __init__(self, name, pairs, slots, kinds, src, cols, weight, first_turn=None, loop=False,
                 gain=None, dst=None, norm=None, stat=None):
        self.name, self.pairs, self.slots, self.kinds = name, pairs, slots, kinds
        self.src, self.cols, self.weight, self.loop = src, cols, weight, loop
        self.first_turn = first_turn
        self.gain, self.dst = gain, dst
        self.norm = norm
        self.stat = stat


def build_phases():
    resid = Kind("resid", "v", 2, True)
    ph = []

    def attn(name, k0, k1, c0, c1, first=False, gates=False):
        ph.append(Phase(name, 1, (8, 8), (k0, k1), "B", (c0, c1), ("w_in_attn", "w_in_attn"),
                        first_turn=first, norm=0))

    qk = Kind("qk", "v", 2)
    attn("qa", qk, qk, Q_A, Q_A + CW, first=True)
    attn("kvcs", Kind("kvc", "v", 2), Kind("kvs", "v", 1), KV_A, KV_A + CW)
    attn("kvwg", Kind("kvw", "v", 1), Kind("gates", "a"), KV_A + 2 * CW, G_A)
    attn("qb", qk, qk, Q_B, Q_B + CW)
    attn("kb", qk, qk, K_B, K_B + CW)
    attn("vb", Kind("vb", "v"), Kind("vb", "v"), V_B, V_B + CW)
    for layer in range(2):
        if layer:
            ph.append(Phase("xb", 2, (8, 8), (Kind("xb", "v", 2),) * 2, "B", (0, CW),
                            ("w_in_rec",) * 2, first_turn=True, norm=3))
            ph.append(Phase("yb", 2, (8, 8), (Kind("yb", "a", 2),) * 2, "B", (D, D + CW),
                            ("w_in_rec",) * 2, norm=3))
        ph.append(Phase(f"out{layer}", 2, (8, 8), (resid, resid), "B", (0, CW),
                        (("w_out_attn", "w_out_rec")[layer],) * 2, first_turn=True,
                        gain=2 + layer, dst="A", stat=1 + 3 * layer))
        ph.append(Phase(f"ffn{layer}", 11, (8, 8), (Kind("gate", "a"), Kind("up", "v", 2, True)), "A",
                        (0, 0), (f"w_gate{layer}", f"w_up{layer}"), first_turn=True, loop=True,
                        dst="H", norm=1 + 3 * layer))
        ph.append(Phase(f"down{layer}", 2, (24, 24), (resid, resid), "H", (0, CW),
                        (f"w_down{layer}",) * 2, first_turn=True, gain=4 + layer, dst="A",
                        stat=2 + 3 * layer))
        last = layer == 1
        ph.append(Phase(f"ple{layer}", 4, (8, 4),
                        (Kind("plegate", "a"), Kind("pleproj", "v", 0 if last else 2, True)), "A",
                        (0, 0), (f"w_ple_gate{layer}", f"w_ple_proj{layer}"), first_turn=True,
                        gain=None if last else 1, dst=None if last else "B", norm=2 + 3 * layer,
                        stat=6 if last else 3))
    slot, va, turn, hi = 0, {"v": 0, "a": 0}, 8, 8
    for p in ph:
        if p.name == "out0":
            turn, hi = turn + 8, hi + 8
        p.slot0, p.v0, p.turn0, p.hi0 = slot, dict(va), turn, hi
        p.per_slot = sum(p.slots)
        p.per_turn = sum(k.banks for k in p.kinds)
        p.per_hi = sum(k.banks for k in p.kinds if k.split)
        p.per_v = {e: sum(k.evac == e for k in p.kinds) for e in "va"}
        slot += p.per_slot * p.pairs
        turn += p.per_turn * p.pairs
        hi += p.per_hi * p.pairs
        for e in "va":
            va[e] += p.per_v[e] * p.pairs
    for a, b in zip([None] + ph[:-1], ph):
        b.before = a
    return ph


def slot_no(p, i, r, j):
    return i * p.per_slot + (p.slot0 + r * p.slots[0] + j)


def chunk_end(p, i, r):
    return slot_no(p, i, r, p.slots[r])


def evac_no(p, i, r):
    e = p.kinds[r].evac
    before = sum(k.evac == e for k in p.kinds[:r])
    return e, i * p.per_v[e] + (p.v0[e] + before + 1)


def turn_no(p, i, r):
    return i * p.per_turn + (p.turn0 + sum(k.banks for k in p.kinds[:r]))


def hi_no(p, i, r):
    return i * p.per_hi + (p.hi0 + sum(k.banks for k in p.kinds[:r] if k.split))


def two_before(p, i, r):
    if isinstance(i, int) and i == 0:
        return (p.before, p.before.pairs - 1, r) if p.before else None
    return (p, i - 1, r)


def slot_shape(p, r, j):
    if p.slots[r] == 4:
        return j % 2, 1, 256 * (j // 2), 256
    if p.slots[r] == 24:
        return (2 * j, 2, 0, CW) if j < 20 else (20 + j, 1, 0, CW)
    return 2 * j, 2, 0, NGATE if p.kinds[r].name == "gates" else CW


def bank_of_ktile(p, j):
    k0, nk, _, _ = slot_shape(p, 0, j)
    return (k0 + nk - 1) // 2


def trunk(nc, x, p, g_mix, g_ffn, g_ple, g_final, w_in_attn, cmp_pe_k, cmp_w1_k, cmp_w2_k,
          cmp_pe_v, cmp_w1_v, cmp_w2_v, diff_lq1, diff_lk1, diff_lq2, diff_lk2, diff_subln,
          w_out_attn, w_in_rec, conv_w, conv_b, lru_wa, lru_ba, lru_wx, lru_bx, lru_lambda,
          w_out_rec, w_ffn_gate, w_ffn_up, w_ffn_down, w_ple_proj, w_ple_gate, out):
    phases = build_phases()
    named = {q.name: q for q in phases}
    ctx = ExitStack()
    with ctx:
        base = (nc.sbuf_base + 63) // 64 * 64
        size = nc.sbuf_usable_end - 64 - base
        ctx.enter_context(nc.sbuf_tensor("slab", [P, size - 64], mybir.dt.uint8))
        top = [base]

        def at(name, shape, dt, offset):
            return nc.alloc_sbuf_tensor_at(name, [P, *shape], dt, offset=offset)

        def put(name, shape, dt=F32):
            n = int(np.prod(shape)) * (2 if dt == BF16 else 4)
            t = at(name, shape, dt, top[0])
            top[0] += (n + 31) // 32 * 32
            return t

        h = put("h", [NT, D])
        raw = put("raw", [NRING, 2 * CW])
        w_hi = put("w_hi", [NRING, 2 * CW], F32R)
        w_lo = put("w_lo", [NRING, 2 * CW], F32R)
        stage = put("stage", [NT, CW])
        sg = put("sg", [NT, CW])
        junk = put("junk", [CW], BF16)
        pT_hi = put("pT_hi", [2, 2, S], F32R)
        pT_lo = put("pT_lo", [2, 2, S], F32R)
        vecT = put("vecT", [3, P])
        ident = put("ident", [P])
        maskd = put("maskd", [3, P])
        maskc = put("maskc", [NT, 16])
        validc = put("validc", [NT, 16])
        gates_sb = put("gates_sb", [NT, NGATE])
        gcol = put("gcol", [KD])
        ssq = put("ssq", [7, NT, 4])
        rstd = put("rstd", [7, NT])
        tiny = put("tiny", [16])
        nmax = put("nmax", [2, 2, NT])
        esum = put("esum", [2, 2, NT])
        coef = put("coef", [2, 2, NT])
        csum = put("csum", [4, 16])
        ssqb = put("ssqb", [NT, HEADS])
        rstdb = put("rstdb", [NT, HEADS])
        sp_t = put("sp_t", [6, KD])
        a_off = top[0]
        big = a_off + 2 * KD * S * 4
        s_off = big + 2 * KD * S * 4
        assert big + 2 * KF * S * 4 <= base + size - 64, (big + 2 * KF * S * 4, base + size)
        X = {"A": (at("xa_hi", [KD, S], F32R, a_off), at("xa_lo", [KD, S], F32R, a_off + KD * S * 4)),
             "B": (at("xb_hi", [KD, S], F32R, big), at("xb_lo", [KD, S], F32R, big + KD * S * 4)),
             "H": (at("hid_hi", [KF, S], F32R, big), at("hid_lo", [KF, S], F32R, big + KF * S * 4))}
        p_tok = at("p_tok", [2, NT, PLE], F32, s_off)
        vrow = at("vrow", [3, P], F32, s_off + 8192)
        qaT = at("qaT", [HEADS, S], F32, a_off)
        qbT = at("qbT", [HEADS, S], F32, a_off + 8192)
        w1 = at("w1", [32, HD], F32, a_off + 16384)
        kbT = at("kbT", [HEADS, S], F32, s_off)
        kvtok = at("kvtok", [2, NT, CW], F32, s_off + 8192)
        vb_tok = at("vb_tok", [NT, 2 * CW], F32, s_off + 16384)
        kT = at("kT", [2, 2, S], F32, s_off + 24576)
        cmpT = at("cmpT", [4, S], F32, s_off + 28672)
        o_all = at("o_all", [NT, D], F32, s_off + 32768)
        w2 = at("w2", [2, HD], F32, s_off + 49152)
        lam_in = at("lam_in", [4, DQK], F32, s_off + 50176)
        prob = at("prob", [2, 2, 3 * P], F32, big)
        prob2 = at("prob2", [2, 3 * P], F32, big + 6144)
        probT = at("probT", [2, 3 * P], F32, big + 9216)
        cz = at("cz", [2, 2, NCMP * CSTR], F32, big + 12288)
        gz = at("gz", [2, 2 * NCMP + 2], F32, big + 16384)
        kcT = at("kcT", [2, 16], F32, big + 16896)
        vc = at("vc", [2, HD], F32, big + 17408)
        sc_s = at("sc_s", [16, 16], F32, big + 18432)
        pc_T = at("pc_T", [16, P], F32, big + 19456)
        lru_w = at("lru_w", [2, NBLK, 2, 2 * P], F32, a_off)
        xbT = at("xbT", [KD, XPAD], F32, s_off)
        xc = at("xc", [KD, S], F32, s_off + KD * XPAD * 4)
        yT = at("yT", [KD, S], F32, s_off + KD * XPAD * 4 + KD * S * 4)
        i_t = at("i_t", [2, 2, S], F32, s_off + KD * XPAD * 4 + 2 * KD * S * 4)
        decay = at("decay", [KD, S], F32, big)
        th = at("th", [KD, S], F32, big + KD * S * 4)
        gf = at("gf", [D], F32, s_off)
        fin = at("fin", [NT, D], F32, s_off + 8192)

        ps = ctx.enter_context(nc.psum_tensor("ps", [P, 8, CW], F32))
        TP, EX = 4, 6

        def sem(name):
            return ctx.enter_context(nc.semaphore(name))

        x_in = [sem(f"x_in{c}") for c in range(4)]
        vec_in = sem("vec_in")
        p_in = sem("p_in")
        raw_in = [sem(f"raw_in{s}") for s in range(NRING)]
        hi_ready, lo_ready, w_used = sem("hi_ready"), sem("lo_ready"), sem("w_used")
        evac = {"v": sem("evac_v"), "a": sem("evac_a")}
        turned, turn_hi, turn_used = sem("turned"), sem("turn_hi"), sem("turn_used")
        consts = sem("consts")
        pool_step = sem("pool_step")
        vec_turned, vec_ready = sem("vec_turned"), sem("vec_ready")
        p_turned, p_hi, p_ready = sem("p_turned"), sem("p_hi"), sem("p_ready")
        gcol_ready = sem("gcol_ready")
        ssq_ready, ms_ready, rms_ready, rstd_ready = (sem("ssq_ready"), sem("ms_ready"),
                                                      sem("rms_ready"), sem("rstd_ready"))
        dve_step = sem("dve_step")
        ple_step = sem("ple_step")
        w1_in, w2_in, lam_in_sem = [sem("w1_in_k"), sem("w1_in_v")], sem("w2_in"), sem("lam_in")
        scored, softmin, expd, prob_ready = sem("scored"), sem("softmin"), sem("expd"), sem("prob_ready")
        pT_made, pT_ready, pv_done, o_done = sem("pT_made"), sem("pT_ready"), sem("pv_done"), sem("o_done")
        cz_ready, z_done, gelu_done, w2_done, kv_cmp = (sem("cz_ready"), sem("z_done"), sem("gelu_done"),
                                                        sem("w2_done"), sem("kv_cmp"))
        c_scored, c_shift, c_exp, c_prob = sem("c_scored"), sem("c_shift"), sem("c_exp"), sem("c_prob")
        c_T, c_Tr, c_pv, c_out = sem("c_T"), sem("c_Tr"), sem("c_pv"), sem("c_out")
        lam_dots, lam_exps = sem("lam_dots"), sem("lam_exps")
        sp_arg, sp_exp = sem("sp_arg"), sem("sp_exp")
        b_sq, b_ms, b_rms, o_ready = sem("b_sq"), sem("b_ms"), sem("b_rms"), sem("o_ready")
        conv_step = sem("conv_step")
        lru_in = sem("lru_in")
        r_mm, r_sig, i_used = sem("r_mm"), sem("r_sig"), sem("i_used")
        r_exp, r_m, r_sqrt, r_h, r_hi, r_lo = (sem("r_exp"), sem("r_m"), sem("r_sqrt"), sem("r_h"),
                                               sem("r_hi"), sem("r_lo"))
        coef_ready = sem("coef_ready")
        gf_in, fin_ready, stored = sem("gf_in"), sem("fin_ready"), sem("stored")

        W = {"w_in_attn": w_in_attn[0], "w_out_attn": w_out_attn[0], "w_in_rec": w_in_rec[0],
             "w_out_rec": w_out_rec[0]}
        for layer in range(2):
            W[f"w_gate{layer}"] = w_ffn_gate[layer]
            W[f"w_up{layer}"] = w_ffn_up[layer]
            W[f"w_down{layer}"] = w_ffn_down[layer]
            W[f"w_ple_gate{layer}"] = w_ple_gate[layer]
            W[f"w_ple_proj{layer}"] = w_ple_proj[layer]
        W = {k: v.rearrange("(k p) n -> p k n", p=P) for k, v in W.items()}

        GAIN = {0: 0, 1: 16, 3: 48, 4: 64, 5: 80}

        def gain_ap(g, k):
            return vecT[:, 0, k + 16 * g:k + 16 * g + 1]


        def walk(run_chunk, after):
            prev = None
            for q in phases:
                run_chunk(q, 0, 0, prev)
                run_chunk(q, 0, 1, (q, 0, 0))
                prev = (q, q.pairs - 1, 1)
                if q.loop:
                    yield q, run_chunk
                else:
                    for i in range(1, q.pairs):
                        run_chunk(q, i, 0, (q, i - 1, 1))
                        run_chunk(q, i, 1, (q, i, 0))
                if q.name in ("vb", "yb", "ple1"):
                    after(q.name, prev)
                    prev = None

        def run(eng, run_chunk, after):
            for q, step in walk(run_chunk, after):
                with eng.Fori(1, q.pairs) as i:
                    step(q, i, 0, (q, i - 1, 1))
                    step(q, i, 1, (q, i, 0))

        block = ctx.enter_context(nc.Block())

        @block.sync
        def _(sp):
            for c in range(4):
                sp.dma_start(h[:, :, c * CW:(c + 1) * CW],
                             x[0].rearrange("(m p) d -> p m d", p=P)[:, :, c * CW:(c + 1) * CW]
                             ).then_inc(x_in[c], 16)

            def load_slot(q, i, r, j):
                t = slot_no(q, i, r, j)
                s = j % NRING
                k0, nk, c0, w = slot_shape(q, r, j)
                if not (isinstance(t, int) and t < NRING):
                    sp.wait_ge(lo_ready, t - (NRING - 1))
                col = q.cols[r] + c0 + i * (CW if q.kinds[0].evac != q.kinds[1].evac and q.name[:3] in ("ffn", "ple")
                                           else 2 * CW)
                src = W[q.weight[r]][:, k0:k0 + nk, bass.ds(col, w)]
                dst = raw[:, s, 0:nk * w].rearrange("p (k n) -> p k n", k=nk)
                sp.dma_start(dst, src).then_inc(raw_in[s], 16)

            def run_chunk(q, i, r, prev):
                for j in range(q.slots[r]):
                    load_slot(q, i, r, j)
                if q.name == "kvcs" and r == 1:
                    sp.dma_start(w1[:], cmp_w1_k[0].rearrange("l d e -> d l e")).then_inc(w1_in[0], 16)
                    sp.dma_start(w2[:, 0, :], cmp_w2_k[0]).then_inc(w2_in, 16)
                    sp.dma_start(w2[:, 1, :], cmp_w2_v[0]).then_inc(w2_in, 16)
                    for n, v in enumerate((diff_lq1, diff_lk1, diff_lq2, diff_lk2)):
                        sp.dma_start(lam_in[:, n, :], v[0].partition_broadcast(P)).then_inc(lam_in_sem, 16)
                if q.name == "xb" and i == 0 and r == 1:
                    sp.wait_ge(w_used, slot_no(named["ple0"], 3, 1, 4))
                    for n, w in enumerate((lru_wa, lru_wx)):
                        sp.dma_start(lru_w[:, n], w[0].rearrange("b (k p) e -> p b k e", p=P)
                                     ).then_inc(lru_in, 16)

            def after(name, prev):
                if name == "vb":
                    sp.wait_ge(z_done, 1)
                    sp.dma_start(w1[:], cmp_w1_v[0].rearrange("l d e -> d l e")).then_inc(w1_in[1], 16)
                if name == "ple1":
                    sp.wait_ge(w_used, chunk_end(named["ple1"], 0, 0))
                    sp.dma_start(gf[:], g_final.partition_broadcast(P)).then_inc(gf_in, 16)
                    for m in range(NT):
                        sp.wait_ge(fin_ready, m + 1)
                        sp.dma_start(out[0].rearrange("(m p) d -> p m d", p=P)[:, m], fin[:, m]
                                     ).then_inc(stored, 16)
                    sp.wait_ge(stored, 16 * NT)

            run(sp, run_chunk, after)

        @block.gpsimd
        def _(pool):
            n = 0

            def step(ins):
                nonlocal n
                n += 1
                ins.then_inc(pool_step, 1)
                pool.wait_ge(pool_step, n)

            step(nc.gpsimd.memset(vrow[:], 0.0))
            for dst, src in ((vrow[0:32, 0], g_mix.rearrange("a (k p) -> (a k) p", p=P)),
                             (vrow[32:64, 0], g_ffn.rearrange("a (k p) -> (a k) p", p=P)),
                             (vrow[64:96, 0], g_ple.rearrange("a (k p) -> (a k) p", p=P)),
                             (vrow[96:104, 0], diff_subln[0]),
                             (vrow[0:64, 1], conv_w[0].rearrange("a (k p) -> (a k) p", p=P)),
                             (vrow[64:80, 1], conv_b[0].rearrange("(k p) -> k p", p=P)),
                             (vrow[80:96, 1], lru_ba[0].rearrange("(k p) -> k p", p=P)),
                             (vrow[96:112, 1], lru_bx[0].rearrange("(k p) -> k p", p=P)),
                             (vrow[112:128, 1], lru_lambda[0].rearrange("(k p) -> k p", p=P)),
                             (vrow[0:32, 2], cmp_pe_k[0]),
                             (vrow[32:64, 2], cmp_pe_v[0])):
                pool.dma_start(dst, src).then_inc(vec_in, 16)
            for layer in range(2):
                pool.dma_start(p_tok[:, layer], p[layer, 0].rearrange("(m p) e -> p m e", p=P)
                               ).then_inc(p_in, 16)
            step(nc.gpsimd.memset(ident[:], 0.0))
            step(nc.gpsimd.memset(maskd[:], 0.0))
            step(nc.gpsimd.memset(maskc[:], 0.0))
            step(nc.gpsimd.memset(validc[:], 1.0))
            step(nc.gpsimd.memset(ssq[:], 0.0))
            step(nc.gpsimd.affine_select(out=ident[:], in_=ident[:], compare_op=ALU.not_equal, fill=1.0,
                                         base=0, pattern=[[-1, P]], channel_multiplier=1))
            for b in (0, 2):
                step(nc.gpsimd.affine_select(out=maskd[:, b], in_=maskd[:, b], compare_op=ALU.is_ge,
                                             fill=NEG, base=0, pattern=[[-1, P]], channel_multiplier=1))
            for t, fill in ((maskc, NEG), (validc, 0.0)):
                for m in range(NT):
                    step(nc.gpsimd.affine_select(out=t[:, m], in_=t[:, m], compare_op=ALU.is_ge,
                                                 fill=fill, base=m * P - (2 * CSTR - 1),
                                                 pattern=[[-CSTR, 16]], channel_multiplier=1))
            nc.gpsimd.memset(tiny[:], 0.0).then_inc(consts, 1)

        @block.scalar
        def _(act):
            def split_slot(q, i, r, j):
                t = slot_no(q, i, r, j)
                s = j % NRING
                _, nk, _, w = slot_shape(q, r, j)
                n = nk * w
                act.wait_ge(raw_in[s], dma_no(t, s))
                if not (isinstance(t, int) and t < NRING):
                    act.wait_ge(w_used, t - (NRING - 1))
                nc.scalar.activation(w_hi[:, s, 0:n], raw[:, s, 0:n], ACT.Copy).then_inc(hi_ready, 1)

            def evacuate(q, i, r):
                kind = q.kinds[r].name
                if q.kinds[r].evac != "a":
                    return
                act.wait_ge(w_used, chunk_end(q, i, r))
                act.wait_ge(rstd_ready, q.norm + 1)
                for m in range(NT):
                    acc = ps[:, 2 * r + m, :]
                    rs = rstd[:, q.norm, m:m + 1]
                    if kind == "gates":
                        ins = nc.scalar.activation(gates_sb[:, m], acc[:, 0:NGATE], ACT.Sigmoid, scale=rs)
                    elif kind in ("gate", "plegate"):
                        if m == 0:
                            e, n = evac_no(q, i, r)
                            if not (isinstance(i, int) and i == 0):
                                ev, nv = evac_no(q, i - 1, 1)
                                act.wait_ge(evac[ev], nv)
                        f = ACT.Silu if kind == "gate" else ACT.Sigmoid
                        ins = nc.scalar.activation(sg[:, m], acc, f, scale=rs)
                    else:
                        if m == 0:
                            act.wait_ge(turned, turn_no(q, i, r))
                        ins = nc.scalar.activation(stage[:, m], acc, ACT.Gelu_apprx_tanh, scale=rs)
                ins.then_inc(evac["a"], 1)

            def turn_split(dst, k0, t0, h0, gain, banks=2, feat=None):
                for b in range(banks):
                    act.wait_ge(turned, t0 + (b + 1))
                    for f in range(2):
                        o = dst[0][:, k0 + 2 * b + f, :] if isinstance(k0, int) else \
                            dst[0][:, bass.ds(k0 + (2 * b + f), 1), :]
                        src = ps[:, TP + b, f * S:(f + 1) * S]
                        if gain is None:
                            ins = nc.scalar.activation(o, src, ACT.Copy)
                        else:
                            ins = nc.scalar.activation(o, src, ACT.Copy, scale=gain(k0 + 2 * b + f))
                    ins.then_inc(turn_hi, 1)

            def squares(stat, c):
                for m in range(NT):
                    n = (4 * stat + c) * NT + m
                    if n:
                        act.wait_ge(ssq_ready, n)
                    nc.scalar.activation(junk[:], h[:, m, c * CW:(c + 1) * CW], ACT.Square,
                                         accum_out=ssq[:, stat, m, c:c + 1]).then_inc(ssq_ready, 1)

            def root(stat):
                act.wait_ge(ms_ready, stat + 1)
                nc.scalar.activation(rstd[:, stat], rstd[:, stat], ACT.Sqrt).then_inc(rms_ready, 1)

            def aftermath(q, i, r):
                k = q.kinds[r]
                col = 2 * i + r if k.name == "resid" else i
                if k.split and k.banks:
                    g = (lambda kt: gain_ap(q.gain, kt)) if q.gain is not None else None
                    turn_split(X[q.dst], 4 * col, turn_no(q, i, r), hi_no(q, i, r), g)
                if q.stat is not None and k.name in ("resid", "pleproj"):
                    act.wait_ge(evac["v"], evac_no(q, i, r)[1])
                    squares(q.stat, col)
                    if col == 3:
                        root(q.stat)

            def run_chunk(q, i, r, prev):
                host = 4 if q.slots[r] == 4 else 8
                for j in range(q.slots[r]):
                    split_slot(q, i, r, j)
                    if prev and j == 3:
                        evacuate(*prev)
                    if prev and j == host - 1:
                        aftermath(*prev)

            def after(name, prev):
                evacuate(*prev)
                aftermath(*prev)
                if name == "vb":
                    attention()
                if name == "yb":
                    griffin()

            def attention():
                act.wait_ge(lam_dots, 1)
                nc.scalar.activation(tiny[:, 2:4], tiny[:, 0:2], ACT.Exp).then_inc(lam_exps, 1)
                act.wait_ge(sp_arg, 1)
                nc.scalar.activation(sp_t[:, 1], sp_t[:, 0], ACT.Exp, scale=-1.0).then_inc(sp_exp, 1)
                for kind in range(2):
                    act.wait_ge(z_done, kind + 1)
                    nc.scalar.activation(gz[:, kind, 0:2 * NCMP], ps[:, EX + kind, 0:2 * NCMP],
                                         ACT.Gelu_apprx_tanh).then_inc(gelu_done, 1)
                act.wait_ge(c_shift, 1)
                nc.scalar.activation(sc_s[:], sc_s[:], ACT.Exp, scale=HD ** -0.5).then_inc(c_exp, 1)
                for b in range(4):
                    act.wait_ge(c_T, b + 1)
                    nc.scalar.activation(pc_T[0:NCMP, 4 * b:4 * b + 4],
                                         ps[0:NCMP, b, :].rearrange("p (a t) -> p a t", a=4),
                                         ACT.Copy).then_inc(c_Tr, 1)
                for u in range(24 + 1):
                    if u < 24:
                        maps = 2 if u >= 16 else 1
                        act.wait_ge(softmin, u + 1)
                        for c in range(maps):
                            for m, cols in enumerate((slice(0, P), slice(P, 3 * P))):
                                pr = prob[:, u % 2, c, cols]
                                ins = nc.scalar.activation(pr, pr, ACT.Exp, scale=-1.0,
                                                           bias=nmax[:, u % 2, c, m:m + 1],
                                                           accum_out=esum[:, u % 2, c, m:m + 1])
                        ins.then_inc(expd, 1)
                    if u >= 1:
                        v = u - 1
                        act.wait_ge(pT_made, v + 1)
                        if v >= 2:
                            act.wait_ge(pv_done, v - 1)
                        nc.scalar.activation(probT[:, v % 2], ps[:, TP + v % 2, 0:3 * P], ACT.Copy
                                             ).then_inc(pT_ready, 1)
                act.wait_ge(o_done, 24)
                for m in range(NT):
                    for hd in range(HEADS):
                        o = o_all[:, m, (HEADS + hd) * P:(HEADS + hd + 1) * P]
                        if m + hd:
                            act.wait_ge(b_sq, HEADS * m + hd)
                        nc.scalar.activation(junk[:, 0:P], o, ACT.Square,
                                             accum_out=ssqb[:, m, hd:hd + 1]).then_inc(b_sq, 1)
                act.wait_ge(b_ms, 1)
                nc.scalar.activation(rstdb[:], rstdb[:], ACT.Sqrt).then_inc(b_rms, 1)
                q = named["out0"]
                for c in range(4):
                    turn_split(X["B"], 4 * c, q.turn0 - 8 + 2 * c, q.hi0 - 8 + 2 * c,
                               lambda kt: gcol[:, kt:kt + 1])

            def griffin():
                for n in range(NBLK):
                    act.wait_ge(r_mm, n + 1)
                    if n >= 2:
                        act.wait_ge(i_used, n - 1)
                    for g in range(2):
                        for e in range(2):
                            f = 2 * n + e
                            o = xbT[:, f, 0:S] if g == 0 else i_t[:, n % 2, e]
                            ins = nc.scalar.activation(o, ps[:, 2 * (n % 2) + g, e * S:(e + 1) * S],
                                                       ACT.Sigmoid, bias=vecT[:, 1, 80 + 16 * g + f:81 + 16 * g + f])
                    ins.then_inc(r_sig, 1)
                act.wait_ge(coef_ready, 1)
                act.wait_ge(i_used, NBLK)
                act.wait_ge(r_sig, NBLK)
                for f in range(KD):
                    nc.scalar.activation(decay[:, f], xbT[:, f, 0:S], ACT.Exp, scale=sp_t[:, 4, f:f + 1])
                    ins = nc.scalar.activation(th[:, f], xbT[:, f, 0:S], ACT.Tanh, scale=sp_t[:, 5, f:f + 1])
                    if f % 4 == 3:
                        ins.then_inc(r_exp, 1)
                for g in range(4):
                    act.wait_ge(r_m, g + 1)
                    nc.scalar.activation(xbT[:, 4 * g:4 * g + 4, 0:S], th[:, 4 * g:4 * g + 4], ACT.Sqrt
                                         ).then_inc(r_sqrt, 1)
                for g in range(4):
                    act.wait_ge(r_h, g + 1)
                    nc.scalar.activation(X["B"][0][:, 4 * g:4 * g + 4], xc[:, 4 * g:4 * g + 4], ACT.Copy
                                         ).then_inc(r_hi, 1)

            act.wait_ge(p_turned, 1)
            nc.scalar.activation(pT_hi[:, 0], ps[:, EX, :].rearrange("p (k t) -> p k t", k=2), ACT.Copy)
            nc.scalar.activation(pT_hi[:, 1], ps[:, EX + 1, :].rearrange("p (k t) -> p k t", k=2), ACT.Copy
                                 ).then_inc(p_hi, 1)
            act.wait_ge(vec_ready, 1)
            for c in range(4):
                turn_split(X["B"], 4 * c, 2 * c, 2 * c, lambda kt: gain_ap(0, kt))
                squares(0, c)
            root(0)
            run(act, run_chunk, after)

        @block.vector
        def _(dve):
            steps = 0

            def step(ins):
                nonlocal steps
                steps += 1
                ins.then_inc(dve_step, 1)
                dve.wait_ge(dve_step, steps)

            def split_slot(q, i, r, j):
                t = slot_no(q, i, r, j)
                s = j % NRING
                _, nk, _, w = slot_shape(q, r, j)
                n = nk * w
                dve.wait_ge(hi_ready, t + 1)
                nc.vector.tensor_tensor(w_lo[:, s, 0:n], raw[:, s, 0:n], w_hi[:, s, 0:n].bitcast(F32),
                                        ALU.subtract).then_inc(lo_ready, 1)

            def evacuate(q, i, r):
                k = q.kinds[r]
                kind = k.name
                if k.evac != "v":
                    return
                dve.wait_ge(w_used, chunk_end(q, i, r))
                if kind in ("qk", "xb", "up") and turn_no(q, i, r) is not 0:
                    dve.wait_ge(turned, turn_no(q, i, r))
                if q.norm is not None and kind != "pleproj":
                    dve.wait_ge(rstd_ready, q.norm + 1)
                if kind == "up" or kind == "pleproj":
                    e, n = evac_no(q, i, 0)
                    dve.wait_ge(evac[e], n)
                for m in range(NT):
                    acc = ps[:, 2 * r + m, :]
                    rs = rstd[:, q.norm, m:m + 1] if q.norm is not None else None
                    if kind == "resid":
                        o = h[:, m, (2 * i + r) * CW:(2 * i + r + 1) * CW]
                        ins = nc.vector.tensor_tensor(o, acc, o, ALU.add)
                    elif kind == "pleproj":
                        ins = nc.vector.tensor_tensor(stage[:, m], acc, sg[:, m], ALU.mult)
                        ins.then_inc(ple_step, 1)
                        n0 = 8 * (q.name == "ple1") + 2 * i + m + 1
                        dve.wait_ge(ple_step, n0)
                        o = h[:, m, i * CW:(i + 1) * CW]
                        ins = nc.vector.tensor_tensor(o, o, stage[:, m], ALU.add)
                    elif kind == "up":
                        ins = nc.vector.scalar_tensor_tensor(out=stage[:, m], in0=acc, scalar=rs, in1=sg[:, m],
                                                             op0=ALU.mult, op1=ALU.mult)
                    else:
                        o = {"qk": lambda: stage[:, m], "xb": lambda: stage[:, m],
                             "kvc": lambda: stage[:, m],
                             "kvs": lambda: kvtok[:, 0, m], "kvw": lambda: kvtok[:, 1, m],
                             "vb": lambda: vb_tok[:, m, r * CW:(r + 1) * CW]}[kind]()
                        ins = nc.vector.tensor_scalar(o, acc, rs, None, ALU.mult)
                ins.then_inc(evac["v"], 1)

            def turn_split(dst, k0, h0, gain):
                for b in range(2):
                    dve.wait_ge(turn_hi, h0 + (b + 1))
                    for f in range(2):
                        if isinstance(k0, int):
                            hi, lo = (dst[z][:, k0 + 2 * b + f, :] for z in range(2))
                        else:
                            hi, lo = (dst[z][:, bass.ds(k0 + (2 * b + f), 1), :] for z in range(2))
                        src = ps[:, TP + b, f * S:(f + 1) * S]
                        if gain is None:
                            ins = nc.vector.tensor_tensor(lo, src, hi.bitcast(F32), ALU.subtract)
                        else:
                            ins = nc.vector.scalar_tensor_tensor(
                                out=lo, in0=src, scalar=gain(k0 + 2 * b + f), in1=hi.bitcast(F32),
                                op0=ALU.mult, op1=ALU.subtract)
                    ins.then_inc(turn_used, 1)

            def mean_square(stat):
                dve.wait_ge(ssq_ready, 4 * NT * (stat + 1))
                step(nc.vector.tensor_reduce(rstd[:, stat], ssq[:, stat], AX_X, ALU.add))
                nc.vector.tensor_scalar(rstd[:, stat], rstd[:, stat], 1.0 / D, EPS, ALU.mult, ALU.add
                                        ).then_inc(ms_ready, 1)
                dve.wait_ge(rms_ready, stat + 1)
                nc.vector.reciprocal(rstd[:, stat], rstd[:, stat]).then_inc(rstd_ready, 1)
                dve.wait_ge(rstd_ready, stat + 1)

            def aftermath(q, i, r):
                k = q.kinds[r]
                col = 2 * i + r if k.name == "resid" else i
                t0 = turn_no(q, i, r)
                if k.split and k.banks:
                    g = (lambda kt: gain_ap(q.gain, kt)) if q.gain is not None else None
                    turn_split(X[q.dst], 4 * col, hi_no(q, i, r), g)
                elif k.banks:
                    for b in range(k.banks):
                        dve.wait_ge(turned, t0 + b + 1)
                        src = ps[:, TP + (t0 + b) % 2, :].rearrange("p (f t) -> p f t", f=2)
                        c = 4 * r + 2 * b
                        o = {"qa": lambda: qaT[:, c:c + 2], "qb": lambda: qbT[:, c:c + 2],
                             "kb": lambda: kbT[:, c:c + 2],
                             "kvcs": lambda: cmpT[:, c:c + 2] if r == 0 else kT[:, 0],
                             "kvwg": lambda: kT[:, 1],
                             "xb": lambda: xbT[:, 8 * i + c:8 * i + c + 2, 3:3 + S],
                             "yb": lambda: yT[:, 8 * i + c:8 * i + c + 2]}[q.name]()
                        nc.vector.tensor_copy(o, src).then_inc(turn_used, 1)
                if k.name == "xb":
                    conv(2 * i + r)
                if q.stat is not None and k.name in ("resid", "pleproj") and col == 3:
                    mean_square(q.stat)

            def conv(c):
                dve.wait_ge(turn_used, named["xb"].turn0 + 2 * c + 2)
                for tap in range(4):
                    if tap:
                        dve.wait_ge(conv_step, 1 + 4 * c + tap)
                    for f in range(4 * c, 4 * c + 4):
                        src = xbT[:, f, 3 - tap:3 - tap + S]
                        w = vecT[:, 1, 16 * (3 - tap) + f:16 * (3 - tap) + f + 1]
                        if tap == 0:
                            ins = nc.vector.tensor_scalar(xc[:, f], src, w, vecT[:, 1, 64 + f:65 + f],
                                                          ALU.mult, ALU.add)
                        else:
                            ins = nc.vector.scalar_tensor_tensor(out=xc[:, f], in0=src, scalar=w, in1=xc[:, f],
                                                                 op0=ALU.mult, op1=ALU.add)
                    ins.then_inc(conv_step, 1)

            def run_chunk(q, i, r, prev):
                host = 4 if q.slots[r] == 4 else 8
                for j in range(q.slots[r]):
                    split_slot(q, i, r, j)
                    if prev and j == 3:
                        evacuate(*prev)
                    if prev and j == host - 1:
                        aftermath(*prev)
                if q.name == "xb" and i == 0 and r == 0:
                    dve.wait_ge(turned, named["xb"].turn0)
                    nc.vector.memset(xbT[:, :, 0:3], 0.0).then_inc(conv_step, 1)
                    dve.wait_ge(conv_step, 1)

            def after(name, prev):
                evacuate(*prev)
                aftermath(*prev)
                if name == "vb":
                    attention()
                elif name == "yb":
                    griffin()
                else:
                    dve.wait_ge(gf_in, 16)
                    for m in range(NT):
                        nc.vector.scalar_tensor_tensor(out=fin[:, m], in0=h[:, m], scalar=rstd[:, 6, m:m + 1],
                                                       in1=gf[:], op0=ALU.mult, op1=ALU.mult
                                                       ).then_inc(fin_ready, 1)

            def attention():
                dve.wait_ge(lam_in_sem, 64)
                for n in range(2):
                    step(nc.vector.tensor_tensor_reduce(
                        out=lam_in[:, 2 * n], in0=lam_in[:, 2 * n], in1=lam_in[:, 2 * n + 1], scale=1.0,
                        scalar=0.0, op0=ALU.mult, op1=ALU.add, accum_out=tiny[:, n:n + 1]))
                nc.vector.tensor_copy(tiny[:, 8:9], tiny[:, 0:1]).then_inc(lam_dots, 1)
                lam = vecT[:, 1, 112:128]
                step(nc.vector.tensor_scalar(sp_t[:, 2], lam, -1.0, None, ALU.mult))
                nc.vector.tensor_tensor(sp_t[:, 0], sp_t[:, 2], lam, ALU.max).then_inc(sp_arg, 1)
                dve.wait_ge(lam_exps, 1)
                step(nc.vector.tensor_tensor(tiny[:, 4:5], tiny[:, 3:4], tiny[:, 2:3], ALU.subtract))
                step(nc.vector.tensor_scalar(tiny[:, 5:6], tiny[:, 4:5], -LAM_INIT, None, ALU.add))
                step(nc.vector.tensor_scalar(sp_t[:, 2], sp_t[:, 2], 0.0, None, ALU.max))
                dve.wait_ge(sp_exp, 1)
                step(nc.vector.tensor_scalar(sp_t[:, 3], sp_t[:, 1], 2.0, None, ALU.add))
                step(nc.vector.reciprocal(sp_t[:, 3], sp_t[:, 3]))
                step(nc.vector.tensor_tensor(sp_t[:, 1], sp_t[:, 1], sp_t[:, 3], ALU.mult))
                step(nc.vector.tensor_tensor(sp_t[:, 3], sp_t[:, 1], sp_t[:, 1], ALU.mult))
                step(nc.vector.tensor_scalar(sp_t[:, 4], sp_t[:, 3], 1.0 / 17, 1.0 / 15, ALU.mult, ALU.add))
                for n in range(13, 0, -2):
                    step(nc.vector.tensor_tensor(sp_t[:, 4], sp_t[:, 4], sp_t[:, 3], ALU.mult))
                    step(nc.vector.tensor_scalar(sp_t[:, 4], sp_t[:, 4], 1.0 / n, None, ALU.add))
                step(nc.vector.tensor_tensor(sp_t[:, 4], sp_t[:, 4], sp_t[:, 1], ALU.mult))
                step(nc.vector.tensor_scalar(sp_t[:, 4], sp_t[:, 4], 2.0, None, ALU.mult))
                step(nc.vector.tensor_tensor(sp_t[:, 5], sp_t[:, 4], sp_t[:, 2], ALU.add))
                step(nc.vector.tensor_scalar(sp_t[:, 5], sp_t[:, 5], LRU_C, None, ALU.mult))
                nc.vector.tensor_scalar(sp_t[:, 4], sp_t[:, 5], -1.0, None, ALU.mult).then_inc(coef_ready, 1)
                step(nc.vector.memset(gcol[:, 0:HEADS], 1.0))
                step(nc.vector.tensor_scalar(gcol[:, HEADS:KD], vecT[:, 0, 96:104], 1.0 - LAM_INIT, None,
                                             ALU.mult))
                dve.wait_ge(turn_used, named["kvwg"].turn0)
                for kind in range(2):
                    if kind:
                        dve.wait_ge(z_done, 1)
                    for half in range(2):
                        for g in range(2):
                            src = cmpT[:, 2 * kind + g, CSTR * half:CSTR * half + NCMP * CSTR]
                            pe = vecT[:, 2, 32 * kind + CSTR * half:32 * kind + CSTR * (half + 1)]
                            ins = nc.vector.tensor_tensor(
                                cz[:, half, g].rearrange("p (n l) -> p n l", l=CSTR),
                                src.rearrange("p (n l) -> p n l", l=CSTR),
                                pe.unsqueeze(1).to_broadcast([P, NCMP, CSTR]), ALU.add)
                    ins.then_inc(cz_ready, 1)
                dve.wait_ge(w2_done, 1)
                nc.vector.tensor_copy(kcT[:, :, 0:NCMP], ps[:, 0, 0:2 * NCMP].rearrange("p (g n) -> p g n", g=2)
                                      ).then_inc(kv_cmp, 1)
                dve.wait_ge(w2_done, 2)
                nc.vector.tensor_copy(vc[0:NCMP], ps[0:NCMP, 1, 0:2 * HD].rearrange("p (g d) -> p g d", g=2)
                                      ).then_inc(kv_cmp, 1)
                dve.wait_ge(c_scored, 1)
                step(nc.vector.memset(sc_s[:], 0.0))
                for m in range(NT):
                    step(nc.vector.tensor_tensor(
                        sc_s[:, 8 * m:8 * m + 8, 0:NCMP],
                        ps[:, 2, 128 * m:128 * m + 128].rearrange("p (a n) -> p a n", n=16)[:, :, 0:NCMP],
                        maskc[:, m, 0:NCMP].unsqueeze(1).to_broadcast([P, HEADS, NCMP]), ALU.add))
                step(nc.vector.tensor_reduce(csum[:, 0], sc_s[:, :, 0:NCMP], AX_X, ALU.max))
                nc.vector.tensor_tensor(sc_s[:, :, 0:NCMP], sc_s[:, :, 0:NCMP],
                                        csum[:, 0].unsqueeze(2).to_broadcast([P, 16, NCMP]), ALU.subtract
                                        ).then_inc(c_shift, 1)
                dve.wait_ge(c_exp, 1)
                step(nc.vector.tensor_reduce(csum[:, 1], sc_s[:, :, 0:NCMP], AX_X, ALU.add))
                for m in range(NT):
                    ins = nc.vector.tensor_tensor(
                        sc_s[:, 8 * m:8 * m + 8, 0:NCMP], sc_s[:, 8 * m:8 * m + 8, 0:NCMP],
                        validc[:, m, 0:NCMP].unsqueeze(1).to_broadcast([P, HEADS, NCMP]), ALU.mult)
                ins.then_inc(c_prob, 1)
                step(nc.vector.reciprocal(csum[:, 2], csum[:, 1]))
                g3 = gates_sb[:, :, :].rearrange("p m (a b) -> p m a b", b=3)
                dve.wait_ge(evac["a"], named["kvwg"].v0["a"] + 1)
                for m in range(NT):
                    step(nc.vector.tensor_tensor(csum[:, 3, 8 * m:8 * m + 8], csum[:, 2, 8 * m:8 * m + 8],
                                                 g3[:, m, :, 0], ALU.mult))
                for b in range(4):
                    dve.wait_ge(c_pv, b + 1)
                    for a in range(4):
                        mh = 4 * b + a
                        m, hd = divmod(mh, HEADS)
                        ins = nc.vector.tensor_scalar(o_all[:, m, hd * P:(hd + 1) * P],
                                                      ps[:, 4 + b, a * P:(a + 1) * P], csum[:, 3, mh:mh + 1],
                                                      None, ALU.mult)
                    ins.then_inc(c_out, 1)
                dve.wait_ge(c_out, 4)

                scale_a, scale_b = HD ** -0.5, DQK ** -0.5

                def softmin_unit(u):
                    maps = 2 if u >= 16 else 1
                    dve.wait_ge(scored, u + 1)
                    if u >= 2:
                        dve.wait_ge(pT_made, u - 1)
                    for c in range(maps):
                        bank = 2 * (u % 2) + c
                        for m, (a, b) in enumerate(((0, P), (P, 3 * P))):
                            ins = nc.vector.tensor_tensor_reduce(
                                out=prob[:, u % 2, c, a:b], in0=ps[:, bank, a:b],
                                in1=maskd[:].rearrange("p b t -> p (b t)")[:, a:b],
                                scale=-(scale_b if u >= 16 else scale_a), scalar=BIGF,
                                op0=ALU.add, op1=ALU.min, accum_out=nmax[:, u % 2, c, m:m + 1])
                    ins.then_inc(softmin, 1)

                def weights_unit(u):
                    maps = 2 if u >= 16 else 1
                    dve.wait_ge(expd, u + 1)
                    b = u % 2
                    step(nc.vector.reciprocal(coef[:, b, 0:maps], esum[:, b, 0:maps]))
                    if u < 16:
                        branch, hd = 1 + u // HEADS, u % HEADS
                        nc.vector.tensor_tensor(coef[:, b, 0], coef[:, b, 0], g3[:, :, hd, branch],
                                                ALU.mult).then_inc(prob_ready, 1)
                        return
                    for m, cols in enumerate((slice(0, P), slice(P, 3 * P))):
                        ins = nc.vector.tensor_scalar(prob2[:, b, cols], prob[:, b, 1, cols],
                                                      coef[:, b, 1, m:m + 1], tiny[:, 5:6], ALU.mult, ALU.mult)
                    step(ins)
                    for m, cols in enumerate((slice(0, P), slice(P, 3 * P))):
                        ins = nc.vector.scalar_tensor_tensor(
                            out=prob[:, b, 0, cols], in0=prob[:, b, 0, cols], scalar=coef[:, b, 0, m:m + 1],
                            in1=prob2[:, b, cols], op0=ALU.mult, op1=ALU.add)
                    ins.then_inc(prob_ready, 1)

                def out_unit(u):
                    dve.wait_ge(pv_done, u + 1)
                    if u < 16:
                        dve.wait_ge(prob_ready, u + 1)
                        if u >= HEADS:
                            dve.wait_ge(o_done, u - HEADS + 1)
                    for m in range(NT):
                        acc = ps[:, EX + u % 2, m * P:(m + 1) * P]
                        if u < 16:
                            o = o_all[:, m, (u % HEADS) * P:(u % HEADS + 1) * P]
                            ins = nc.vector.scalar_tensor_tensor(out=o, in0=acc, scalar=coef[:, u % 2, 0, m:m + 1],
                                                                 in1=o, op0=ALU.mult, op1=ALU.add)
                        else:
                            o = o_all[:, m, (u - HEADS) * P:(u - HEADS + 1) * P]
                            ins = nc.vector.tensor_copy(o, acc)
                    ins.then_inc(o_done, 1)

                for u in range(24 + 1):
                    if u >= 1:
                        weights_unit(u - 1)
                    if u >= 2:
                        out_unit(u - 2)
                    if u < 24:
                        softmin_unit(u)
                out_unit(23)
                dve.wait_ge(b_sq, NT * HEADS)
                nc.vector.tensor_scalar(rstdb[:], ssqb[:], 1.0 / HD, EPS, ALU.mult, ALU.add).then_inc(b_ms, 1)
                dve.wait_ge(b_rms, 1)
                step(nc.vector.reciprocal(rstdb[:], rstdb[:]))
                for hd in range(HEADS):
                    for m in range(NT):
                        o = o_all[:, m, (HEADS + hd) * P:(HEADS + hd + 1) * P]
                        ins = nc.vector.tensor_scalar(o, o, rstdb[:, m, hd:hd + 1], None, ALU.mult)
                ins.then_inc(o_ready, 1)
                q = named["out0"]
                for c in range(4):
                    turn_split(X["B"], 4 * c, q.hi0 - 8 + 2 * c, lambda kt: gcol[:, kt:kt + 1])

            def griffin():
                for n in range(NBLK):
                    dve.wait_ge(r_sig, n + 1)
                    x2 = xc[:, 2 * n:2 * n + 2]
                    nc.vector.tensor_tensor(x2, x2, i_t[:, n % 2], ALU.mult).then_inc(i_used, 1)
                dve.wait_ge(i_used, NBLK)
                for g in range(4):
                    t4 = slice(4 * g, 4 * g + 4)
                    dve.wait_ge(r_exp, g + 1)
                    step(nc.vector.tensor_tensor(xbT[:, t4, 0:S], decay[:, t4], decay[:, t4], ALU.mult))
                    nc.vector.scalar_tensor_tensor(out=th[:, t4], in0=xbT[:, t4, 0:S], scalar=1.0, in1=th[:, t4],
                                                   op0=ALU.add, op1=ALU.mult).then_inc(r_m, 1)
                for g in range(4):
                    t4 = slice(4 * g, 4 * g + 4)
                    dve.wait_ge(r_sqrt, g + 1)
                    step(nc.vector.tensor_tensor(xc[:, t4], xbT[:, t4, 0:S], xc[:, t4], ALU.mult))
                    for f in range(4 * g, 4 * g + 4):
                        ins = nc.vector.tensor_tensor_scan(xbT[:, f, 0:S], decay[:, f], xc[:, f], 0.0,
                                                           ALU.mult, ALU.add)
                    step(ins)
                    nc.vector.tensor_tensor(xc[:, t4], xbT[:, t4, 0:S], yT[:, t4], ALU.mult).then_inc(r_h, 1)
                for g in range(4):
                    t4 = slice(4 * g, 4 * g + 4)
                    dve.wait_ge(r_hi, g + 1)
                    nc.vector.tensor_tensor(X["B"][1][:, t4], xc[:, t4], X["B"][0][:, t4].bitcast(F32),
                                            ALU.subtract).then_inc(r_lo, 1)

            dve.wait_ge(vec_turned, 1)
            nc.vector.tensor_copy(vecT[:].rearrange("p a b -> p (a b)"), ps[:, 0, 0:3 * P]).then_inc(vec_ready, 1)
            dve.wait_ge(p_hi, 1)
            for layer in range(2):
                ins = nc.vector.tensor_tensor(pT_lo[:, layer], ps[:, EX + layer, :].rearrange("p (k t) -> p k t", k=2),
                                              pT_hi[:, layer].bitcast(F32), ALU.subtract)
            ins.then_inc(p_ready, 1)
            dve.wait_ge(vec_ready, 1)
            dve.wait_ge(consts, 1)
            for c in range(4):
                turn_split(X["B"], 4 * c, 2 * c, lambda kt: gain_ap(0, kt))
            mean_square(0)
            run(dve, run_chunk, after)

        @block.tensor
        def _(pe):
            def transpose4(src, t0, tiles=4):
                for f in range(tiles):
                    b = f // 2
                    if f % 2 == 0 and not (isinstance(t0, int) and t0 + b < 2):
                        pe.wait_ge(turn_used, t0 + (b - 1))
                    for m in range(NT):
                        bank = (t0 + b) % 2 if isinstance(t0, int) else b
                        o = ps[:, TP + bank, (f % 2) * S + m * P:(f % 2) * S + (m + 1) * P]
                        ins = nc.tensor.transpose(o, src(m, f), ident[:])
                    if f % 2 == 1:
                        ins.then_inc(turned, 1)

            def multiply_slot(q, i, r, j):
                t = slot_no(q, i, r, j)
                s = j % NRING
                k0, nk, c0, w = slot_shape(q, r, j)
                pe.wait_ge(lo_ready, t + 1)
                if j == 0:
                    pre = two_before(q, i, r)
                    if pre:
                        e, n = evac_no(*pre)
                        pe.wait_ge(evac[e], n)
                ple_p = q.name[:3] == "ple" and r == 1
                if ple_p:
                    if j == 0:
                        pe.wait_ge(p_ready, 1)
                    layer = int(q.name[3])
                    xh, xl = pT_hi[:, layer], pT_lo[:, layer]
                else:
                    xh, xl = X[q.src]
                if q.first_turn and isinstance(i, int) and i == 0 and r == 0:
                    if q.name == "out1":
                        pe.wait_ge(r_lo, j // 2 + 1)
                    else:
                        pe.wait_ge(turn_used, src_turn0(q) + bank_of_ktile(q, j) + 1)
                nkt = 2 if ple_p else (KF if q.slots[r] == 24 else KD)
                for m in range(NT):
                    o = ps[:, 2 * r + m, c0:c0 + w]
                    for k in range(k0, k0 + nk):
                        tok = slice(m * P, (m + 1) * P)
                        wk = slice((k - k0) * w, (k - k0 + 1) * w)
                        nc.tensor.matmul(o, xh[:, k, tok], w_hi[:, s, wk], start=(k == 0), stop=False)
                        nc.tensor.matmul(o, xh[:, k, tok], w_lo[:, s, wk], start=False, stop=False)
                        ins = nc.tensor.matmul(o, xl[:, k, tok], w_hi[:, s, wk], start=False,
                                               stop=(k == nkt - 1))
                ins.then_inc(w_used, 1)

            def turn(q, i, r):
                k = q.kinds[r]
                if not k.banks:
                    return
                e, n = evac_no(q, i, r)
                pe.wait_ge(evac[e], n)
                t0 = turn_no(q, i, r)
                if k.name in ("resid", "pleproj"):
                    c = 2 * i + r if k.name == "resid" else i
                    transpose4(lambda m, f: h[:, m, c * CW + f * P:c * CW + (f + 1) * P], t0)
                elif k.name in ("kvs", "kvw"):
                    which = k.name == "kvw"
                    transpose4(lambda m, f: kvtok[:, int(which), m, f * P:(f + 1) * P], t0, tiles=2)
                else:
                    transpose4(lambda m, f: stage[:, m, f * P:(f + 1) * P], t0)

            def run_chunk(q, i, r, prev):
                for j in range(q.slots[r]):
                    multiply_slot(q, i, r, j)
                    if prev and j == 3:
                        turn(*prev)

            def after(name, prev):
                turn(*prev)
                if name == "vb":
                    attention()
                elif name == "yb":
                    griffin()

            def attention():
                pe.wait_ge(evac["v"], named["out0"].v0["v"])
                pe.wait_ge(evac["a"], named["out0"].v0["a"])
                for kind in range(2):
                    pe.wait_ge(w1_in[kind], 16)
                    pe.wait_ge(cz_ready, kind + 1)
                    for l in range(2 * CSTR):
                        x30 = cz[:, l // CSTR].rearrange("p g (n l) -> p g n l", l=CSTR)[:, :, :, l % CSTR]
                        ins = nc.tensor.matmul(ps[:, EX + kind, 0:2 * NCMP].rearrange("p (g n) -> p g n", g=2),
                                               w1[:, l], x30, start=(l == 0), stop=(l == 2 * CSTR - 1))
                    ins.then_inc(z_done, 1)
                pe.wait_ge(w2_in, 32)
                pe.wait_ge(gelu_done, 1)
                nc.tensor.matmul(ps[:, 0, 0:2 * NCMP], w2[:, 0], gz[:, 0, 0:2 * NCMP], start=True, stop=True
                                 ).then_inc(w2_done, 1)
                pe.wait_ge(gelu_done, 2)
                for g in range(2):
                    ins = nc.tensor.matmul(ps[0:NCMP, 1, g * HD:(g + 1) * HD], gz[:, 1, g * NCMP:(g + 1) * NCMP],
                                           w2[:, 1], start=True, stop=True)
                ins.then_inc(w2_done, 1)
                pe.wait_ge(kv_cmp, 2)
                for m in range(NT):
                    for hd in range(HEADS):
                        mh = HEADS * m + hd
                        ins = nc.tensor.matmul(ps[:, 2, 16 * mh:16 * mh + NCMP], qaT[:, hd, m * P:(m + 1) * P],
                                               kcT[:, hd // KVG, 0:NCMP], start=True, stop=True)
                ins.then_inc(c_scored, 1)
                pe.wait_ge(c_prob, 1)
                for mh in range(16):
                    ins = nc.tensor.matmul(ps[0:NCMP, mh // 4, (mh % 4) * P:(mh % 4 + 1) * P],
                                           sc_s[:, mh, 0:NCMP], ident[:], start=True, stop=True)
                    if mh % 4 == 3:
                        ins.then_inc(c_T, 1)
                for b in range(4):
                    pe.wait_ge(c_Tr, b + 1)
                    for a in range(4):
                        mh = 4 * b + a
                        g = (mh % HEADS) // KVG
                        ins = nc.tensor.matmul(ps[:, 4 + b, a * P:(a + 1) * P], pc_T[0:NCMP, mh], vc[0:NCMP, g],
                                               start=True, stop=True)
                    ins.then_inc(c_pv, 1)
                pe.wait_ge(c_out, 4)

                def score_unit(u):
                    if u >= 2:
                        pe.wait_ge(softmin, u - 1)
                    for c in range(2 if u >= 16 else 1):
                        bank = 2 * (u % 2) + c
                        if u < 16:
                            q_t, k_t = qaT[:, u % HEADS], kT[:, u // HEADS, (u % HEADS) // KVG]
                        else:
                            rows = slice(DQK * c, DQK * (c + 1))
                            q_t, k_t = qbT[rows, u - 16], kbT[rows, u - 16]
                        nc.tensor.matmul(ps[:, bank, 0:P], q_t[:, 0:P], k_t[:, 0:P], start=True, stop=True)
                        ins = nc.tensor.matmul(ps[:, bank, P:3 * P], q_t[:, P:S], k_t[:, 0:S],
                                               start=True, stop=True)
                    ins.then_inc(scored, 1)

                def turn_unit(u):
                    pe.wait_ge(prob_ready, u + 1)
                    if u >= 2:
                        pe.wait_ge(pT_ready, u - 1)
                    for b in range(3):
                        ins = nc.tensor.transpose(ps[:, TP + u % 2, b * P:(b + 1) * P],
                                                  prob[:, u % 2, 0, b * P:(b + 1) * P], ident[:])
                    ins.then_inc(pT_made, 1)

                def value_unit(u):
                    pe.wait_ge(pT_ready, u + 1)
                    if u >= 2:
                        pe.wait_ge(o_done, u - 1)
                    if u < 16:
                        c = 2 * P + ((u % HEADS) // KVG) * P
                        v = [kvtok[:, u // HEADS, m, c:c + P] for m in range(NT)]
                    else:
                        v = [vb_tok[:, m, (u - 16) * P:(u - 15) * P] for m in range(NT)]
                    o = ps[:, EX + u % 2, :]
                    pt = probT[:, u % 2]
                    nc.tensor.matmul(o[:, 0:P], pt[:, 0:P], v[0], start=True, stop=True)
                    nc.tensor.matmul(o[:, P:S], pt[:, P:2 * P], v[0], start=True, stop=False)
                    nc.tensor.matmul(o[:, P:S], pt[:, 2 * P:3 * P], v[1], start=False, stop=True
                                     ).then_inc(pv_done, 1)

                score_unit(0)
                for u in range(24):
                    if u + 1 < 24:
                        score_unit(u + 1)
                    turn_unit(u)
                    if u >= 1:
                        value_unit(u - 1)
                value_unit(23)
                pe.wait_ge(o_ready, 1)
                pe.wait_ge(softmin, 24)
                q = named["out0"]
                for c in range(4):
                    transpose4(lambda m, f: o_all[:, m, c * CW + f * P:c * CW + (f + 1) * P],
                               q.turn0 - 8 + 2 * c)

            def griffin():
                pe.wait_ge(lru_in, 32)
                pe.wait_ge(conv_step, 17)
                pe.wait_ge(evac["v"], named["out1"].v0["v"])
                pe.wait_ge(evac["a"], named["out1"].v0["a"])
                for n in range(NBLK):
                    if n >= 2:
                        pe.wait_ge(r_sig, n - 1)
                    for g in range(2):
                        for e in range(2):
                            for k in range(2):
                                ins = nc.tensor.matmul(ps[:, 2 * (n % 2) + g, e * S:(e + 1) * S],
                                                       lru_w[:, g, n, k, e * P:(e + 1) * P], xc[:, 2 * n + k],
                                                       start=(k == 0), stop=(k == 1))
                    ins.then_inc(r_mm, 1)
                pe.wait_ge(r_sig, NBLK)

            pe.wait_ge(consts, 1)
            pe.wait_ge(vec_in, 16 * 11)
            for a in range(3):
                ins = nc.tensor.transpose(ps[:, 0, a * P:(a + 1) * P], vrow[:, a], ident[:])
            ins.then_inc(vec_turned, 1)
            pe.wait_ge(p_in, 32)
            for layer in range(2):
                for k in range(2):
                    for m in range(NT):
                        ins = nc.tensor.transpose(ps[:, EX + layer, k * S + m * P:k * S + (m + 1) * P],
                                                  p_tok[:, layer, m, k * P:(k + 1) * P], ident[:])
            ins.then_inc(p_turned, 1)
            for c in range(4):
                pe.wait_ge(x_in[c], 16)
                transpose4(lambda m, f: h[:, m, c * CW + f * P:c * CW + (f + 1) * P], 2 * c)
            pe.wait_ge(vec_ready, 1)
            run(pe, run_chunk, after)


def dma_no(t, s):
    return (t - s) * (16 // NRING) + 16


def src_turn0(q):
    if q.name == "qa":
        return 0
    if q.name == "out0":
        return q.turn0 - 8
    b = q.before
    return q.turn0 - b.per_turn * b.pairs


_INS = ["x", "p", "g_mix", "g_ffn", "g_ple", "g_final", "w_in_attn", "cmp_pe_k", "cmp_w1_k", "cmp_w2_k",
        "cmp_pe_v", "cmp_w1_v", "cmp_w2_v", "diff_lq1", "diff_lk1", "diff_lq2", "diff_lk2", "diff_subln",
        "w_out_attn", "w_in_rec", "conv_w", "conv_b", "lru_wa", "lru_ba", "lru_wx", "lru_bx",
        "lru_lambda", "w_out_rec", "w_ffn_gate", "w_ffn_up", "w_ffn_down", "w_ple_proj", "w_ple_gate"]
_OUTS = [((1, 256, 2048), "float32")]


def kernel(**inputs):
    import numpy as _np
    import concourse.bacc as _bacc
    from concourse import mybir as _mybir
    from concourse.bass_utils import run_bass_kernel_spmd as _run

    nc = _bacc.Bacc("TRN2", target_bir_lowering=False, num_devices=1)
    arrays, args = {}, []
    for name in _INS:
        a = _np.ascontiguousarray(inputs[name])
        arrays[f"in_{name}_dram"] = a
        args.append(nc.dram_tensor(f"in_{name}_dram", a.shape, _mybir.dt.from_np(a.dtype), kind="ExternalInput").ap())
    for i, (shape, dtype) in enumerate(_OUTS):
        dt = _mybir.dt.from_np(_np.dtype(dtype))
        args.append(nc.dram_tensor(f"out_{i}_dram", shape, dt, kind="ExternalOutput").ap())
    trunk(nc, *args)
    r = _run(nc, [arrays], core_ids=[0])
    got = tuple(r.results[0][f"out_{i}_dram"] for i in range(len(_OUTS)))
    return got[0]
```

```python
from contextlib import ExitStack
import math

import numpy as np

import concourse.bass as bass
from concourse import mybir

F32 = mybir.dt.float32
F32R = mybir.dt.float32r
BF16 = mybir.dt.bfloat16
ALU = mybir.AluOpType
ACT = mybir.ActivationFunctionType
AX_X = mybir.AxisListType.X

P = 128
NT = 2
S = NT * P
D = 2048
KD = D // P
DFF = 5632
KF = DFF // P
CW = 512
EPS = 1e-6
PLE = 256
NRING = 4

HEADS = 8
KVG = 4
HD = 128
NCMP = 15
CSTR = 16
DQK = 64
Q_A, KV_A, G_A = 0, 1024, 2560
Q_B, K_B, V_B = 2584, 3608, 4632
NGATE = 24
NEG = -1e30
BIGF = 3e38
LAM_INIT = 0.8 - 0.6 * math.exp(-0.3 * 0)
LRU_C = 8.0
NBLK = 8
XPAD = 260


class Kind:

    def __init__(self, name, evac, banks=0, split=False):
        self.name, self.evac, self.banks, self.split = name, evac, banks, split


class Phase:

    def __init__(self, name, pairs, slots, kinds, src, cols, weight, first_turn=None, loop=False,
                 gain=None, dst=None, norm=None, stat=None):
        self.name, self.pairs, self.slots, self.kinds = name, pairs, slots, kinds
        self.src, self.cols, self.weight, self.loop = src, cols, weight, loop
        self.first_turn = first_turn
        self.gain, self.dst = gain, dst
        self.norm = norm
        self.stat = stat


def build_phases():
    resid = Kind("resid", "v", 2, True)
    ph = []

    def attn(name, kinds, cols, first=False, slots=(8, 8)):
        ph.append(Phase(name, 1, slots, kinds, "B", cols, ("w_in_attn", "w_in_attn"),
                        first_turn=first, norm=0))

    qk = Kind("qk", "v", 2)
    vb = Kind("vb", "v")
    attn("qa", (qk, qk), (Q_A, Q_A + CW), first=True)
    attn("kvcs", (Kind("kvc", "v", 2), Kind("kvs", "v", 1)), (KV_A, KV_A + CW))
    attn("kvwg", (Kind("kvw", "v", 1), Kind("gates", "a")), (KV_A + 2 * CW, G_A), slots=(8, 4))
    attn("qk0", (qk, qk), (Q_B, K_B))
    attn("qk1", (qk, qk), (Q_B + CW, K_B + CW))
    attn("vb", (vb, vb), (V_B, V_B + CW))
    for layer in range(2):
        if layer:
            ph.append(Phase("xb", 2, (8, 8), (Kind("xb", "v", 2),) * 2, "B", (0, CW),
                            ("w_in_rec",) * 2, first_turn=True, norm=3))
            ph.append(Phase("yb", 2, (8, 8), (Kind("yb", "a", 2),) * 2, "B", (D, D + CW),
                            ("w_in_rec",) * 2, norm=3))
        ph.append(Phase(f"out{layer}", 2, (8, 8), (resid, resid), "B", (0, CW),
                        (("w_out_attn", "w_out_rec")[layer],) * 2, first_turn=True,
                        gain=2 + layer, dst="A", stat=1 + 3 * layer))
        ph.append(Phase(f"ffn{layer}", 11, (8, 8), (Kind("gate", "a"), Kind("up", "v", 2, True)), "A",
                        (0, 0), (f"w_gate{layer}", f"w_up{layer}"), first_turn=True, loop=True,
                        dst="H", norm=1 + 3 * layer))
        ph.append(Phase(f"down{layer}", 2, (24, 24), (resid, resid), "H", (0, CW),
                        (f"w_down{layer}",) * 2, first_turn=True, gain=4 + layer, dst="A",
                        stat=2 + 3 * layer))
        last = layer == 1
        ple = Kind("ple", "v", 0 if last else 2, True)
        ph.append(Phase(f"ple{layer}", 2, (12, 12), (ple, ple), "A",
                        (0, CW), (f"w_ple_gate{layer}",) * 2, first_turn=True,
                        gain=None if last else 1, dst=None if last else "B", norm=2 + 3 * layer,
                        stat=6 if last else 3))
    slot, va, turn, hi = 0, {"v": 0, "a": 0}, 8, 8
    for p in ph:
        if p.name == "out0":
            turn, hi = turn + 8, hi + 8
        p.slot0, p.v0, p.turn0, p.hi0 = slot, dict(va), turn, hi
        p.per_slot = sum(p.slots)
        p.per_turn = sum(k.banks for k in p.kinds)
        p.per_hi = sum(k.banks for k in p.kinds if k.split)
        p.per_v = {e: sum(k.evac == e for k in p.kinds) for e in "va"}
        slot += p.per_slot * p.pairs
        turn += p.per_turn * p.pairs
        hi += p.per_hi * p.pairs
        for e in "va":
            va[e] += p.per_v[e] * p.pairs
    for a, b in zip([None] + ph[:-1], ph):
        b.before = a
    return ph


def slot_no(p, i, r, j):
    return i * p.per_slot + (p.slot0 + r * p.slots[0] + j)


def chunk_end(p, i, r):
    return slot_no(p, i, r, p.slots[r])


def evac_no(p, i, r):
    e = p.kinds[r].evac
    before = sum(k.evac == e for k in p.kinds[:r])
    return e, i * p.per_v[e] + (p.v0[e] + before + 1)


def turn_no(p, i, r):
    return i * p.per_turn + (p.turn0 + sum(k.banks for k in p.kinds[:r]))


def hi_no(p, i, r):
    return i * p.per_hi + (p.hi0 + sum(k.banks for k in p.kinds[:r] if k.split))


def two_before(p, i, r):
    if isinstance(i, int) and i == 0:
        return (p.before, p.before.pairs - 1, r) if p.before else None
    return (p, i - 1, r)


def slot_shape(p, r, j):
    if is_proj(p, j):
        return j % 2, 1, 256 * ((j - 4) // 2), 256
    if p.slots[r] == 12:
        return 2 * (j if j < 4 else j - 4), 2, 0, CW
    if p.slots[r] == 4:
        return 4 * j, 4, 0, NGATE
    if p.slots[r] == 24:
        return (2 * j, 2, 0, CW) if j < 20 else (20 + j, 1, 0, CW)
    return 2 * j, 2, 0, CW


def is_proj(p, j):
    return p.slots[0] == 12 and 4 <= j < 8


def bank_of_ktile(p, j):
    k0, nk, _, _ = slot_shape(p, 0, j)
    return (k0 + nk - 1) // 2


AT_SOFTPLUS, AT_LAM = 10, 12
AT_CZ, AT_Z, AT_W2, AT_CSCORE = (28, 30), (29, 38), 39, 40
AT_CT = 43
AT_NSA = 48
AT_DIFF = (64, 80)
AT_VALUE = (84, 92)
AT_NORM = (89, 94)
AT_OUT = {91: (0,), 92: (1,), 93: (2,), 95: (3,)}
AT_GATE = 20
AT_EXP, AT_SQRT, AT_SCAN = 26, 28, 30
AT_PROD = {44: 0, 52: 1, 60: 2, 67: 3}
AT_SPLIT = {63: 0, 64: 1, 65: 2, 67: 3}


def unit_at(t, lag):
    t -= lag
    if AT_NSA <= t < AT_NSA + 16:
        return t - AT_NSA
    for n, first in enumerate(AT_DIFF):
        if first <= t < first + 8:
            return 16 + 8 * n + t - first
    return None


def trunk(nc, x, p, g_mix, g_ffn, g_ple, g_final, w_in_attn, cmp_pe_k, cmp_w1_k, cmp_w2_k,
          cmp_pe_v, cmp_w1_v, cmp_w2_v, diff_lq1, diff_lk1, diff_lq2, diff_lk2, diff_subln,
          w_out_attn, w_in_rec, conv_w, conv_b, lru_wa, lru_ba, lru_wx, lru_bx, lru_lambda,
          w_out_rec, w_ffn_gate, w_ffn_up, w_ffn_down, w_ple_proj, w_ple_gate, out):
    phases = build_phases()
    named = {q.name: q for q in phases}
    ctx = ExitStack()
    with ctx:
        base = (nc.sbuf_base + 63) // 64 * 64
        size = nc.sbuf_usable_end - 64 - base
        ctx.enter_context(nc.sbuf_tensor("slab", [P, size - 64], mybir.dt.uint8))
        top = [base]

        def at(name, shape, dt, offset):
            return nc.alloc_sbuf_tensor_at(name, [P, *shape], dt, offset=offset)

        def put(name, shape, dt=F32):
            n = int(np.prod(shape)) * (2 if dt == BF16 else 4)
            t = at(name, shape, dt, top[0])
            top[0] += (n + 31) // 32 * 32
            return t

        h = put("h", [NT, D])
        raw = put("raw", [NRING, 2 * CW])
        w_hi = put("w_hi", [NRING, 2 * CW], F32R)
        w_lo = put("w_lo", [NRING, 2 * CW], F32R)
        stage = put("stage", [NT, CW])
        sg = put("sg", [NT, CW])
        junk = put("junk", [CW], BF16)
        pT_off = top[0]
        pT_hi = put("pT_hi", [2, 2, S], F32R)
        pT_lo = put("pT_lo", [2, 2, S], F32R)
        vecT = put("vecT", [3, P])
        ident = put("ident", [P])
        maskd = put("maskd", [3, P])
        maskc = put("maskc", [NT, 16])
        validc = put("validc", [NT, 16])
        gates_sb = put("gates_sb", [NT, NGATE])
        gcol = put("gcol", [KD])
        ssq = put("ssq", [7, NT, 4])
        rstd = put("rstd", [7, NT])
        tiny = put("tiny", [16])
        nmax = put("nmax", [2, NT])
        esum = put("esum", [2, NT])
        coef = put("coef", [4, NT])
        kcT = put("kcT", [2, 16])
        csum = put("csum", [4, 16])
        ssqb = put("ssqb", [NT, HEADS])
        rstdb = put("rstdb", [NT, HEADS])
        sp_t = put("sp_t", [6, KD])
        a_off = top[0]
        big = a_off + 2 * KD * S * 4
        s_off = big + 2 * KD * S * 4
        assert big + 2 * KF * S * 4 <= base + size - 64, (big + 2 * KF * S * 4, base + size)
        X = {"A": (at("xa_hi", [KD, S], F32R, a_off), at("xa_lo", [KD, S], F32R, a_off + KD * S * 4)),
             "B": (at("xb_hi", [KD, S], F32R, big), at("xb_lo", [KD, S], F32R, big + KD * S * 4)),
             "H": (at("hid_hi", [KF, S], F32R, big), at("hid_lo", [KF, S], F32R, big + KF * S * 4))}
        vrow = at("vrow", [3, P], F32, s_off + 28672)
        p_tok = at("p_tok", [2, NT, PLE], F32, s_off)
        qaT = at("qaT", [HEADS, S], F32, a_off)
        qbT = at("qbT", [HEADS, S], F32, a_off + 8192)
        w1 = at("w1", [32, HD], F32, a_off + 16384)
        probTd = at("probTd", [HEADS, 3 * P], F32, a_off + 16384)
        kbT = at("kbT", [HEADS, S], F32, s_off)
        vtok = at("vtok", [2, NT, 2 * HD], F32, s_off + 8192)
        vb_tok = at("vb_tok", [NT, 2 * CW], F32, s_off + 12288)
        kT = at("kT", [2, 2, S], F32, s_off + 20480)
        cmpT = at("cmpT", [4, S], F32, s_off + 24576)
        o_all = at("o_all", [NT, D], F32, s_off + 28672)
        w2 = at("w2", [2, HD], F32, s_off + 45056)
        lam_in = at("lam_in", [4, DQK], F32, s_off + 46080)
        cz = at("cz", [2, 2, NCMP * CSTR], F32, s_off + 47104)
        pc_T = at("pc_T", [2, 4, P], F32, s_off + 50944)
        vc = at("vc", [2, HD], F32, s_off + 55040)
        sc_s = at("sc_s", [16, 16], F32, s_off + 56064)
        gz = at("gz", [2, 2 * NCMP + 2], F32, s_off + 57088)
        prob = at("prob", [2, CW], F32, pT_off)
        prob2 = at("prob2", [S], F32, pT_off + 4096)
        probT = at("probT", [2, 3 * P], F32, pT_off + 5120)
        lru_w = at("lru_w", [2, NBLK, 2, 2 * P], F32, a_off)
        decay = at("decay", [KD, S], F32, a_off)
        th = at("th", [KD, S], F32, a_off + KD * S * 4)
        xbT = at("xbT", [KD, XPAD], F32, s_off)
        xc = at("xc", [KD, S], F32, s_off + KD * XPAD * 4)
        yT = at("yT", [KD, S], F32, s_off + KD * XPAD * 4 + KD * S * 4)
        i_t = at("i_t", [2, 2, S], F32, s_off + KD * XPAD * 4 + 2 * KD * S * 4)
        gf = at("gf", [D], F32, s_off)
        fin = at("fin", [NT, D], F32, s_off + 8192)

        ps = ctx.enter_context(nc.psum_tensor("ps", [P, 8, CW], F32))
        TP, EX = 4, 6

        def sem(name):
            return ctx.enter_context(nc.semaphore(name))

        x_in = [sem(f"x_in{c}") for c in range(4)]
        vec_in = sem("vec_in")
        p_in = sem("p_in")
        raw_in = [sem(f"raw_in{s}") for s in range(NRING)]
        hi_ready, lo_ready, w_used = sem("hi_ready"), sem("lo_ready"), sem("w_used")
        evac = {"v": sem("evac_v"), "a": sem("evac_a")}
        turned, turn_hi, turn_used = sem("turned"), sem("turn_hi"), sem("turn_used")
        consts = sem("consts")
        pool_step = sem("pool_step")
        vrow_clear = sem("vrow_clear")
        sg_ready = sem("sg_ready")
        vec_turned, vec_ready = sem("vec_turned"), sem("vec_ready")
        p_turned, p_hi, p_ready = sem("p_turned"), sem("p_hi"), sem("p_ready")
        gcol_ready = sem("gcol_ready")
        ssq_ready, ms_ready, rms_ready, rstd_ready = (sem("ssq_ready"), sem("ms_ready"),
                                                      sem("rms_ready"), sem("rstd_ready"))
        dve_step = sem("dve_step")
        ple_step = sem("ple_step")
        w1_in, w2_in, lam_in_sem = [sem("w1_in_k"), sem("w1_in_v")], sem("w2_in"), sem("lam_in")
        map0_scored = sem("map0_scored")
        scored, softmin, expd, prob_ready = sem("scored"), sem("softmin"), sem("expd"), sem("prob_ready")
        pT_made, pT_ready, pv_done, o_done = sem("pT_made"), sem("pT_ready"), sem("pv_done"), sem("o_done")
        cz_ready, z_done, gelu_done, w2_done, kv_cmp = (sem("cz_ready"), sem("z_done"), sem("gelu_done"),
                                                        sem("w2_done"), sem("kv_cmp"))
        c_scored, c_shift, c_exp, c_prob = sem("c_scored"), sem("c_shift"), sem("c_exp"), sem("c_prob")
        c_T, c_Tr, c_pv, c_out = sem("c_T"), sem("c_Tr"), sem("c_pv"), sem("c_out")
        lam_dots, lam_exps = sem("lam_dots"), sem("lam_exps")
        sp_arg, sp_exp = sem("sp_arg"), sem("sp_exp")
        b_sq, b_ms, b_rms, o_ready = sem("b_sq"), sem("b_ms"), sem("b_rms"), sem("o_ready")
        conv_step = sem("conv_step")
        lru_in = sem("lru_in")
        r_mm, r_sig, i_used = sem("r_mm"), sem("r_sig"), sem("i_used")
        r_exp, r_m, r_sqrt, r_h, r_hi, r_lo = (sem("r_exp"), sem("r_m"), sem("r_sqrt"), sem("r_h"),
                                               sem("r_hi"), sem("r_lo"))
        coef_ready, r_scan = sem("coef_ready"), sem("r_scan")
        gf_in, fin_ready, stored = sem("gf_in"), sem("fin_ready"), sem("stored")

        W = {"w_in_attn": w_in_attn[0], "w_out_attn": w_out_attn[0], "w_in_rec": w_in_rec[0],
             "w_out_rec": w_out_rec[0]}
        for layer in range(2):
            W[f"w_gate{layer}"] = w_ffn_gate[layer]
            W[f"w_up{layer}"] = w_ffn_up[layer]
            W[f"w_down{layer}"] = w_ffn_down[layer]
            W[f"w_ple_gate{layer}"] = w_ple_gate[layer]
            W[f"w_ple_proj{layer}"] = w_ple_proj[layer]
        W = {k: v.rearrange("(k p) n -> p k n", p=P) for k, v in W.items()}

        GAIN = {0: 0, 1: 16, 3: 48, 4: 64, 5: 80}

        def gain_ap(g, k):
            return vecT[:, 0, k + 16 * g:k + 16 * g + 1]


        def walk(run_chunk, after):
            prev = None
            for q in phases:
                run_chunk(q, 0, 0, prev)
                run_chunk(q, 0, 1, (q, 0, 0))
                prev = (q, q.pairs - 1, 1)
                if q.loop:
                    yield q, run_chunk
                else:
                    for i in range(1, q.pairs):
                        run_chunk(q, i, 0, (q, i - 1, 1))
                        run_chunk(q, i, 1, (q, i, 0))
            after(prev)

        def run(eng, run_chunk, after):
            for q, step in walk(run_chunk, after):
                with eng.Fori(1, q.pairs) as i:
                    step(q, i, 0, (q, i - 1, 1))
                    step(q, i, 1, (q, i, 0))

        block = ctx.enter_context(nc.Block())

        @block.sync
        def _(sp):
            def load_slot(q, i, r, j):
                t = slot_no(q, i, r, j)
                s = j % NRING
                k0, nk, c0, w = slot_shape(q, r, j)
                if not (isinstance(t, int) and t < NRING):
                    sp.wait_ge(lo_ready, t - (NRING - 1))
                col = q.cols[r] + c0 + i * (CW if q.loop else 2 * CW)
                weight = q.weight[r].replace("gate", "proj") if is_proj(q, j) else q.weight[r]
                src = W[weight][:, k0:k0 + nk, bass.ds(col, w)]
                dst = raw[:, s, 0:nk * w].rearrange("p (k n) -> p k n", k=nk)
                sp.dma_start(dst, src).then_inc(raw_in[s], 16)

            def run_chunk(q, i, r, prev):
                for j in range(q.slots[r]):
                    if q.name == "qa" and r == 0 and j < 4:
                        sp.dma_start(h[:, :, j * CW:(j + 1) * CW],
                                     x[0].rearrange("(m p) d -> p m d", p=P)[:, :, j * CW:(j + 1) * CW]
                                     ).then_inc(x_in[j], 16)
                    load_slot(q, i, r, j)
                if q.name == "qa" and r == 1:
                    sp.dma_start(w1[:], cmp_w1_k[0].rearrange("l d e -> d l e")).then_inc(w1_in[0], 16)
                    sp.dma_start(w2[:, 0, :], cmp_w2_k[0]).then_inc(w2_in, 16)
                    sp.dma_start(w2[:, 1, :], cmp_w2_v[0]).then_inc(w2_in, 16)
                    for n, v in enumerate((diff_lq1, diff_lk1, diff_lq2, diff_lk2)):
                        sp.dma_start(lam_in[:, n, :], v[0].partition_broadcast(P)).then_inc(lam_in_sem, 16)
                if q.name == "kvwg" and r == 1:
                    sp.wait_ge(z_done, 1)
                    sp.dma_start(w1[:], cmp_w1_v[0].rearrange("l d e -> d l e")).then_inc(w1_in[1], 16)
                if q.name == "out0" and i == 0 and r == 1:
                    sp.wait_ge(scored, 32)
                    for layer in range(2):
                        sp.dma_start(p_tok[:, layer], p[layer, 0].rearrange("(m p) e -> p m e", p=P)
                                     ).then_inc(p_in, 16)
                if q.name == "xb" and i == 0 and r == 1:
                    sp.wait_ge(w_used, q.slot0)
                    for n, w in enumerate((lru_wa, lru_wx)):
                        sp.dma_start(lru_w[:, n], w[0].rearrange("b (k p) e -> p b k e", p=P)
                                     ).then_inc(lru_in, 16)
                if q.name == "ple1" and i == 0 and r == 1:
                    sp.wait_ge(w_used, q.slot0)
                    sp.dma_start(gf[:], g_final.partition_broadcast(P)).then_inc(gf_in, 16)

            def after(prev):
                for n in range(4):
                    m, half = divmod(n, 2)
                    cols = slice(half * D // 2, (half + 1) * D // 2)
                    sp.wait_ge(fin_ready, n + 1)
                    sp.dma_start(out[0].rearrange("(m p) d -> p m d", p=P)[:, m, cols], fin[:, m, cols]
                                 ).then_inc(stored, 16)
                sp.wait_ge(stored, 16 * 4)

            run(sp, run_chunk, after)

        @block.gpsimd
        def _(pool):
            n = 0

            def step(ins):
                nonlocal n
                n += 1
                ins.then_inc(pool_step, 1)
                pool.wait_ge(pool_step, n)

            nc.gpsimd.memset(vrow[:], 0.0).then_inc(vrow_clear, 1)
            step(nc.gpsimd.memset(ident[:], 0.0))
            step(nc.gpsimd.memset(maskd[:], 0.0))
            step(nc.gpsimd.memset(maskc[:], 0.0))
            step(nc.gpsimd.memset(validc[:], 1.0))
            step(nc.gpsimd.memset(ssq[:], 0.0))
            step(nc.gpsimd.affine_select(out=ident[:], in_=ident[:], compare_op=ALU.not_equal, fill=1.0,
                                         base=0, pattern=[[-1, P]], channel_multiplier=1))
            for b in (0, 2):
                step(nc.gpsimd.affine_select(out=maskd[:, b], in_=maskd[:, b], compare_op=ALU.is_ge,
                                             fill=NEG, base=0, pattern=[[-1, P]], channel_multiplier=1))
            for t, fill in ((maskc, NEG), (validc, 0.0)):
                for m in range(NT):
                    step(nc.gpsimd.affine_select(out=t[:, m], in_=t[:, m], compare_op=ALU.is_ge,
                                                 fill=fill, base=m * P - (2 * CSTR - 1),
                                                 pattern=[[-CSTR, 16]], channel_multiplier=1))
            nc.gpsimd.memset(tiny[:], 0.0).then_inc(consts, 1)

        @block.scalar
        def _(act):
            def split_slot(q, i, r, j):
                t = slot_no(q, i, r, j)
                s = j % NRING
                _, nk, _, w = slot_shape(q, r, j)
                n = nk * w
                act.wait_ge(raw_in[s], dma_no(t, s))
                if not (isinstance(t, int) and t < NRING):
                    act.wait_ge(w_used, t - (NRING - 1))
                nc.scalar.activation(w_hi[:, s, 0:n], raw[:, s, 0:n], ACT.Copy).then_inc(hi_ready, 1)

            def evacuate(q, i, r):
                kind = q.kinds[r].name
                if q.kinds[r].evac != "a" and kind != "ple":
                    return
                act.wait_ge(w_used, chunk_end(q, i, r))
                act.wait_ge(rstd_ready, q.norm + 1)
                for m in range(NT):
                    acc = ps[:, 2 * r + m, :]
                    rs = rstd[:, q.norm, m:m + 1]
                    if kind == "gates":
                        ins = nc.scalar.activation(gates_sb[:, m], acc[:, 0:NGATE], ACT.Sigmoid, scale=rs)
                    elif kind == "gate":
                        if m == 0 and not (isinstance(i, int) and i == 0):
                            act.wait_ge(evac["v"], evac_no(q, i - 1, 1)[1])
                        ins = nc.scalar.activation(sg[:, m], acc, ACT.Silu, scale=rs)
                    elif kind == "ple":
                        if m == 0 and 2 * i + r > 0:
                            act.wait_ge(evac["v"], evac_no(q, i, r)[1] - 1)
                        ins = nc.scalar.activation(sg[:, m], acc, ACT.Sigmoid, scale=rs)
                    else:
                        if m == 0:
                            act.wait_ge(turned, turn_no(q, i, r))
                        ins = nc.scalar.activation(stage[:, m], acc, ACT.Gelu_apprx_tanh, scale=rs)
                ins.then_inc(sg_ready if kind == "ple" else evac["a"], 1)

            def turn_split(dst, k0, t0, gain):
                for b in range(2):
                    act.wait_ge(turned, t0 + (b + 1))
                    for f in range(2):
                        o = dst[0][:, k0 + 2 * b + f, :] if isinstance(k0, int) else \
                            dst[0][:, bass.ds(k0 + (2 * b + f), 1), :]
                        src = ps[:, TP + b, f * S:(f + 1) * S]
                        if gain is None:
                            ins = nc.scalar.activation(o, src, ACT.Copy)
                        else:
                            ins = nc.scalar.activation(o, src, ACT.Copy, scale=gain(k0 + 2 * b + f))
                    ins.then_inc(turn_hi, 1)

            def squares(stat, c):
                for m in range(NT):
                    n = (4 * stat + c) * NT + m
                    if n:
                        act.wait_ge(ssq_ready, n)
                    nc.scalar.activation(junk[:], h[:, m, c * CW:(c + 1) * CW], ACT.Square,
                                         accum_out=ssq[:, stat, m, c:c + 1]).then_inc(ssq_ready, 1)

            def root(stat):
                act.wait_ge(ms_ready, stat + 1)
                nc.scalar.activation(rstd[:, stat], rstd[:, stat], ACT.Sqrt).then_inc(rms_ready, 1)

            def aftermath(q, i, r):
                k = q.kinds[r]
                col = i if q.loop else 2 * i + r
                if k.split and k.banks:
                    g = (lambda kt: gain_ap(q.gain, kt)) if q.gain is not None else None
                    turn_split(X[q.dst], 4 * col, turn_no(q, i, r), g)
                if q.stat is not None:
                    act.wait_ge(evac["v"], evac_no(q, i, r)[1])
                    squares(q.stat, col)
                    if col == 3:
                        root(q.stat)

            def run_chunk(q, i, r, prev):
                host = 4 if q.slots[r] == 4 else 8
                for j in range(q.slots[r]):
                    split_slot(q, i, r, j)
                    if not prev and j < 4:
                        continue
                    if prev and j == host - 1 and host == 8:
                        aftermath(*prev)
                    if q.norm == 0 or q.name == "out0":
                        attention(slot_no(q, i, r, j) - NRING)
                    if q.norm == 3 or q.name == "out1":
                        griffin(slot_no(q, i, r, j) - NRING - named["xb"].slot0)
                    if prev and j == 3:
                        evacuate(*prev)
                        if host == 4:
                            aftermath(*prev)
                    if q.name == "ffn0" and isinstance(i, int) and r == 0 and j == 1:
                        act.wait_ge(p_turned, 1)
                        for layer in range(2):
                            ins = nc.scalar.activation(
                                pT_hi[:, layer], ps[:, EX + layer, :].rearrange("p (k t) -> p k t", k=2), ACT.Copy)
                        ins.then_inc(p_hi, 1)

            def after(prev):
                evacuate(*prev)
                aftermath(*prev)

            def attention(t):
                if t == AT_SOFTPLUS:
                    act.wait_ge(sp_arg, 1)
                    nc.scalar.activation(sp_t[:, 1], sp_t[:, 0], ACT.Exp, scale=-1.0).then_inc(sp_exp, 1)
                if t == AT_LAM:
                    act.wait_ge(lam_dots, 1)
                    nc.scalar.activation(tiny[:, 2:4], tiny[:, 0:2], ACT.Exp).then_inc(lam_exps, 1)
                if t in AT_Z:
                    kind = AT_Z.index(t)
                    act.wait_ge(z_done, kind + 1)
                    nc.scalar.activation(gz[:, kind, 0:2 * NCMP], ps[:, EX + kind, 0:2 * NCMP],
                                         ACT.Gelu_apprx_tanh).then_inc(gelu_done, 1)
                if t == AT_CSCORE:
                    act.wait_ge(c_shift, 1)
                    nc.scalar.activation(sc_s[:, :, 0:NCMP], sc_s[:, :, 0:NCMP], ACT.Exp, scale=HD ** -0.5
                                         ).then_inc(c_exp, 1)
                if AT_CT <= t < AT_CT + 4:
                    b = t - AT_CT
                    act.wait_ge(c_T, b + 1)
                    if b >= 2:
                        act.wait_ge(c_pv, b - 1)
                    nc.scalar.activation(pc_T[0:NCMP, b % 2],
                                         ps[0:NCMP, EX, :].rearrange("p (a t) -> p a t", a=4),
                                         ACT.Copy).then_inc(c_Tr, 1)
                if (u := unit_at(t, 0)) is not None:
                    act.wait_ge(softmin, u + 1)
                    for n, cols in enumerate(unit_parts(u)):
                        pr = prob[:, u % 2, cols]
                        ins = nc.scalar.activation(pr, pr, ACT.Exp, scale=-1.0, bias=nmax[:, u % 2, n:n + 1],
                                                   accum_out=esum[:, u % 2, n:n + 1])
                    ins.then_inc(expd, 1)
                if (u := unit_at(t, 2)) is not None:
                    act.wait_ge(pT_made, u + 1)
                    if u < 16:
                        if u >= 2:
                            act.wait_ge(pv_done, u - 1)
                        o, n = probT[:, u % 2], 3 * P
                    else:
                        hd, m = divmod(u - 16, NT)
                        o = probTd[:, hd, (0, P)[m]:(P, 3 * P)[m]]
                        n = P * (m + 1)
                    nc.scalar.activation(o, ps[:, TP + u % 2, 0:n], ACT.Copy).then_inc(pT_ready, 1)
                for grp, heads in heads_at(t - 1):
                    for hd in heads:
                        act.wait_ge(o_done, 16 + hd + 1)
                        for m in range(NT):
                            n = NT * hd + m
                            if n:
                                act.wait_ge(b_sq, n)
                            nc.scalar.activation(junk[:, 0:P], o_all[:, m, (HEADS + hd) * P:(HEADS + hd + 1) * P],
                                                 ACT.Square, accum_out=ssqb[:, m, hd:hd + 1]).then_inc(b_sq, 1)
                if t in AT_NORM:
                    g = AT_NORM.index(t)
                    act.wait_ge(b_ms, g + 1)
                    r4 = rstdb[:, :, 4 * g:4 * g + 4]
                    nc.scalar.activation(r4, r4, ACT.Sqrt).then_inc(b_rms, 1)
                for c in AT_OUT.get(t, ()):
                    turn_split(X["B"], 4 * c, named["out0"].turn0 - 8 + 2 * c,
                               lambda kt: gcol[:, kt:kt + 1])

            def griffin(t):
                n, off = divmod(t - AT_GATE, 4)
                if off == 0 and 0 <= n < NBLK:
                    act.wait_ge(r_mm, n + 1)
                    if n >= 2:
                        act.wait_ge(i_used, n - 1)
                    for g in range(2):
                        for e in range(2):
                            f = 2 * n + e
                            o = xbT[:, f, 0:S] if g == 0 else i_t[:, n % 2, e]
                            ins = nc.scalar.activation(o, ps[:, EX + g, e * S:(e + 1) * S],
                                                       ACT.Sigmoid, bias=vecT[:, 1, 80 + 16 * g + f:81 + 16 * g + f])
                    ins.then_inc(r_sig, 1)
                g, off = divmod(t - AT_EXP, 8)
                if off == 0 and 0 <= g < 4:
                    act.wait_ge(coef_ready, 1)
                    act.wait_ge(r_sig, 2 * g + 2)
                    for f in range(4 * g, 4 * g + 4):
                        nc.scalar.activation(decay[:, f], xbT[:, f, 0:S], ACT.Exp, scale=sp_t[:, 4, f:f + 1])
                        ins = nc.scalar.activation(th[:, f], xbT[:, f, 0:S], ACT.Tanh, scale=sp_t[:, 5, f:f + 1])
                    ins.then_inc(r_exp, 1)
                g, off = divmod(t - AT_SQRT, 8)
                if off == 0 and 0 <= g < 4:
                    act.wait_ge(r_m, g + 1)
                    nc.scalar.activation(xbT[:, 4 * g:4 * g + 4, 0:S], th[:, 4 * g:4 * g + 4], ACT.Sqrt
                                         ).then_inc(r_sqrt, 1)
                if t in AT_SPLIT:
                    g = AT_SPLIT[t]
                    act.wait_ge(r_h, g + 1)
                    act.wait_ge(w_used, named["out1"].slot0)
                    nc.scalar.activation(X["B"][0][:, 4 * g:4 * g + 4], xc[:, 4 * g:4 * g + 4], ACT.Copy
                                         ).then_inc(r_hi, 1)

            act.wait_ge(vrow_clear, 1)
            for dst, src in ((vrow[0:32, 0], g_mix.rearrange("a (k p) -> (a k) p", p=P)),
                             (vrow[32:64, 0], g_ffn.rearrange("a (k p) -> (a k) p", p=P)),
                             (vrow[64:96, 0], g_ple.rearrange("a (k p) -> (a k) p", p=P)),
                             (vrow[96:104, 0], diff_subln[0]),
                             (vrow[0:64, 1], conv_w[0].rearrange("a (k p) -> (a k) p", p=P)),
                             (vrow[64:80, 1], conv_b[0].rearrange("(k p) -> k p", p=P)),
                             (vrow[80:96, 1], lru_ba[0].rearrange("(k p) -> k p", p=P)),
                             (vrow[96:112, 1], lru_bx[0].rearrange("(k p) -> k p", p=P)),
                             (vrow[112:128, 1], lru_lambda[0].rearrange("(k p) -> k p", p=P)),
                             (vrow[0:32, 2], cmp_pe_k[0]),
                             (vrow[32:64, 2], cmp_pe_v[0])):
                act.dma_start(dst, src).then_inc(vec_in, 16)
            act.wait_ge(vec_ready, 1)
            for c in range(4):
                turn_split(X["B"], 4 * c, 2 * c, lambda kt: gain_ap(0, kt))
                squares(0, c)
            root(0)
            run(act, run_chunk, after)

        @block.vector
        def _(dve):
            steps = 0

            def step(ins):
                nonlocal steps
                steps += 1
                ins.then_inc(dve_step, 1)
                dve.wait_ge(dve_step, steps)

            def split_slot(q, i, r, j):
                t = slot_no(q, i, r, j)
                s = j % NRING
                _, nk, _, w = slot_shape(q, r, j)
                n = nk * w
                dve.wait_ge(hi_ready, t + 1)
                nc.vector.tensor_tensor(w_lo[:, s, 0:n], raw[:, s, 0:n], w_hi[:, s, 0:n].bitcast(F32),
                                        ALU.subtract).then_inc(lo_ready, 1)

            def evacuate(q, i, r):
                k = q.kinds[r]
                kind = k.name
                if k.evac != "v":
                    return
                dve.wait_ge(w_used, chunk_end(q, i, r))
                if kind in ("qk", "kvc", "kvs", "kvw", "xb", "up"):
                    dve.wait_ge(turned, turn_no(q, i, r))
                if q.norm is not None and kind != "ple":
                    dve.wait_ge(rstd_ready, q.norm + 1)
                if kind == "up":
                    dve.wait_ge(evac["a"], evac_no(q, i, 0)[1])
                if kind == "ple":
                    dve.wait_ge(sg_ready, 4 * (q.name == "ple1") + 2 * i + r + 1)
                for m in range(NT):
                    acc = ps[:, 2 * r + m, :]
                    rs = rstd[:, q.norm, m:m + 1] if q.norm is not None else None
                    if kind == "resid":
                        o = h[:, m, (2 * i + r) * CW:(2 * i + r + 1) * CW]
                        ins = nc.vector.tensor_tensor(o, acc, o, ALU.add)
                    elif kind == "ple":
                        c = 2 * i + r
                        nc.vector.tensor_tensor(stage[:, m], ps[:, EX + m, :], sg[:, m], ALU.mult
                                                ).then_inc(ple_step, 1)
                        dve.wait_ge(ple_step, 8 * (q.name == "ple1") + NT * c + m + 1)
                        o = h[:, m, c * CW:(c + 1) * CW]
                        ins = nc.vector.tensor_tensor(o, o, stage[:, m], ALU.add)
                    elif kind in ("kvs", "kvw"):
                        which = int(kind == "kvw")
                        nc.vector.tensor_scalar(vtok[:, which, m], acc[:, S:2 * S], rs, None, ALU.mult)
                        ins = nc.vector.tensor_scalar(stage[:, m, 0:S], acc[:, 0:S], rs, None, ALU.mult)
                    elif kind == "up":
                        ins = nc.vector.scalar_tensor_tensor(out=stage[:, m], in0=acc, scalar=rs, in1=sg[:, m],
                                                             op0=ALU.mult, op1=ALU.mult)
                    else:
                        o = {"qk": lambda: stage[:, m], "xb": lambda: stage[:, m],
                             "kvc": lambda: stage[:, m],
                             "vb": lambda: vb_tok[:, m, r * CW:(r + 1) * CW]}[kind]()
                        ins = nc.vector.tensor_scalar(o, acc, rs, None, ALU.mult)
                ins.then_inc(evac["v"], 1)

            def turn_split(dst, k0, h0, gain):
                for b in range(2):
                    dve.wait_ge(turn_hi, h0 + (b + 1))
                    for f in range(2):
                        if isinstance(k0, int):
                            hi, lo = (dst[z][:, k0 + 2 * b + f, :] for z in range(2))
                        else:
                            hi, lo = (dst[z][:, bass.ds(k0 + (2 * b + f), 1), :] for z in range(2))
                        src = ps[:, TP + b, f * S:(f + 1) * S]
                        if gain is None:
                            ins = nc.vector.tensor_tensor(lo, src, hi.bitcast(F32), ALU.subtract)
                        else:
                            ins = nc.vector.scalar_tensor_tensor(
                                out=lo, in0=src, scalar=gain(k0 + 2 * b + f), in1=hi.bitcast(F32),
                                op0=ALU.mult, op1=ALU.subtract)
                    ins.then_inc(turn_used, 1)

            def mean_square(stat):
                dve.wait_ge(ssq_ready, 4 * NT * (stat + 1))
                step(nc.vector.tensor_reduce(rstd[:, stat], ssq[:, stat], AX_X, ALU.add))
                nc.vector.tensor_scalar(rstd[:, stat], rstd[:, stat], 1.0 / D, EPS, ALU.mult, ALU.add
                                        ).then_inc(ms_ready, 1)
                dve.wait_ge(rms_ready, stat + 1)
                nc.vector.reciprocal(rstd[:, stat], rstd[:, stat]).then_inc(rstd_ready, 1)
                dve.wait_ge(rstd_ready, stat + 1)

            def aftermath(q, i, r):
                k = q.kinds[r]
                col = i if q.loop else 2 * i + r
                t0 = turn_no(q, i, r)
                if k.split and k.banks:
                    g = (lambda kt: gain_ap(q.gain, kt)) if q.gain is not None else None
                    turn_split(X[q.dst], 4 * col, hi_no(q, i, r), g)
                elif k.banks:
                    for b in range(k.banks):
                        dve.wait_ge(turned, t0 + b + 1)
                        src = ps[:, TP + (t0 + b) % 2, :].rearrange("p (f t) -> p f t", f=2)
                        c = 4 * r + 2 * b
                        g = 4 * (q.name == "qk1") + 2 * b
                        o = {"qa": lambda: qaT[:, c:c + 2],
                             "qk0": lambda: (qbT, kbT)[r][:, g:g + 2], "qk1": lambda: (qbT, kbT)[r][:, g:g + 2],
                             "kvcs": lambda: cmpT[:, c:c + 2] if r == 0 else kT[:, 0],
                             "kvwg": lambda: kT[:, 1],
                             "xb": lambda: xbT[:, 8 * i + c:8 * i + c + 2, 3:3 + S],
                             "yb": lambda: yT[:, 8 * i + c:8 * i + c + 2]}[q.name]()
                        nc.vector.tensor_copy(o, src).then_inc(turn_used, 1)
                if k.name == "xb":
                    conv(2 * i + r)
                if q.stat is not None and col == 3:
                    mean_square(q.stat)

            def conv(c):
                dve.wait_ge(turn_used, named["xb"].turn0 + 2 * c + 2)
                for tap in range(4):
                    if tap:
                        dve.wait_ge(conv_step, 1 + 4 * c + tap)
                    for f in range(4 * c, 4 * c + 4):
                        src = xbT[:, f, 3 - tap:3 - tap + S]
                        w = vecT[:, 1, 16 * (3 - tap) + f:16 * (3 - tap) + f + 1]
                        if tap == 0:
                            ins = nc.vector.tensor_scalar(xc[:, f], src, w, vecT[:, 1, 64 + f:65 + f],
                                                          ALU.mult, ALU.add)
                        else:
                            ins = nc.vector.scalar_tensor_tensor(out=xc[:, f], in0=src, scalar=w, in1=xc[:, f],
                                                                 op0=ALU.mult, op1=ALU.add)
                    ins.then_inc(conv_step, 1)

            def run_chunk(q, i, r, prev):
                host = 4 if q.slots[r] == 4 else 8
                for j in range(q.slots[r]):
                    split_slot(q, i, r, j)
                    if not prev and j < 4:
                        continue
                    if prev and j == host - 1 and host == 8:
                        aftermath(*prev)
                    if q.norm == 0 or q.name == "out0":
                        attention(slot_no(q, i, r, j) - NRING)
                    if q.norm == 3 or q.name == "out1":
                        griffin(slot_no(q, i, r, j) - NRING - named["xb"].slot0)
                    if prev and j == 3:
                        evacuate(*prev)
                        if host == 4:
                            aftermath(*prev)
                    if q.name == "ffn0" and isinstance(i, int) and r == 0 and j == 1:
                        dve.wait_ge(p_hi, 1)
                        for layer in range(2):
                            ins = nc.vector.tensor_tensor(
                                pT_lo[:, layer], ps[:, EX + layer, :].rearrange("p (k t) -> p k t", k=2),
                                pT_hi[:, layer].bitcast(F32), ALU.subtract)
                        ins.then_inc(p_ready, 1)
                if q.name == "xb" and i == 0 and r == 0:
                    dve.wait_ge(turned, named["xb"].turn0)
                    nc.vector.memset(xbT[:, :, 0:3], 0.0).then_inc(conv_step, 1)
                    dve.wait_ge(conv_step, 1)

            def after(prev):
                evacuate(*prev)
                aftermath(*prev)
                dve.wait_ge(gf_in, 16)
                for n in range(4):
                    m, half = divmod(n, 2)
                    cols = slice(half * D // 2, (half + 1) * D // 2)
                    nc.vector.scalar_tensor_tensor(out=fin[:, m, cols], in0=h[:, m, cols],
                                                   scalar=rstd[:, 6, m:m + 1], in1=gf[:, cols],
                                                   op0=ALU.mult, op1=ALU.mult).then_inc(fin_ready, 1)

            g3 = gates_sb[:, :, :].rearrange("p m (a b) -> p m a b", b=3)

            def softplus_argument():
                lam = vecT[:, 1, 112:128]
                step(nc.vector.tensor_scalar(sp_t[:, 2], lam, -1.0, None, ALU.mult))
                nc.vector.tensor_tensor(sp_t[:, 0], sp_t[:, 2], lam, ALU.max).then_inc(sp_arg, 1)

            def softplus():
                step(nc.vector.tensor_scalar(sp_t[:, 2], sp_t[:, 2], 0.0, None, ALU.max))
                dve.wait_ge(sp_exp, 1)
                step(nc.vector.tensor_scalar(sp_t[:, 3], sp_t[:, 1], 2.0, None, ALU.add))
                step(nc.vector.reciprocal(sp_t[:, 3], sp_t[:, 3]))
                step(nc.vector.tensor_tensor(sp_t[:, 1], sp_t[:, 1], sp_t[:, 3], ALU.mult))
                step(nc.vector.tensor_tensor(sp_t[:, 3], sp_t[:, 1], sp_t[:, 1], ALU.mult))
                step(nc.vector.tensor_scalar(sp_t[:, 4], sp_t[:, 3], 1.0 / 17, 1.0 / 15, ALU.mult, ALU.add))
                for n in range(13, 0, -2):
                    step(nc.vector.tensor_tensor(sp_t[:, 4], sp_t[:, 4], sp_t[:, 3], ALU.mult))
                    step(nc.vector.tensor_scalar(sp_t[:, 4], sp_t[:, 4], 1.0 / n, None, ALU.add))
                step(nc.vector.tensor_tensor(sp_t[:, 4], sp_t[:, 4], sp_t[:, 1], ALU.mult))
                step(nc.vector.tensor_scalar(sp_t[:, 4], sp_t[:, 4], 2.0, None, ALU.mult))
                step(nc.vector.tensor_tensor(sp_t[:, 5], sp_t[:, 4], sp_t[:, 2], ALU.add))
                step(nc.vector.tensor_scalar(sp_t[:, 5], sp_t[:, 5], LRU_C, None, ALU.mult))
                nc.vector.tensor_scalar(sp_t[:, 4], sp_t[:, 5], -1.0, None, ALU.mult).then_inc(coef_ready, 1)

            def lambda_dots():
                dve.wait_ge(lam_in_sem, 64)
                for n in range(2):
                    step(nc.vector.tensor_tensor_reduce(
                        out=lam_in[:, 2 * n], in0=lam_in[:, 2 * n], in1=lam_in[:, 2 * n + 1], scale=1.0,
                        scalar=0.0, op0=ALU.mult, op1=ALU.add, accum_out=tiny[:, n:n + 1]))
                nc.vector.tensor_copy(tiny[:, 8:9], tiny[:, 0:1]).then_inc(lam_dots, 1)

            def lambda_value():
                dve.wait_ge(lam_exps, 1)
                step(nc.vector.tensor_tensor(tiny[:, 4:5], tiny[:, 3:4], tiny[:, 2:3], ALU.subtract))
                step(nc.vector.tensor_scalar(tiny[:, 5:6], tiny[:, 4:5], -LAM_INIT, None, ALU.add))
                step(nc.vector.memset(gcol[:, 0:HEADS], 1.0))
                step(nc.vector.tensor_scalar(gcol[:, HEADS:KD], vecT[:, 0, 96:104], 1.0 - LAM_INIT, None,
                                             ALU.mult))

            def window_halves(kind):
                dve.wait_ge(turn_used, named["kvcs"].turn0 + 2)
                if kind:
                    dve.wait_ge(z_done, 1)
                for half in range(2):
                    for g in range(2):
                        src = cmpT[:, 2 * kind + g, CSTR * half:CSTR * half + NCMP * CSTR]
                        pe_l = vecT[:, 2, 32 * kind + CSTR * half:32 * kind + CSTR * (half + 1)]
                        ins = nc.vector.tensor_tensor(
                            cz[:, half, g].rearrange("p (n l) -> p n l", l=CSTR),
                            src.rearrange("p (n l) -> p n l", l=CSTR),
                            pe_l.unsqueeze(1).to_broadcast([P, NCMP, CSTR]), ALU.add)
                ins.then_inc(cz_ready, 1)

            def compressed_shift():
                dve.wait_ge(c_scored, 1)
                for m in range(NT):
                    step(nc.vector.tensor_tensor(
                        sc_s[:, 8 * m:8 * m + 8, 0:NCMP],
                        ps[:, EX + 1, 128 * m:128 * m + 128].rearrange("p (a n) -> p a n", n=16)[:, :, 0:NCMP],
                        maskc[:, m, 0:NCMP].unsqueeze(1).to_broadcast([P, HEADS, NCMP]), ALU.add))
                step(nc.vector.tensor_reduce(csum[:, 0], sc_s[:, :, 0:NCMP], AX_X, ALU.max))
                nc.vector.tensor_tensor(sc_s[:, :, 0:NCMP], sc_s[:, :, 0:NCMP],
                                        csum[:, 0].unsqueeze(2).to_broadcast([P, 16, NCMP]), ALU.subtract
                                        ).then_inc(c_shift, 1)

            def compressed_weights():
                dve.wait_ge(c_exp, 1)
                step(nc.vector.tensor_reduce(csum[:, 1], sc_s[:, :, 0:NCMP], AX_X, ALU.add))
                for m in range(NT):
                    ins = nc.vector.tensor_tensor(
                        sc_s[:, 8 * m:8 * m + 8, 0:NCMP], sc_s[:, 8 * m:8 * m + 8, 0:NCMP],
                        validc[:, m, 0:NCMP].unsqueeze(1).to_broadcast([P, HEADS, NCMP]), ALU.mult)
                ins.then_inc(c_prob, 1)
                step(nc.vector.reciprocal(csum[:, 2], csum[:, 1]))

            def compressed_gate():
                dve.wait_ge(evac["a"], named["kvwg"].v0["a"] + 1)
                for m in range(NT):
                    step(nc.vector.tensor_tensor(csum[:, 3, 8 * m:8 * m + 8], csum[:, 2, 8 * m:8 * m + 8],
                                                 g3[:, m, :, 0], ALU.mult))

            def compressed_out(b):
                dve.wait_ge(c_pv, b + 1)
                for a in range(4):
                    mh = 4 * b + a
                    m, hd = divmod(mh, HEADS)
                    ins = nc.vector.tensor_scalar(o_all[:, m, hd * P:(hd + 1) * P],
                                                  ps[:, EX + 1, a * P:(a + 1) * P], csum[:, 3, mh:mh + 1],
                                                  None, ALU.mult)
                ins.then_inc(c_out, 1)

            def softmin_unit(u):
                dve.wait_ge(scored, u + 1)
                if u >= 2:
                    dve.wait_ge(pT_made, u - 1)
                for n, cols in enumerate(unit_parts(u)):
                    m = n if u < 16 else u % NT
                    mask = maskd[:].rearrange("p b t -> p (b t)")[:, (0, P)[m]:(P, 3 * P)[m]]
                    ins = nc.vector.tensor_tensor_reduce(
                        out=prob[:, u % 2, cols], in0=ps[:, EX, cols], in1=mask,
                        scale=-(HD if u < 16 else DQK) ** -0.5, scalar=BIGF,
                        op0=ALU.add, op1=ALU.min, accum_out=nmax[:, u % 2, n:n + 1])
                ins.then_inc(softmin, 1)

            def weights_unit(u):
                dve.wait_ge(expd, u + 1)
                b, c4 = u % 2, u % 4
                step(nc.vector.reciprocal(coef[:, c4], esum[:, b]))
                if u < 16:
                    branch, hd = 1 + u // HEADS, u % HEADS
                    nc.vector.tensor_tensor(coef[:, c4], coef[:, c4], g3[:, :, hd, branch],
                                            ALU.mult).then_inc(prob_ready, 1)
                    return
                c0, c1 = unit_parts(u)
                n = c0.stop
                step(nc.vector.tensor_scalar(prob2[:, 0:n], prob[:, b, c1], coef[:, c4, 1:2], tiny[:, 5:6],
                                             ALU.mult, ALU.mult))
                nc.vector.scalar_tensor_tensor(out=prob[:, b, c0], in0=prob[:, b, c0], scalar=coef[:, c4, 0:1],
                                               in1=prob2[:, 0:n], op0=ALU.mult, op1=ALU.add
                                               ).then_inc(prob_ready, 1)

            def out_unit(v):
                dve.wait_ge(pv_done, v + 1)
                if v < 16:
                    dve.wait_ge(prob_ready, v + 1)
                    if v >= HEADS:
                        dve.wait_ge(o_done, v - HEADS + 1)
                    else:
                        dve.wait_ge(c_out, 4)
                for m in range(NT):
                    acc = ps[:, EX + 1, m * P:(m + 1) * P] if v < 20 else \
                        ps[:, EX + 1 - v % 2, m * P:(m + 1) * P]
                    if v < 16:
                        o = o_all[:, m, (v % HEADS) * P:(v % HEADS + 1) * P]
                        ins = nc.vector.scalar_tensor_tensor(out=o, in0=acc, scalar=coef[:, v % 4, m:m + 1],
                                                             in1=o, op0=ALU.mult, op1=ALU.add)
                    else:
                        o = o_all[:, m, (v - HEADS) * P:(v - HEADS + 1) * P]
                        ins = nc.vector.tensor_copy(o, acc)
                ins.then_inc(o_done, 1)

            def norm_heads(g):
                dve.wait_ge(b_sq, NT * 4 * (g + 1))
                r4 = rstdb[:, :, 4 * g:4 * g + 4]
                nc.vector.tensor_scalar(r4, ssqb[:, :, 4 * g:4 * g + 4], 1.0 / HD, EPS, ALU.mult, ALU.add
                                        ).then_inc(b_ms, 1)
                dve.wait_ge(b_rms, g + 1)
                step(nc.vector.reciprocal(r4, r4))
                for hd in range(4 * g, 4 * g + 4):
                    for m in range(NT):
                        o = o_all[:, m, (HEADS + hd) * P:(HEADS + hd + 1) * P]
                        ins = nc.vector.tensor_scalar(o, o, rstdb[:, m, hd:hd + 1], None, ALU.mult)
                ins.then_inc(o_ready, 1)

            def attention(t):
                if t == AT_SOFTPLUS:
                    softplus_argument()
                if t == AT_SOFTPLUS + 1:
                    softplus()
                if t == AT_LAM:
                    lambda_dots()
                if t == AT_LAM + 1:
                    lambda_value()
                if t in AT_CZ:
                    window_halves(AT_CZ.index(t))
                if t == AT_W2:
                    dve.wait_ge(w2_done, 1)
                    nc.vector.tensor_copy(kcT[:, :, 0:NCMP],
                                          ps[:, EX, 0:2 * NCMP].rearrange("p (g n) -> p g n", g=2))
                    nc.vector.tensor_copy(vc[0:NCMP],
                                          ps[0:NCMP, EX, S:2 * S].rearrange("p (g d) -> p g d", g=2)
                                          ).then_inc(kv_cmp, 1)
                if t == AT_CSCORE:
                    compressed_shift()
                if t == AT_CSCORE + 1:
                    compressed_weights()
                if t == AT_CT + 1:
                    compressed_gate()
                if AT_CT + 1 <= t < AT_CT + 5:
                    compressed_out(t - AT_CT - 1)
                if (u := unit_at(t, 0)) is not None:
                    softmin_unit(u)
                if (u := unit_at(t, 1)) is not None:
                    weights_unit(u)
                if (u := unit_at(t, 3)) is not None and u < 16:
                    out_unit(u)
                for grp, heads in heads_at(t):
                    for hd in heads:
                        out_unit(16 + hd)
                if t in AT_NORM:
                    norm_heads(AT_NORM.index(t))
                for c in AT_OUT.get(t, ()):
                    turn_split(X["B"], 4 * c, named["out0"].hi0 - 8 + 2 * c, lambda kt: gcol[:, kt:kt + 1])

            def griffin(t):
                n, off = divmod(t - AT_GATE - 1, 4)
                if off == 0 and 0 <= n < NBLK:
                    dve.wait_ge(r_sig, n + 1)
                    x2 = xc[:, 2 * n:2 * n + 2]
                    nc.vector.tensor_tensor(x2, x2, i_t[:, n % 2], ALU.mult).then_inc(i_used, 1)
                g, off = divmod(t - AT_SQRT, 8)
                t4 = slice(4 * g, 4 * g + 4)
                if off == 0 and 0 <= g < 4:
                    dve.wait_ge(r_exp, g + 1)
                    step(nc.vector.tensor_tensor(xbT[:, t4, 0:S], decay[:, t4], decay[:, t4], ALU.mult))
                    nc.vector.scalar_tensor_tensor(out=th[:, t4], in0=xbT[:, t4, 0:S], scalar=1.0, in1=th[:, t4],
                                                   op0=ALU.add, op1=ALU.mult).then_inc(r_m, 1)
                g, off = divmod(t - AT_SCAN, 8)
                t4 = slice(4 * g, 4 * g + 4)
                if off == 0 and 0 <= g < 4:
                    dve.wait_ge(r_sqrt, g + 1)
                    dve.wait_ge(i_used, 2 * g + 2)
                    step(nc.vector.tensor_tensor(xc[:, t4], xbT[:, t4, 0:S], xc[:, t4], ALU.mult))
                    for f in range(4 * g, 4 * g + 4):
                        ins = nc.vector.tensor_tensor_scan(xbT[:, f, 0:S], decay[:, f], xc[:, f], 0.0,
                                                           ALU.mult, ALU.add)
                    ins.then_inc(r_scan, 1)
                if t in AT_PROD:
                    g = AT_PROD[t]
                    t4 = slice(4 * g, 4 * g + 4)
                    dve.wait_ge(r_scan, g + 1)
                    dve.wait_ge(turn_used, named["yb"].turn0 + 2 * (g + 1))
                    nc.vector.tensor_tensor(xc[:, t4], xbT[:, t4, 0:S], yT[:, t4], ALU.mult).then_inc(r_h, 1)
                if t in AT_SPLIT:
                    g = AT_SPLIT[t]
                    t4 = slice(4 * g, 4 * g + 4)
                    dve.wait_ge(r_hi, g + 1)
                    nc.vector.tensor_tensor(X["B"][1][:, t4], xc[:, t4], X["B"][0][:, t4].bitcast(F32),
                                            ALU.subtract).then_inc(r_lo, 1)

            dve.wait_ge(vec_turned, 1)
            nc.vector.tensor_copy(vecT[:].rearrange("p a b -> p (a b)"), ps[:, 0, 0:3 * P]).then_inc(vec_ready, 1)
            dve.wait_ge(vec_ready, 1)
            dve.wait_ge(consts, 1)
            for c in range(4):
                turn_split(X["B"], 4 * c, 2 * c, lambda kt: gain_ap(0, kt))
            mean_square(0)
            run(dve, run_chunk, after)

        @block.tensor
        def _(pe):
            units_turned = 0
            banks_turned = 0

            def transpose4(src, t0, tiles=4):
                if units_turned:
                    pe.wait_ge(pT_ready, units_turned)
                for f in range(tiles):
                    b = f // 2
                    if f % 2 == 0 and not (isinstance(t0, int) and t0 + b < 2):
                        pe.wait_ge(turn_used, t0 + (b - 1))
                    for m in range(NT):
                        bank = (t0 + b) % 2 if isinstance(t0, int) else b
                        o = ps[:, TP + bank, (f % 2) * S + m * P:(f % 2) * S + (m + 1) * P]
                        ins = nc.tensor.transpose(o, src(m, f), ident[:])
                    if f % 2 == 1:
                        ins.then_inc(turned, 1)

            def multiply_slot(q, i, r, j):
                t = slot_no(q, i, r, j)
                s = j % NRING
                k0, nk, c0, w = slot_shape(q, r, j)
                pe.wait_ge(lo_ready, t + 1)
                if j == 0:
                    pre = two_before(q, i, r)
                    if pre:
                        e, n = evac_no(*pre)
                        pe.wait_ge(evac[e], n)
                ple_p = is_proj(q, j)
                if ple_p:
                    if j == 4:
                        pe.wait_ge(p_ready, 1)
                        if 2 * i + r:
                            pe.wait_ge(evac["v"], evac_no(q, i, r)[1] - 1)
                    layer = int(q.name[3])
                    xh, xl = pT_hi[:, layer], pT_lo[:, layer]
                else:
                    xh, xl = X[q.src]
                if q.first_turn and isinstance(i, int) and i == 0 and r == 0 and not ple_p:
                    if q.name == "out1":
                        pe.wait_ge(r_lo, j // 2 + 1)
                    else:
                        pe.wait_ge(turn_used, src_turn0(q) + bank_of_ktile(q, j) + 1)
                nkt = 2 if ple_p else (KF if q.slots[r] == 24 else KD)
                for m in range(NT):
                    o = ps[:, EX + m if ple_p else 2 * r + m, c0:c0 + w]
                    for k in range(k0, k0 + nk):
                        tok = slice(m * P, (m + 1) * P)
                        wk = slice((k - k0) * w, (k - k0 + 1) * w)
                        nc.tensor.matmul(o, xh[:, k, tok], w_hi[:, s, wk], start=(k == 0), stop=False)
                        nc.tensor.matmul(o, xh[:, k, tok], w_lo[:, s, wk], start=False, stop=False)
                        ins = nc.tensor.matmul(o, xl[:, k, tok], w_hi[:, s, wk], start=False,
                                               stop=(k == nkt - 1))
                ins.then_inc(w_used, 1)

            def turn(q, i, r):
                nonlocal banks_turned
                k = q.kinds[r]
                if not k.banks:
                    return
                e, n = evac_no(q, i, r)
                pe.wait_ge(evac[e], n)
                t0 = turn_no(q, i, r)
                banks_turned = t0 + k.banks
                if k.name in ("resid", "ple"):
                    c = 2 * i + r
                    transpose4(lambda m, f: h[:, m, c * CW + f * P:c * CW + (f + 1) * P], t0)
                else:
                    transpose4(lambda m, f: stage[:, m, f * P:(f + 1) * P], t0, tiles=2 * k.banks)

            def run_chunk(q, i, r, prev):
                for j in range(q.slots[r]):
                    multiply_slot(q, i, r, j)
                    if prev and j == 3:
                        turn(*prev)
                    if q.norm == 0 or q.name == "out0":
                        attention(slot_no(q, i, r, j))
                    if q.norm == 3 or q.name == "out1":
                        griffin(slot_no(q, i, r, j) - named["xb"].slot0)
                    if q.name == "out0" and i == 1 and r == 1 and j == 5:
                        pe.wait_ge(p_in, 32)
                        pe.wait_ge(o_done, 24)
                        for layer in range(2):
                            for k in range(2):
                                for m in range(NT):
                                    ins = nc.tensor.transpose(
                                        ps[:, EX + layer, k * S + m * P:k * S + (m + 1) * P],
                                        p_tok[:, layer, m, k * P:(k + 1) * P], ident[:])
                        ins.then_inc(p_turned, 1)

            def after(prev):
                turn(*prev)

            def compress(kind):
                pe.wait_ge(w1_in[kind], 16)
                pe.wait_ge(cz_ready, kind + 1)
                for l in range(2 * CSTR):
                    x30 = cz[:, l // CSTR].rearrange("p g (n l) -> p g n l", l=CSTR)[:, :, :, l % CSTR]
                    ins = nc.tensor.matmul(ps[:, EX + kind, 0:2 * NCMP].rearrange("p (g n) -> p g n", g=2),
                                           w1[:, l], x30, start=(l == 0), stop=(l == 2 * CSTR - 1))
                ins.then_inc(z_done, 1)

            def compress_out():
                pe.wait_ge(w2_in, 32)
                pe.wait_ge(gelu_done, 2)
                nc.tensor.matmul(ps[:, EX, 0:2 * NCMP], w2[:, 0], gz[:, 0, 0:2 * NCMP], start=True, stop=True)
                for g in range(2):
                    ins = nc.tensor.matmul(ps[0:NCMP, EX, S + g * HD:S + (g + 1) * HD],
                                           gz[:, 1, g * NCMP:(g + 1) * NCMP], w2[:, 1], start=True, stop=True)
                ins.then_inc(w2_done, 1)

            def compressed_scores():
                pe.wait_ge(kv_cmp, 1)
                for m in range(NT):
                    for hd in range(HEADS):
                        mh = HEADS * m + hd
                        ins = nc.tensor.matmul(ps[:, EX + 1, 16 * mh:16 * mh + NCMP], qaT[:, hd, m * P:(m + 1) * P],
                                               kcT[:, hd // KVG, 0:NCMP], start=True, stop=True)
                ins.then_inc(c_scored, 1)

            def compressed_turn(b):
                pe.wait_ge(c_prob, 1)
                if b:
                    pe.wait_ge(c_Tr, b)
                for a in range(4):
                    ins = nc.tensor.matmul(ps[0:NCMP, EX, a * P:(a + 1) * P], sc_s[:, 4 * b + a, 0:NCMP],
                                           ident[:], start=True, stop=True)
                ins.then_inc(c_T, 1)

            def compressed_value(b):
                pe.wait_ge(c_Tr, b + 1)
                if b:
                    pe.wait_ge(c_out, b)
                for a in range(4):
                    g = ((4 * b + a) % HEADS) // KVG
                    ins = nc.tensor.matmul(ps[:, EX + 1, a * P:(a + 1) * P], pc_T[0:NCMP, b % 2, a],
                                           vc[0:NCMP, g], start=True, stop=True)
                ins.then_inc(c_pv, 1)

            def score_unit(u):
                if u:
                    pe.wait_ge(softmin, u)
                else:
                    pe.wait_ge(c_Tr, 4)
                if u in (0, 16, 24):
                    pe.wait_ge(turn_used, banks_turned)
                for n, cols in enumerate(unit_parts(u)):
                    m = n if u < 16 else u % NT
                    if u < 16:
                        q_t, k_t = qaT[:, u % HEADS], kT[:, u // HEADS, (u % HEADS) // KVG]
                    else:
                        rows = slice(DQK * n, DQK * (n + 1))
                        q_t, k_t = qbT[rows, (u - 16) // NT], kbT[rows, (u - 16) // NT]
                    ins = nc.tensor.matmul(ps[:, EX, cols], q_t[:, m * P:(m + 1) * P], k_t[:, 0:(m + 1) * P],
                                           start=True, stop=True)
                    if u >= 16 and n == 0:
                        ins.then_inc(map0_scored, 1)
                        pe.wait_ge(map0_scored, u - 15)
                ins.then_inc(scored, 1)

            def turn_unit(u):
                nonlocal units_turned
                units_turned += 1
                pe.wait_ge(prob_ready, u + 1)
                pe.wait_ge(turn_used, banks_turned)
                if u >= 2:
                    pe.wait_ge(pT_ready, u - 1)
                for b in range(3 if u < 16 else u % NT + 1):
                    ins = nc.tensor.transpose(ps[:, TP + u % 2, b * P:(b + 1) * P],
                                              prob[:, u % 2, b * P:(b + 1) * P], ident[:])
                ins.then_inc(pT_made, 1)

            def value_unit(v):
                bank = EX + 1 if v < 20 else EX + 1 - v % 2
                if v < 16:
                    pe.wait_ge(pT_ready, v + 1)
                    c = ((v % HEADS) // KVG) * HD
                    val = [vtok[:, v // HEADS, m, c:c + HD] for m in range(NT)]
                    pt = probT[:, v % 2]
                else:
                    pe.wait_ge(pT_ready, 16 + NT * (v - 15))
                    val = [vb_tok[:, m, (v - 16) * P:(v - 15) * P] for m in range(NT)]
                    pt = probTd[:, v - 16]
                    pe.wait_ge(evac["v"], named["vb"].v0["v"] + (v - 16) // 4 + 1)
                if v == 0:
                    pe.wait_ge(c_out, 4)
                elif v <= 20:
                    pe.wait_ge(o_done, v)
                else:
                    pe.wait_ge(o_done, v - 1)
                o = ps[:, bank, :]
                nc.tensor.matmul(o[:, 0:P], pt[:, 0:P], val[0], start=True, stop=True)
                nc.tensor.matmul(o[:, P:S], pt[:, P:2 * P], val[0], start=True, stop=False)
                nc.tensor.matmul(o[:, P:S], pt[:, 2 * P:3 * P], val[1], start=False, stop=True
                                 ).then_inc(pv_done, 1)

            def attention(t):
                if t in AT_Z:
                    compress(AT_Z.index(t))
                if t == AT_W2:
                    compress_out()
                if t == AT_CSCORE:
                    compressed_scores()
                if AT_CT + 1 <= t < AT_CT + 5:
                    compressed_value(t - AT_CT - 1)
                if AT_CT <= t < AT_CT + 4:
                    compressed_turn(t - AT_CT)
                if (u := unit_at(t, 3)) is not None and u < 16:
                    value_unit(u)
                if (u := unit_at(t, 2)) is not None:
                    turn_unit(u)
                if (u := unit_at(t, 0)) is not None:
                    score_unit(u)
                for grp, heads in heads_at(t):
                    for hd in heads:
                        value_unit(16 + hd)
                for c in AT_OUT.get(t, ()):
                    if c >= 2:
                        pe.wait_ge(o_ready, c - 1)
                    pe.wait_ge(o_done, 16)
                    transpose4(lambda m, f: o_all[:, m, c * CW + f * P:c * CW + (f + 1) * P],
                               named["out0"].turn0 - 8 + 2 * c)

            def griffin(t):
                n, off = divmod(t - AT_GATE, 4)
                if off or not 0 <= n < NBLK:
                    return
                pe.wait_ge(lru_in, 32)
                pe.wait_ge(conv_step, 1 + 4 * (n // 2 + 1))
                if n:
                    pe.wait_ge(r_sig, n)
                else:
                    pe.wait_ge(evac["v"], named["xb"].v0["v"])
                for g in range(2):
                    for e in range(2):
                        for k in range(2):
                            ins = nc.tensor.matmul(ps[:, EX + g, e * S:(e + 1) * S],
                                                   lru_w[:, g, n, k, e * P:(e + 1) * P], xc[:, 2 * n + k],
                                                   start=(k == 0), stop=(k == 1))
                ins.then_inc(r_mm, 1)

            pe.wait_ge(consts, 1)
            pe.wait_ge(vec_in, 16 * 11)
            for a in range(3):
                ins = nc.tensor.transpose(ps[:, 0, a * P:(a + 1) * P], vrow[:, a], ident[:])
            ins.then_inc(vec_turned, 1)
            for c in range(4):
                pe.wait_ge(x_in[c], 16)
                transpose4(lambda m, f: h[:, m, c * CW + f * P:c * CW + (f + 1) * P], 2 * c)
            pe.wait_ge(vec_ready, 1)
            run(pe, run_chunk, after)


def unit_parts(u):
    if u < 16:
        return slice(0, P), slice(P, 3 * P)
    n = P * (u % NT + 1)
    return slice(0, n), slice(n, 2 * n)


def heads_at(t):
    if AT_VALUE[0] <= t < AT_VALUE[0] + 4:
        return ((0, (t - AT_VALUE[0],)),)
    if AT_VALUE[1] <= t < AT_VALUE[1] + 2:
        h0 = 4 + 2 * (t - AT_VALUE[1])
        return ((1, (h0, h0 + 1)),)
    return ()


def dma_no(t, s):
    return (t - s) * (16 // NRING) + 16


def src_turn0(q):
    if q.name == "qa":
        return 0
    if q.name == "out0":
        return q.turn0 - 8
    b = q.before
    return q.turn0 - b.per_turn * b.pairs


_INS = ["x", "p", "g_mix", "g_ffn", "g_ple", "g_final", "w_in_attn", "cmp_pe_k", "cmp_w1_k", "cmp_w2_k",
        "cmp_pe_v", "cmp_w1_v", "cmp_w2_v", "diff_lq1", "diff_lk1", "diff_lq2", "diff_lk2", "diff_subln",
        "w_out_attn", "w_in_rec", "conv_w", "conv_b", "lru_wa", "lru_ba", "lru_wx", "lru_bx",
        "lru_lambda", "w_out_rec", "w_ffn_gate", "w_ffn_up", "w_ffn_down", "w_ple_proj", "w_ple_gate"]
_OUTS = [((1, 256, 2048), "float32")]


def kernel(**inputs):
    import numpy as _np
    import concourse.bacc as _bacc
    from concourse import mybir as _mybir
    from concourse.bass_utils import run_bass_kernel_spmd as _run

    nc = _bacc.Bacc("TRN2", target_bir_lowering=False, num_devices=1)
    arrays, args = {}, []
    for name in _INS:
        a = _np.ascontiguousarray(inputs[name])
        arrays[f"in_{name}_dram"] = a
        args.append(nc.dram_tensor(f"in_{name}_dram", a.shape, _mybir.dt.from_np(a.dtype), kind="ExternalInput").ap())
    for i, (shape, dtype) in enumerate(_OUTS):
        dt = _mybir.dt.from_np(_np.dtype(dtype))
        args.append(nc.dram_tensor(f"out_{i}_dram", shape, dt, kind="ExternalOutput").ap())
    trunk(nc, *args)
    r = _run(nc, [arrays], core_ids=[0])
    got = tuple(r.results[0][f"out_{i}_dram"] for i in range(len(_OUTS)))
    return got[0]
```

```python
from contextlib import ExitStack
import math

import numpy as np

import concourse.bass as bass
from concourse import mybir

F32 = mybir.dt.float32
F32R = mybir.dt.float32r
BF16 = mybir.dt.bfloat16
ALU = mybir.AluOpType
ACT = mybir.ActivationFunctionType
AX_X = mybir.AxisListType.X

P = 128
NT = 2
S = NT * P
D = 2048
KD = D // P
DFF = 5632
KF = DFF // P
CW = 512
EPS = 1e-6
PLE = 256
NRING = 4

HEADS = 8
KVG = 4
HD = 128
NCMP = 15
CSTR = 16
DQK = 64
Q_A, KV_A, G_A = 0, 1024, 2560
Q_B, K_B, V_B = 2584, 3608, 4632
NGATE = 24
NEG = -1e30
BIGF = 3e38
LAM_INIT = 0.8 - 0.6 * math.exp(-0.3 * 0)
LRU_C = 8.0
NBLK = 8
XPAD = 260


class Kind:

    def __init__(self, name, evac, banks=0, split=False):
        self.name, self.evac, self.banks, self.split = name, evac, banks, split


class Phase:

    def __init__(self, name, pairs, slots, kinds, src, cols, weight, first_turn=None, loop=False,
                 gain=None, dst=None, norm=None, stat=None):
        self.name, self.pairs, self.slots, self.kinds = name, pairs, slots, kinds
        self.src, self.cols, self.weight, self.loop = src, cols, weight, loop
        self.first_turn = first_turn
        self.gain, self.dst = gain, dst
        self.norm = norm
        self.stat = stat


def build_phases():
    resid = Kind("resid", "v", 2, True)
    ph = []

    def attn(name, kinds, cols, first=False, slots=(8, 8)):
        ph.append(Phase(name, 1, slots, kinds, "B", cols, ("w_in_attn", "w_in_attn"),
                        first_turn=first, norm=0))

    qk = Kind("qk", "a", 2)
    vb = Kind("vb", "v")
    attn("qa", (qk, qk), (Q_A, Q_A + CW), first=True)
    attn("gkvc", (Kind("gates", "v", 2), Kind("kvc", "v", 2)), (G_A, KV_A), slots=(4, 8))
    attn("kvsw", (Kind("kvs", "v", 1), Kind("kvw", "v", 1)), (KV_A + CW, KV_A + 2 * CW))
    attn("qk0", (qk, qk), (Q_B, K_B))
    attn("qk1", (qk, qk), (Q_B + CW, K_B + CW))
    attn("vb", (vb, vb), (V_B, V_B + CW))
    for layer in range(2):
        if layer:
            ph.append(Phase("xb", 2, (8, 8), (Kind("xb", "v", 2),) * 2, "B", (0, CW),
                            ("w_in_rec",) * 2, first_turn=True, norm=3))
            ph.append(Phase("yb", 2, (8, 8), (Kind("yb", "a", 2),) * 2, "B", (D, D + CW),
                            ("w_in_rec",) * 2, norm=3))
        ph.append(Phase(f"out{layer}", 2, (8, 8), (resid, resid), "B", (0, CW),
                        (("w_out_attn", "w_out_rec")[layer],) * 2, first_turn=True,
                        gain=2 + layer, dst="A", stat=1 + 3 * layer))
        ph.append(Phase(f"ffn{layer}", 11, (8, 8), (Kind("gate", "a"), Kind("up", "v", 2, True)), "A",
                        (0, 0), (f"w_gate{layer}", f"w_up{layer}"), first_turn=True, loop=True,
                        dst="H", norm=1 + 3 * layer))
        ph.append(Phase(f"down{layer}", 2, (22, 22), (resid, resid), "H", (0, CW),
                        (f"w_down{layer}",) * 2, first_turn=True, gain=4 + layer, dst="A",
                        stat=2 + 3 * layer))
        last = layer == 1
        ple = Kind("ple", "v", 0 if last else 2, True)
        ph.append(Phase(f"ple{layer}", 2, (9, 9), (ple, ple), "A",
                        (0, CW), (f"w_ple_gate{layer}",) * 2, first_turn=True,
                        gain=None if last else 1, dst=None if last else "B", norm=2 + 3 * layer,
                        stat=6 if last else 3))
    slot, va, turn, hi = 0, {"v": 0, "a": 0}, 8, 8
    for p in ph:
        if p.name == "out0":
            turn, hi = turn + 8, hi + 8
        p.slot0, p.v0, p.turn0, p.hi0 = slot, dict(va), turn, hi
        p.per_slot = sum(p.slots)
        p.per_turn = sum(k.banks for k in p.kinds)
        p.per_hi = sum(k.banks for k in p.kinds if k.split)
        p.per_v = {e: sum(k.evac == e for k in p.kinds) for e in "va"}
        slot += p.per_slot * p.pairs
        turn += p.per_turn * p.pairs
        hi += p.per_hi * p.pairs
        for e in "va":
            va[e] += p.per_v[e] * p.pairs
    for a, b in zip([None] + ph[:-1], ph):
        b.before = a
    return ph


def slot_no(p, i, r, j):
    return i * p.per_slot + (p.slot0 + r * p.slots[0] + j)


def chunk_end(p, i, r):
    return slot_no(p, i, r, p.slots[r])


def evac_no(p, i, r):
    e = p.kinds[r].evac
    before = sum(k.evac == e for k in p.kinds[:r])
    return e, i * p.per_v[e] + (p.v0[e] + before + 1)


def turn_no(p, i, r):
    return i * p.per_turn + (p.turn0 + sum(k.banks for k in p.kinds[:r]))


def hi_no(p, i, r):
    return i * p.per_hi + (p.hi0 + sum(k.banks for k in p.kinds[:r] if k.split))


def two_before(p, i, r):
    if isinstance(i, int) and i == 0:
        return (p.before, p.before.pairs - 1, r) if p.before else None
    return (p, i - 1, r)


def slot_shape(p, r, j):
    if is_proj(p, j):
        return 0, 2, 0, CW
    if p.slots[r] == 4:
        return 4 * j, 4, 0, NGATE
    return 2 * j, 2, 0, CW


def is_proj(p, j):
    return p.slots[0] == 9 and j == 8


def ring_place(t, j):
    return (t if isinstance(t, int) else j) % NRING


def bank_of_ktile(p, j):
    k0, nk, _, _ = slot_shape(p, 0, j)
    return (k0 + nk - 1) // 2


AT_SOFTPLUS, AT_LAM = 10, 12
AT_GATES = 28
AT_CZ, AT_Z, AT_W2, AT_CSCORE = 31, (32, 36), 41, 42
AT_CT = 45
AT_UNIT = [t for t in range(49, 76) if (t + 2) % 8 != 7] + [*range(81, 89)]
AT_VALUE = (85, 92)
AT_NORM = (90, 94)
AT_OUT = {91: (0,), 92: (1,), 93: (2,), 96: (3,)}
AT_GATE = 20
AT_EXP, AT_SQRT, AT_SCAN = 26, 28, 30
AT_PROD = {44: 0, 52: 1, 60: 2, 67: 3}
AT_SPLIT = {59: 0, 61: 1, 63: 2, 67: 3}


def unit_at(t, lag):
    return AT_UNIT.index(t - lag) if t - lag in AT_UNIT else None


def trunk(nc, x, p, g_mix, g_ffn, g_ple, g_final, w_in_attn, cmp_pe_k, cmp_w1_k, cmp_w2_k,
          cmp_pe_v, cmp_w1_v, cmp_w2_v, diff_lq1, diff_lk1, diff_lq2, diff_lk2, diff_subln,
          w_out_attn, w_in_rec, conv_w, conv_b, lru_wa, lru_ba, lru_wx, lru_bx, lru_lambda,
          w_out_rec, w_ffn_gate, w_ffn_up, w_ffn_down, w_ple_proj, w_ple_gate, out):
    phases = build_phases()
    named = {q.name: q for q in phases}
    ctx = ExitStack()
    with ctx:
        base = (nc.sbuf_base + 63) // 64 * 64
        size = nc.sbuf_usable_end - 64 - base
        ctx.enter_context(nc.sbuf_tensor("slab", [P, size - 64], mybir.dt.uint8))
        top = [base]

        def at(name, shape, dt, offset):
            return nc.alloc_sbuf_tensor_at(name, [P, *shape], dt, offset=offset)

        def put(name, shape, dt=F32):
            n = int(np.prod(shape)) * (2 if dt == BF16 else 4)
            t = at(name, shape, dt, top[0])
            top[0] += (n + 31) // 32 * 32
            return t

        h = put("h", [NT, D])
        raw = put("raw", [NRING, 2 * CW])
        w_hi = put("w_hi", [NRING, 2 * CW], F32R)
        w_lo = put("w_lo", [NRING, 2 * CW], F32R)
        stage = put("stage", [NT, CW])
        sg = put("sg", [NT, CW])
        junk = put("junk", [CW], BF16)
        pT_off = top[0]
        pT_hi = put("pT_hi", [2, 2, S], F32R)
        pT_lo = put("pT_lo", [2, 2, S], F32R)
        vecT = put("vecT", [3, P])
        ident = put("ident", [P])
        maskd = put("maskd", [3, P])
        maskc = put("maskc", [NT, 16])
        validc = put("validc", [NT, 16])
        gates_sb = put("gates_sb", [NT, NGATE])
        gcol = put("gcol", [KD])
        ssq = put("ssq", [7, NT, 4])
        rstd = put("rstd", [7, NT])
        tiny = put("tiny", [16])
        nmax = put("nmax", [2, NT])
        esum = put("esum", [2, NT])
        coef = put("coef", [4, NT])
        kcT = put("kcT", [2, 16])
        csum = put("csum", [4, 16])
        ssqb = put("ssqb", [NT, HEADS])
        rstdb = put("rstdb", [NT, HEADS])
        sp_t = put("sp_t", [6, KD])
        a_off = top[0]
        big = a_off + 2 * KD * S * 4
        s_off = big + 2 * KD * S * 4
        assert big + 2 * KF * S * 4 <= base + size - 64, (big + 2 * KF * S * 4, base + size)
        X = {"A": (at("xa_hi", [KD, S], F32R, a_off), at("xa_lo", [KD, S], F32R, a_off + KD * S * 4)),
             "B": (at("xb_hi", [KD, S], F32R, big), at("xb_lo", [KD, S], F32R, big + KD * S * 4)),
             "H": (at("hid_hi", [KF, S], F32R, big), at("hid_lo", [KF, S], F32R, big + KF * S * 4))}
        vrow = at("vrow", [3, P], F32, s_off + 28672)
        gmix = at("gmix", [P], F32, s_off + 28672 + 3 * P * 4)
        p_tok = at("p_tok", [2, NT, PLE], F32, s_off)
        qaT = at("qaT", [HEADS, S], F32, a_off)
        qbT = at("qbT", [HEADS, S], F32, a_off + 8192)
        w1 = [at("w1_k", [32, HD], F32, a_off + 16384),
              at("w1_v", [32, HD], F32, s_off + 28672)]
        probTd = at("probTd", [HEADS, 3 * P], F32, a_off + 16384)
        kbT = at("kbT", [HEADS, S], F32, s_off)
        vtok = at("vtok", [2, NT, 2 * HD], F32, s_off + 8192)
        vb_tok = at("vb_tok", [NT, 2 * CW], F32, s_off + 12288)
        kT = at("kT", [2, 2, S], F32, s_off + 20480)
        cmpT = at("cmpT", [4, S], F32, s_off + 24576)
        o_all = at("o_all", [NT, D], F32, s_off + 28672)
        w2 = at("w2", [2, HD], F32, s_off + 45056)
        lam_in = at("lam_in", [4, DQK], F32, s_off + 46080)
        cz = [at("cz_k", [2, 2, NCMP * CSTR], F32, s_off + 47104),
              at("cz_v", [2, 2, NCMP * CSTR], F32, s_off)]
        pc_T = at("pc_T", [2, 4, P], F32, s_off + 50944)
        vc = at("vc", [2, HD], F32, s_off + 55040)
        sc_s = at("sc_s", [16, 16], F32, s_off + 56064)
        gz = at("gz", [2, 2 * NCMP + 2], F32, s_off + 57088)
        prob = at("prob", [2, CW], F32, pT_off)
        prob2 = at("prob2", [S], F32, pT_off + 4096)
        probT = at("probT", [2, 3 * P], F32, pT_off + 5120)
        lru_w = at("lru_w", [2, NBLK, 2, 2 * P], F32, a_off)
        decay = at("decay", [KD, S], F32, a_off)
        th = at("th", [KD, S], F32, a_off + KD * S * 4)
        xbT = at("xbT", [KD, XPAD], F32, s_off)
        xc = at("xc", [KD, S], F32, s_off + KD * XPAD * 4)
        yT = at("yT", [KD, S], F32, s_off + KD * XPAD * 4 + KD * S * 4)
        i_t = at("i_t", [2, 2, S], F32, s_off + KD * XPAD * 4 + 2 * KD * S * 4)
        gf = at("gf", [D], F32, s_off)
        fin = at("fin", [NT, D], F32, s_off + 8192)

        ps = ctx.enter_context(nc.psum_tensor("ps", [P, 8, CW], F32))
        TP, EX = 4, 6

        def sem(name):
            return ctx.enter_context(nc.semaphore(name))

        x_in = [sem(f"x_in{c}") for c in range(4)]
        vec_in = sem("vec_in")
        p_in = sem("p_in")
        raw_in = [sem(f"raw_in{s}") for s in range(NRING)]
        hi_ready, lo_ready, w_used = sem("hi_ready"), sem("lo_ready"), sem("w_used")
        evac = {"v": sem("evac_v"), "a": sem("evac_a")}
        turned, turn_hi, turn_used = sem("turned"), sem("turn_hi"), sem("turn_used")
        consts, ident_ready, gmix_in = sem("consts"), sem("ident_ready"), sem("gmix_in")
        pool_step = sem("pool_step")
        vrow_clear = sem("vrow_clear")
        sg_ready = sem("sg_ready")
        vec_turned, vec_ready = sem("vec_turned"), sem("vec_ready")
        p_turned, p_hi, p_ready = sem("p_turned"), sem("p_hi"), sem("p_ready")
        gcol_ready = sem("gcol_ready")
        ssq_ready, ms_ready, rms_ready, rstd_ready = (sem("ssq_ready"), sem("ms_ready"),
                                                      sem("rms_ready"), sem("rstd_ready"))
        dve_step = sem("dve_step")
        ple_step = sem("ple_step")
        w1_in, w2_in, lam_in_sem = [sem("w1_in_k"), sem("w1_in_v")], sem("w2_in"), sem("lam_in")
        gates_ready = sem("gates_ready")
        map0_scored = sem("map0_scored")
        scored, softmin, expd, prob_ready = sem("scored"), sem("softmin"), sem("expd"), sem("prob_ready")
        pT_made, pT_ready, pv_done, o_done = sem("pT_made"), sem("pT_ready"), sem("pv_done"), sem("o_done")
        cz_ready, z_done, gelu_done, w2_done, kv_cmp = (sem("cz_ready"), sem("z_done"), sem("gelu_done"),
                                                        sem("w2_done"), sem("kv_cmp"))
        c_scored, c_shift, c_exp, c_prob = sem("c_scored"), sem("c_shift"), sem("c_exp"), sem("c_prob")
        c_T, c_Tr, c_pv, c_out = sem("c_T"), sem("c_Tr"), sem("c_pv"), sem("c_out")
        lam_dots, lam_exps = sem("lam_dots"), sem("lam_exps")
        sp_arg, sp_exp = sem("sp_arg"), sem("sp_exp")
        b_sq, b_ms, b_rms, o_ready = sem("b_sq"), sem("b_ms"), sem("b_rms"), sem("o_ready")
        conv_step = sem("conv_step")
        lru_in = sem("lru_in")
        r_mm, r_sig, i_used = sem("r_mm"), sem("r_sig"), sem("i_used")
        r_exp, r_m, r_sqrt, r_h, r_hi, r_lo = (sem("r_exp"), sem("r_m"), sem("r_sqrt"), sem("r_h"),
                                               sem("r_hi"), sem("r_lo"))
        coef_ready, r_scan = sem("coef_ready"), sem("r_scan")
        ple_half, fin_part = sem("ple_half"), sem("fin_part")
        gf_in, fin_ready, stored = sem("gf_in"), [sem("fin_ready_v"), sem("fin_ready_a")], sem("stored")

        W = {"w_in_attn": w_in_attn[0], "w_out_attn": w_out_attn[0], "w_in_rec": w_in_rec[0],
             "w_out_rec": w_out_rec[0]}
        for layer in range(2):
            W[f"w_gate{layer}"] = w_ffn_gate[layer]
            W[f"w_up{layer}"] = w_ffn_up[layer]
            W[f"w_down{layer}"] = w_ffn_down[layer]
            W[f"w_ple_gate{layer}"] = w_ple_gate[layer]
            W[f"w_ple_proj{layer}"] = w_ple_proj[layer]
        W = {k: v.rearrange("(k p) n -> p k n", p=P) for k, v in W.items()}

        GAIN = {0: 0, 1: 16, 3: 48, 4: 64, 5: 80}

        def gain_ap(g, k):
            return vecT[:, 0, k + 16 * g:k + 16 * g + 1]


        def walk(run_chunk, after):
            prev = None
            for q in phases:
                run_chunk(q, 0, 0, prev)
                run_chunk(q, 0, 1, (q, 0, 0))
                prev = (q, q.pairs - 1, 1)
                if q.loop:
                    yield q, run_chunk
                else:
                    for i in range(1, q.pairs):
                        run_chunk(q, i, 0, (q, i - 1, 1))
                        run_chunk(q, i, 1, (q, i, 0))
            after(prev)

        def run(eng, run_chunk, after):
            for q, step in walk(run_chunk, after):
                with eng.Fori(1, q.pairs) as i:
                    step(q, i, 0, (q, i - 1, 1))
                    step(q, i, 1, (q, i, 0))

        block = ctx.enter_context(nc.Block())

        @block.sync
        def _(sp):
            def load_slot(q, i, r, j):
                t = slot_no(q, i, r, j)
                s = ring_place(t, j)
                k0, nk, c0, w = slot_shape(q, r, j)
                if not (isinstance(t, int) and t < NRING):
                    sp.wait_ge(lo_ready, t - (NRING - 1))
                col = q.cols[r] + c0 + i * (CW if q.loop else 2 * CW)
                weight = q.weight[r].replace("gate", "proj") if is_proj(q, j) else q.weight[r]
                src = W[weight][:, k0:k0 + nk, bass.ds(col, w)]
                dst = raw[:, s, 0:nk * w].rearrange("p (k n) -> p k n", k=nk)
                sp.dma_start(dst, src).then_inc(raw_in[s], 16)

            def load_vectors():
                sp.wait_ge(vrow_clear, 1)
                for dst, src in ((vrow[32:64, 0], g_ffn.rearrange("a (k p) -> (a k) p", p=P)),
                                 (vrow[64:96, 0], g_ple.rearrange("a (k p) -> (a k) p", p=P)),
                                 (vrow[96:104, 0], diff_subln[0]),
                                 (vrow[0:64, 1], conv_w[0].rearrange("a (k p) -> (a k) p", p=P)),
                                 (vrow[64:80, 1], conv_b[0].rearrange("(k p) -> k p", p=P)),
                                 (vrow[80:96, 1], lru_ba[0].rearrange("(k p) -> k p", p=P)),
                                 (vrow[96:112, 1], lru_bx[0].rearrange("(k p) -> k p", p=P)),
                                 (vrow[112:128, 1], lru_lambda[0].rearrange("(k p) -> k p", p=P)),
                                 (vrow[0:32, 2], cmp_pe_k[0]),
                                 (vrow[32:64, 2], cmp_pe_v[0])):
                    sp.dma_start(dst, src).then_inc(vec_in, 16)

            def run_chunk(q, i, r, prev):
                for j in range(q.slots[r]):
                    if q.name == "qa" and r == 0 and j == 4:
                        load_vectors()
                    if q.name == "qa" and r == 0 and j < 4:
                        sp.dma_start(h[:, :, j * CW:(j + 1) * CW],
                                     x[0].rearrange("(m p) d -> p m d", p=P)[:, :, j * CW:(j + 1) * CW]
                                     ).then_inc(x_in[j], 16)
                    load_slot(q, i, r, j)
                if q.name == "qa" and r == 1:
                    sp.dma_start(w1[0][:], cmp_w1_k[0].rearrange("l d e -> d l e")).then_inc(w1_in[0], 16)
                    sp.dma_start(w2[:, 0, :], cmp_w2_k[0]).then_inc(w2_in, 16)
                    sp.dma_start(w2[:, 1, :], cmp_w2_v[0]).then_inc(w2_in, 16)
                    for n, v in enumerate((diff_lq1, diff_lk1, diff_lq2, diff_lk2)):
                        sp.dma_start(lam_in[:, n, :], v[0].partition_broadcast(P)).then_inc(lam_in_sem, 16)
                if q.name == "gkvc" and r == 1:
                    sp.wait_ge(vec_turned, 2)
                    sp.dma_start(w1[1][:], cmp_w1_v[0].rearrange("l d e -> d l e")).then_inc(w1_in[1], 16)
                if q.name == "out0" and i == 0 and r == 1:
                    sp.wait_ge(scored, 32)
                    for layer in range(2):
                        sp.dma_start(p_tok[:, layer], p[layer, 0].rearrange("(m p) e -> p m e", p=P)
                                     ).then_inc(p_in, 16)
                if q.name == "xb" and i == 0 and r == 1:
                    sp.wait_ge(w_used, q.slot0)
                    for n, w in enumerate((lru_wa, lru_wx)):
                        sp.dma_start(lru_w[:, n], w[0].rearrange("b (k p) e -> p b k e", p=P)
                                     ).then_inc(lru_in, 16)
                if q.name == "ple1" and i == 0 and r == 1:
                    sp.wait_ge(w_used, q.slot0)
                    sp.dma_start(gf[:], g_final.partition_broadcast(P)).then_inc(gf_in, 16)

            def after(prev):
                for n in range(4):
                    half, m = divmod(n, NT)
                    cols = slice(half * D // 2, (half + 1) * D // 2)
                    sp.wait_ge(fin_ready[m], half + 1)
                    sp.dma_start(out[0].rearrange("(m p) d -> p m d", p=P)[:, m, cols], fin[:, m, cols]
                                 ).then_inc(stored, 16)
                sp.wait_ge(stored, 16 * 4)

            run(sp, run_chunk, after)

        @block.gpsimd
        def _(pool):
            n = 0

            def step(ins):
                nonlocal n
                n += 1
                ins.then_inc(pool_step, 1)
                pool.wait_ge(pool_step, n)

            step(nc.gpsimd.memset(ident[:], 0.0))
            nc.gpsimd.affine_select(out=ident[:], in_=ident[:], compare_op=ALU.not_equal, fill=1.0,
                                    base=0, pattern=[[-1, P]], channel_multiplier=1).then_inc(ident_ready, 1)
            nc.gpsimd.memset(vrow[:], 0.0).then_inc(vrow_clear, 1)
            step(nc.gpsimd.memset(maskd[:], 0.0))
            step(nc.gpsimd.memset(maskc[:], 0.0))
            step(nc.gpsimd.memset(validc[:], 1.0))
            for b in (0, 2):
                step(nc.gpsimd.affine_select(out=maskd[:, b], in_=maskd[:, b], compare_op=ALU.is_ge,
                                             fill=NEG, base=0, pattern=[[-1, P]], channel_multiplier=1))
            for t, fill in ((maskc, NEG), (validc, 0.0)):
                for m in range(NT):
                    step(nc.gpsimd.affine_select(out=t[:, m], in_=t[:, m], compare_op=ALU.is_ge,
                                                 fill=fill, base=m * P - (2 * CSTR - 1),
                                                 pattern=[[-CSTR, 16]], channel_multiplier=1))
            nc.gpsimd.memset(tiny[:], 0.0).then_inc(consts, 1)

        @block.scalar
        def _(act):
            def split_slot(q, i, r, j):
                t = slot_no(q, i, r, j)
                s = ring_place(t, j)
                _, nk, _, w = slot_shape(q, r, j)
                n = nk * w
                act.wait_ge(raw_in[s], dma_no(t, s))
                if not (isinstance(t, int) and t < NRING):
                    act.wait_ge(w_used, t - (NRING - 1))
                nc.scalar.activation(w_hi[:, s, 0:n], raw[:, s, 0:n], ACT.Copy).then_inc(hi_ready, 1)

            def evacuate(q, i, r):
                kind = q.kinds[r].name
                if q.kinds[r].evac != "a" and kind != "ple":
                    return
                act.wait_ge(w_used, chunk_end(q, i, r) - (kind == "ple"))
                act.wait_ge(rstd_ready, q.norm + 1)
                for m in range(NT):
                    acc = ps[:, 2 * r + m, :]
                    rs = rstd[:, q.norm, m:m + 1]
                    if kind == "gate":
                        if m == 0 and not (isinstance(i, int) and i == 0):
                            act.wait_ge(evac["v"], evac_no(q, i - 1, 1)[1])
                        ins = nc.scalar.activation(sg[:, m], acc, ACT.Silu, scale=rs)
                    elif kind == "ple":
                        if m == 0 and 2 * i + r > 0:
                            act.wait_ge(evac["v"], evac_no(q, i, r)[1] - 1)
                        ins = nc.scalar.activation(sg[:, m], acc, ACT.Sigmoid, scale=rs)
                    else:
                        if m == 0:
                            act.wait_ge(turned, turn_no(q, i, r))
                        ins = nc.scalar.activation(stage[:, m], acc, ACT.Copy if kind == "qk" else
                                                   ACT.Gelu_apprx_tanh, scale=rs)
                ins.then_inc(sg_ready if kind == "ple" else evac["a"], 1)

            def turn_split(dst, k0, t0, gain):
                for b in range(2):
                    act.wait_ge(turned, t0 + (b + 1))
                    for f in range(2):
                        o = dst[0][:, k0 + 2 * b + f, :] if isinstance(k0, int) else \
                            dst[0][:, bass.ds(k0 + (2 * b + f), 1), :]
                        src = ps[:, TP + b, f * S:(f + 1) * S]
                        if gain is None:
                            ins = nc.scalar.activation(o, src, ACT.Copy)
                        else:
                            ins = nc.scalar.activation(o, src, ACT.Copy, scale=gain(k0 + 2 * b + f))
                    ins.then_inc(turn_hi, 1)

            def squares(stat, c, wait=None):
                for m in range(NT):
                    if wait:
                        act.wait_ge(*wait[m])
                    n = (4 * stat + c) * NT + m
                    if n:
                        act.wait_ge(ssq_ready, n)
                    nc.scalar.activation(junk[:], h[:, m, c * CW:(c + 1) * CW], ACT.Square,
                                         accum_out=ssq[:, stat, m, c:c + 1]).then_inc(ssq_ready, 1)

            def root(stat):
                act.wait_ge(ms_ready, stat + 1)
                nc.scalar.activation(rstd[:, stat], rstd[:, stat], ACT.Sqrt).then_inc(rms_ready, 1)

            def aftermath(q, i, r):
                k = q.kinds[r]
                col = i if q.loop else 2 * i + r
                if k.split and k.banks:
                    g = (lambda kt: gain_ap(q.gain, kt)) if q.gain is not None else None
                    turn_split(X[q.dst], 4 * col, turn_no(q, i, r), g)
                if q.stat is not None:
                    done = evac["v"], evac_no(q, i, r)[1]
                    first = (ple_half, 4 * (q.name == "ple1") + col + 1) if k.name == "ple" else done
                    squares(q.stat, col, (first, done))
                    if col == 3:
                        root(q.stat)

            def run_chunk(q, i, r, prev):
                if not prev:
                    return
                in_attention = q.norm == 0 or q.name == "out0"
                for j in range(q.slots[r]):
                    if j == 7 and in_attention:
                        aftermath(*prev)
                    if in_attention:
                        attention(slot_no(q, i, r, j) - NRING)
                    split_slot(q, i, r, j)
                    if j == 1 and prev[0].slots[prev[2]] == 4:
                        aftermath(*two_before(q, i, r))
                    if j == 7 and not in_attention:
                        aftermath(*prev)
                    if q.norm == 3 or q.name == "out1":
                        griffin(slot_no(q, i, r, j) - NRING - named["xb"].slot0)
                    if q.name == "qa" and j < 2:
                        for c in (2 * j, 2 * j + 1):
                            act.wait_ge(x_in[c], 16)
                            squares(0, c)
                    if q.name == "qa" and j == 2:
                        root(0)
                    if j == 3:
                        evacuate(*prev)
                    if q.name == "ffn0" and isinstance(i, int) and r == 0 and j == 1:
                        act.wait_ge(p_turned, 1)
                        for layer in range(2):
                            ins = nc.scalar.activation(
                                pT_hi[:, layer], ps[:, EX + layer, :].rearrange("p (k t) -> p k t", k=2), ACT.Copy)
                        ins.then_inc(p_hi, 1)

            def after(prev):
                evacuate(*prev)
                aftermath(*prev)
                act.wait_ge(fin_part, 4)
                act.wait_ge(rstd_ready, 7)
                for cols in (slice(0, D // 2), slice(D // 2, D)):
                    nc.scalar.activation(fin[:, 1, cols], fin[:, 1, cols], ACT.Copy,
                                         scale=rstd[:, 6, 1:2]).then_inc(fin_ready[1], 1)

            def attention(t):
                if t == AT_SOFTPLUS:
                    act.wait_ge(sp_arg, 1)
                    nc.scalar.activation(sp_t[:, 1], sp_t[:, 0], ACT.Exp, scale=-1.0).then_inc(sp_exp, 1)
                if t == AT_LAM:
                    act.wait_ge(lam_dots, 1)
                    nc.scalar.activation(tiny[:, 2:4], tiny[:, 0:2], ACT.Exp).then_inc(lam_exps, 1)
                if t == AT_GATES:
                    act.wait_ge(turn_used, turn_no(named["gkvc"], 0, 1))
                    nc.scalar.activation(gates_sb[:], gates_sb[:], ACT.Sigmoid).then_inc(gates_ready, 1)
                if t - 3 in AT_Z:
                    kind = AT_Z.index(t - 3)
                    act.wait_ge(z_done, kind + 1)
                    nc.scalar.activation(gz[:, kind, 0:2 * NCMP], ps[:, EX + kind, 0:2 * NCMP],
                                         ACT.Gelu_apprx_tanh).then_inc(gelu_done, 1)
                if t == AT_CSCORE + 1:
                    act.wait_ge(c_shift, 1)
                    nc.scalar.activation(sc_s[:, :, 0:NCMP], sc_s[:, :, 0:NCMP], ACT.Exp, scale=HD ** -0.5
                                         ).then_inc(c_exp, 1)
                if AT_CT <= t < AT_CT + 4:
                    b = t - AT_CT
                    act.wait_ge(c_T, b + 1)
                    if b >= 2:
                        act.wait_ge(c_pv, b - 1)
                    nc.scalar.activation(pc_T[0:NCMP, b % 2],
                                         ps[0:NCMP, EX, :].rearrange("p (a t) -> p a t", a=4),
                                         ACT.Copy).then_inc(c_Tr, 1)
                if (u := unit_at(t, 2)) is not None:
                    act.wait_ge(pT_made, u + 1)
                    if u < 16:
                        if u >= 2:
                            act.wait_ge(pv_done, u - 1)
                        o, n = probT[:, u % 2], 3 * P
                    else:
                        hd, m = divmod(u - 16, NT)
                        o = probTd[:, hd, (0, P)[m]:(P, 3 * P)[m]]
                        n = P * (m + 1)
                    nc.scalar.activation(o, ps[:, TP + u % 2, 0:n], ACT.Copy).then_inc(pT_ready, 1)
                if (u := unit_at(t, 0)) is not None:
                    act.wait_ge(softmin, u + 1)
                    for n, cols in enumerate(unit_parts(u)):
                        pr = prob[:, u % 2, cols]
                        ins = nc.scalar.activation(pr, pr, ACT.Exp, scale=-1.0, bias=nmax[:, u % 2, n:n + 1],
                                                   accum_out=esum[:, u % 2, n:n + 1])
                    ins.then_inc(expd, 1)
                for grp, heads in heads_at(t - 1):
                    for hd in heads:
                        act.wait_ge(o_done, 16 + hd + 1)
                        for m in range(NT):
                            n = NT * hd + m
                            if n:
                                act.wait_ge(b_sq, n)
                            nc.scalar.activation(junk[:, 0:P], o_all[:, m, (HEADS + hd) * P:(HEADS + hd + 1) * P],
                                                 ACT.Square, accum_out=ssqb[:, m, hd:hd + 1]).then_inc(b_sq, 1)
                if t in AT_NORM:
                    g = AT_NORM.index(t)
                    act.wait_ge(b_ms, g + 1)
                    r4 = rstdb[:, :, 4 * g:4 * g + 4]
                    nc.scalar.activation(r4, r4, ACT.Sqrt).then_inc(b_rms, 1)
                for c in AT_OUT.get(t, ()):
                    turn_split(X["B"], 4 * c, named["out0"].turn0 - 8 + 2 * c,
                               lambda kt: gcol[:, kt:kt + 1])

            def griffin(t):
                n, off = divmod(t - AT_GATE, 4)
                if off == 0 and 0 <= n < NBLK:
                    act.wait_ge(r_mm, n + 1)
                    if n >= 2:
                        act.wait_ge(i_used, n - 1)
                    for g in range(2):
                        for e in range(2):
                            f = 2 * n + e
                            o = xbT[:, f, 0:S] if g == 0 else i_t[:, n % 2, e]
                            ins = nc.scalar.activation(o, ps[:, EX + g, e * S:(e + 1) * S],
                                                       ACT.Sigmoid, bias=vecT[:, 1, 80 + 16 * g + f:81 + 16 * g + f])
                    ins.then_inc(r_sig, 1)
                g, off = divmod(t - AT_EXP, 8)
                if off == 0 and 0 <= g < 4:
                    act.wait_ge(coef_ready, 1)
                    act.wait_ge(r_sig, 2 * g + 2)
                    for f in range(4 * g, 4 * g + 4):
                        nc.scalar.activation(decay[:, f], xbT[:, f, 0:S], ACT.Exp, scale=sp_t[:, 4, f:f + 1])
                        ins = nc.scalar.activation(th[:, f], xbT[:, f, 0:S], ACT.Tanh, scale=sp_t[:, 5, f:f + 1])
                    ins.then_inc(r_exp, 1)
                g, off = divmod(t - AT_SQRT, 8)
                if off == 0 and 0 <= g < 4:
                    act.wait_ge(r_m, g + 1)
                    nc.scalar.activation(xbT[:, 4 * g:4 * g + 4, 0:S], th[:, 4 * g:4 * g + 4], ACT.Sqrt
                                         ).then_inc(r_sqrt, 1)
                if t in AT_SPLIT:
                    g = AT_SPLIT[t]
                    act.wait_ge(r_h, g + 1)
                    act.wait_ge(w_used, named["out1"].slot0 - 8 + 2 * g + 2)
                    nc.scalar.activation(X["B"][0][:, 4 * g:4 * g + 4], xc[:, 4 * g:4 * g + 4], ACT.Copy
                                         ).then_inc(r_hi, 1)

            act.dma_start(gmix[0:32], g_mix.rearrange("a (k p) -> (a k) p", p=P)).then_inc(gmix_in, 16)
            act.wait_ge(vec_ready, 1)
            for c in range(4):
                turn_split(X["B"], 4 * c, 2 * c, lambda kt: gain_ap(0, kt))
                for j in (2 * c, 2 * c + 1):
                    split_slot(named["qa"], 0, 0, j)
            run(act, run_chunk, after)

        @block.vector
        def _(dve):
            steps = 0

            def step(ins):
                nonlocal steps
                steps += 1
                ins.then_inc(dve_step, 1)
                dve.wait_ge(dve_step, steps)

            def split_slot(q, i, r, j):
                t = slot_no(q, i, r, j)
                s = ring_place(t, j)
                _, nk, _, w = slot_shape(q, r, j)
                n = nk * w
                dve.wait_ge(hi_ready, t + 1)
                nc.vector.tensor_tensor(w_lo[:, s, 0:n], raw[:, s, 0:n], w_hi[:, s, 0:n].bitcast(F32),
                                        ALU.subtract).then_inc(lo_ready, 1)

            def evacuate(q, i, r):
                k = q.kinds[r]
                kind = k.name
                if k.evac != "v":
                    return
                dve.wait_ge(w_used, chunk_end(q, i, r))
                if kind in ("gates", "kvc", "kvs", "kvw", "xb", "up"):
                    dve.wait_ge(turned, turn_no(q, i, r))
                if q.norm is not None and kind != "ple":
                    dve.wait_ge(rstd_ready, q.norm + 1)
                if kind == "gates":
                    nc.vector.tensor_copy(stage[0:NGATE, 0, 0:S], ps[0:NGATE, 2 * r, 0:S]
                                          ).then_inc(evac["v"], 1)
                    return
                if kind == "up":
                    dve.wait_ge(evac["a"], evac_no(q, i, 0)[1])
                if kind == "ple":
                    dve.wait_ge(sg_ready, 4 * (q.name == "ple1") + 2 * i + r + 1)
                for m in range(NT):
                    acc = ps[:, 2 * r + m, :]
                    rs = rstd[:, q.norm, m:m + 1] if q.norm is not None else None
                    if kind == "resid":
                        o = h[:, m, (2 * i + r) * CW:(2 * i + r + 1) * CW]
                        ins = nc.vector.tensor_tensor(o, acc, o, ALU.add)
                    elif kind == "ple":
                        c = 2 * i + r
                        nc.vector.tensor_tensor(stage[:, m], ps[:, EX + m, :], sg[:, m], ALU.mult
                                                ).then_inc(ple_step, 1)
                        dve.wait_ge(ple_step, 8 * (q.name == "ple1") + NT * c + m + 1)
                        o = h[:, m, c * CW:(c + 1) * CW]
                        ins = nc.vector.tensor_tensor(o, o, stage[:, m], ALU.add)
                        if m == 0:
                            ins.then_inc(ple_half, 1)
                    elif kind in ("kvs", "kvw"):
                        which = int(kind == "kvw")
                        nc.vector.tensor_scalar(vtok[:, which, m], acc[:, S:2 * S], rs, None, ALU.mult)
                        ins = nc.vector.tensor_scalar(stage[:, m, 0:S], acc[:, 0:S], rs, None, ALU.mult)
                    elif kind == "up":
                        ins = nc.vector.scalar_tensor_tensor(out=stage[:, m], in0=acc, scalar=rs, in1=sg[:, m],
                                                             op0=ALU.mult, op1=ALU.mult)
                    else:
                        o = {"xb": lambda: stage[:, m],
                             "kvc": lambda: stage[:, m],
                             "vb": lambda: vb_tok[:, m, r * CW:(r + 1) * CW]}[kind]()
                        ins = nc.vector.tensor_scalar(o, acc, rs, None, ALU.mult)
                ins.then_inc(evac["v"], 1)

            def turn_split(dst, k0, h0, gain):
                for b in range(2):
                    dve.wait_ge(turn_hi, h0 + (b + 1))
                    for f in range(2):
                        if isinstance(k0, int):
                            hi, lo = (dst[z][:, k0 + 2 * b + f, :] for z in range(2))
                        else:
                            hi, lo = (dst[z][:, bass.ds(k0 + (2 * b + f), 1), :] for z in range(2))
                        src = ps[:, TP + b, f * S:(f + 1) * S]
                        if gain is None:
                            ins = nc.vector.tensor_tensor(lo, src, hi.bitcast(F32), ALU.subtract)
                        else:
                            ins = nc.vector.scalar_tensor_tensor(
                                out=lo, in0=src, scalar=gain(k0 + 2 * b + f), in1=hi.bitcast(F32),
                                op0=ALU.mult, op1=ALU.subtract)
                    ins.then_inc(turn_used, 1)

            def mean_square(stat):
                dve.wait_ge(ssq_ready, 4 * NT * (stat + 1))
                step(nc.vector.tensor_reduce(rstd[:, stat], ssq[:, stat], AX_X, ALU.add))
                nc.vector.tensor_scalar(rstd[:, stat], rstd[:, stat], 1.0 / D, EPS, ALU.mult, ALU.add
                                        ).then_inc(ms_ready, 1)
                dve.wait_ge(rms_ready, stat + 1)
                nc.vector.reciprocal(rstd[:, stat], rstd[:, stat]).then_inc(rstd_ready, 1)
                dve.wait_ge(rstd_ready, stat + 1)

            def aftermath(q, i, r):
                k = q.kinds[r]
                col = i if q.loop else 2 * i + r
                t0 = turn_no(q, i, r)
                if k.split and k.banks:
                    g = (lambda kt: gain_ap(q.gain, kt)) if q.gain is not None else None
                    turn_split(X[q.dst], 4 * col, hi_no(q, i, r), g)
                elif k.banks:
                    for b in range(k.banks):
                        dve.wait_ge(turned, t0 + b + 1)
                        if k.name == "gates":
                            nc.vector.tensor_scalar(gates_sb[:, b], ps[:, TP + (t0 + b) % 2, 0:NGATE],
                                                    rstd[:, 0, b:b + 1], None, ALU.mult).then_inc(turn_used, 1)
                            continue
                        src = ps[:, TP + (t0 + b) % 2, :].rearrange("p (f t) -> p f t", f=2)
                        c = 4 * r + 2 * b
                        g = 4 * (q.name == "qk1") + 2 * b
                        o = {"qa": lambda: qaT[:, c:c + 2],
                             "qk0": lambda: (qbT, kbT)[r][:, g:g + 2], "qk1": lambda: (qbT, kbT)[r][:, g:g + 2],
                             "gkvc": lambda: cmpT[:, 2 * b:2 * b + 2], "kvsw": lambda: kT[:, r],
                             "xb": lambda: xbT[:, 8 * i + c:8 * i + c + 2, 3:3 + S],
                             "yb": lambda: yT[:, 8 * i + c:8 * i + c + 2]}[q.name]()
                        nc.vector.tensor_copy(o, src).then_inc(turn_used, 1)
                if k.name == "xb":
                    conv(2 * i + r)
                if q.stat is not None and col == 3:
                    mean_square(q.stat)

            def conv(c):
                dve.wait_ge(turn_used, named["xb"].turn0 + 2 * c + 2)
                for tap in range(4):
                    if tap:
                        dve.wait_ge(conv_step, 1 + 4 * c + tap)
                    for f in range(4 * c, 4 * c + 4):
                        src = xbT[:, f, 3 - tap:3 - tap + S]
                        w = vecT[:, 1, 16 * (3 - tap) + f:16 * (3 - tap) + f + 1]
                        if tap == 0:
                            ins = nc.vector.tensor_scalar(xc[:, f], src, w, vecT[:, 1, 64 + f:65 + f],
                                                          ALU.mult, ALU.add)
                        else:
                            ins = nc.vector.scalar_tensor_tensor(out=xc[:, f], in0=src, scalar=w, in1=xc[:, f],
                                                                 op0=ALU.mult, op1=ALU.add)
                    ins.then_inc(conv_step, 1)

            def run_chunk(q, i, r, prev):
                if not prev:
                    return
                in_attention = q.norm == 0 or q.name == "out0"
                for j in range(q.slots[r]):
                    if j == 7 and in_attention:
                        aftermath(*prev)
                    if in_attention:
                        attention(slot_no(q, i, r, j) - NRING)
                    split_slot(q, i, r, j)
                    if j == 1 and prev[0].slots[prev[2]] == 4:
                        aftermath(*two_before(q, i, r))
                    if j == 7 and not in_attention:
                        aftermath(*prev)
                    if q.name == "ple1" and i == 1 and r == 1 and 4 <= j < 7:
                        final_gain(j - 4)
                    if q.norm == 3 or q.name == "out1":
                        griffin(slot_no(q, i, r, j) - NRING - named["xb"].slot0)
                    if q.name == "qa" and j == 2:
                        mean_square(0)
                    if j == 3:
                        evacuate(*prev)
                    if q.name == "ffn0" and isinstance(i, int) and r == 0 and j == 1:
                        dve.wait_ge(p_hi, 1)
                        for layer in range(2):
                            ins = nc.vector.tensor_tensor(
                                pT_lo[:, layer], ps[:, EX + layer, :].rearrange("p (k t) -> p k t", k=2),
                                pT_hi[:, layer].bitcast(F32), ALU.subtract)
                        ins.then_inc(p_ready, 1)
                if q.name == "xb" and i == 0 and r == 0:
                    dve.wait_ge(turned, named["xb"].turn0)
                    nc.vector.memset(xbT[:, :, 0:3], 0.0).then_inc(conv_step, 1)
                    dve.wait_ge(conv_step, 1)

            def after(prev):
                evacuate(*prev)
                final_gain(3)
                aftermath(*prev)
                dve.wait_ge(fin_part, 4)
                for cols in (slice(0, D // 2), slice(D // 2, D)):
                    nc.vector.tensor_scalar(fin[:, 0, cols], fin[:, 0, cols], rstd[:, 6, 0:1], None,
                                            ALU.mult).then_inc(fin_ready[0], 1)

            def final_gain(c):
                cols = slice(c * CW, (c + 1) * CW)
                if c == 0:
                    dve.wait_ge(gf_in, 16)
                dve.wait_ge(evac["v"], evac_no(named["ple1"], c // 2, c % 2)[1])
                for m in range(NT):
                    ins = nc.vector.tensor_tensor(fin[:, m, cols], h[:, m, cols], gf[:, cols], ALU.mult)
                ins.then_inc(fin_part, 1)

            g3 = gates_sb[:, :, :].rearrange("p m (a b) -> p m a b", b=3)

            def softplus_argument():
                lam = vecT[:, 1, 112:128]
                step(nc.vector.tensor_scalar(sp_t[:, 2], lam, -1.0, None, ALU.mult))
                nc.vector.tensor_tensor(sp_t[:, 0], sp_t[:, 2], lam, ALU.max).then_inc(sp_arg, 1)

            def softplus():
                step(nc.vector.tensor_scalar(sp_t[:, 2], sp_t[:, 2], 0.0, None, ALU.max))
                dve.wait_ge(sp_exp, 1)
                step(nc.vector.tensor_scalar(sp_t[:, 3], sp_t[:, 1], 2.0, None, ALU.add))
                step(nc.vector.reciprocal(sp_t[:, 3], sp_t[:, 3]))
                step(nc.vector.tensor_tensor(sp_t[:, 1], sp_t[:, 1], sp_t[:, 3], ALU.mult))
                step(nc.vector.tensor_tensor(sp_t[:, 3], sp_t[:, 1], sp_t[:, 1], ALU.mult))
                step(nc.vector.tensor_scalar(sp_t[:, 4], sp_t[:, 3], 1.0 / 17, 1.0 / 15, ALU.mult, ALU.add))
                for n in range(13, 0, -2):
                    step(nc.vector.tensor_tensor(sp_t[:, 4], sp_t[:, 4], sp_t[:, 3], ALU.mult))
                    step(nc.vector.tensor_scalar(sp_t[:, 4], sp_t[:, 4], 1.0 / n, None, ALU.add))
                step(nc.vector.tensor_tensor(sp_t[:, 4], sp_t[:, 4], sp_t[:, 1], ALU.mult))
                step(nc.vector.tensor_scalar(sp_t[:, 4], sp_t[:, 4], 2.0, None, ALU.mult))
                step(nc.vector.tensor_tensor(sp_t[:, 5], sp_t[:, 4], sp_t[:, 2], ALU.add))
                step(nc.vector.tensor_scalar(sp_t[:, 5], sp_t[:, 5], LRU_C, None, ALU.mult))
                nc.vector.tensor_scalar(sp_t[:, 4], sp_t[:, 5], -1.0, None, ALU.mult).then_inc(coef_ready, 1)

            def lambda_dots():
                dve.wait_ge(lam_in_sem, 64)
                for n in range(2):
                    step(nc.vector.tensor_tensor_reduce(
                        out=lam_in[:, 2 * n], in0=lam_in[:, 2 * n], in1=lam_in[:, 2 * n + 1], scale=1.0,
                        scalar=0.0, op0=ALU.mult, op1=ALU.add, accum_out=tiny[:, n:n + 1]))
                nc.vector.tensor_copy(tiny[:, 8:9], tiny[:, 0:1]).then_inc(lam_dots, 1)

            def lambda_value():
                dve.wait_ge(lam_exps, 1)
                step(nc.vector.tensor_tensor(tiny[:, 4:5], tiny[:, 3:4], tiny[:, 2:3], ALU.subtract))
                step(nc.vector.tensor_scalar(tiny[:, 5:6], tiny[:, 4:5], -LAM_INIT, None, ALU.add))
                step(nc.vector.memset(gcol[:, 0:HEADS], 1.0))
                step(nc.vector.tensor_scalar(gcol[:, HEADS:KD], vecT[:, 0, 96:104], 1.0 - LAM_INIT, None,
                                             ALU.mult))

            def window_halves(kind):
                dve.wait_ge(turn_used, named["kvsw"].turn0)
                for half in range(2):
                    for g in range(2):
                        src = cmpT[:, 2 * kind + g, CSTR * half:CSTR * half + NCMP * CSTR]
                        pe_l = vecT[:, 2, 32 * kind + CSTR * half:32 * kind + CSTR * (half + 1)]
                        ins = nc.vector.tensor_tensor(
                            cz[kind][:, half, g].rearrange("p (n l) -> p n l", l=CSTR),
                            src.rearrange("p (n l) -> p n l", l=CSTR),
                            pe_l.unsqueeze(1).to_broadcast([P, NCMP, CSTR]), ALU.add)
                ins.then_inc(cz_ready, 1)

            def compressed_shift():
                dve.wait_ge(c_scored, 1)
                for m in range(NT):
                    step(nc.vector.tensor_tensor(
                        sc_s[:, 8 * m:8 * m + 8, 0:NCMP],
                        ps[:, EX + 1, 128 * m:128 * m + 128].rearrange("p (a n) -> p a n", n=16)[:, :, 0:NCMP],
                        maskc[:, m, 0:NCMP].unsqueeze(1).to_broadcast([P, HEADS, NCMP]), ALU.add))
                step(nc.vector.tensor_reduce(csum[:, 0], sc_s[:, :, 0:NCMP], AX_X, ALU.max))
                nc.vector.tensor_tensor(sc_s[:, :, 0:NCMP], sc_s[:, :, 0:NCMP],
                                        csum[:, 0].unsqueeze(2).to_broadcast([P, 16, NCMP]), ALU.subtract
                                        ).then_inc(c_shift, 1)

            def compressed_weights():
                dve.wait_ge(c_exp, 1)
                step(nc.vector.tensor_reduce(csum[:, 1], sc_s[:, :, 0:NCMP], AX_X, ALU.add))
                for m in range(NT):
                    ins = nc.vector.tensor_tensor(
                        sc_s[:, 8 * m:8 * m + 8, 0:NCMP], sc_s[:, 8 * m:8 * m + 8, 0:NCMP],
                        validc[:, m, 0:NCMP].unsqueeze(1).to_broadcast([P, HEADS, NCMP]), ALU.mult)
                ins.then_inc(c_prob, 1)
                step(nc.vector.reciprocal(csum[:, 2], csum[:, 1]))

            def compressed_gate():
                dve.wait_ge(gates_ready, 1)
                for m in range(NT):
                    step(nc.vector.tensor_tensor(csum[:, 3, 8 * m:8 * m + 8], csum[:, 2, 8 * m:8 * m + 8],
                                                 g3[:, m, :, 0], ALU.mult))

            def compressed_out(b):
                dve.wait_ge(c_pv, b + 1)
                for a in range(4):
                    mh = 4 * b + a
                    m, hd = divmod(mh, HEADS)
                    ins = nc.vector.tensor_scalar(o_all[:, m, hd * P:(hd + 1) * P],
                                                  ps[:, EX + 1, a * P:(a + 1) * P], csum[:, 3, mh:mh + 1],
                                                  None, ALU.mult)
                ins.then_inc(c_out, 1)

            def softmin_unit(u):
                dve.wait_ge(scored, u + 1)
                if u >= 2:
                    dve.wait_ge(pT_made, u - 1)
                for n, cols in enumerate(unit_parts(u)):
                    m = n if u < 16 else u % NT
                    mask = maskd[:].rearrange("p b t -> p (b t)")[:, (0, P)[m]:(P, 3 * P)[m]]
                    ins = nc.vector.tensor_tensor_reduce(
                        out=prob[:, u % 2, cols], in0=ps[:, EX, cols], in1=mask,
                        scale=-(HD if u < 16 else DQK) ** -0.5, scalar=BIGF,
                        op0=ALU.add, op1=ALU.min, accum_out=nmax[:, u % 2, n:n + 1])
                ins.then_inc(softmin, 1)

            def weights_unit(u):
                dve.wait_ge(expd, u + 1)
                b, c4 = u % 2, u % 4
                step(nc.vector.reciprocal(coef[:, c4], esum[:, b]))
                if u < 16:
                    branch, hd = 1 + u // HEADS, u % HEADS
                    nc.vector.tensor_tensor(coef[:, c4], coef[:, c4], g3[:, :, hd, branch],
                                            ALU.mult).then_inc(prob_ready, 1)
                    return
                c0, c1 = unit_parts(u)
                n = c0.stop
                step(nc.vector.tensor_scalar(prob2[:, 0:n], prob[:, b, c1], coef[:, c4, 1:2], tiny[:, 5:6],
                                             ALU.mult, ALU.mult))
                nc.vector.scalar_tensor_tensor(out=prob[:, b, c0], in0=prob[:, b, c0], scalar=coef[:, c4, 0:1],
                                               in1=prob2[:, 0:n], op0=ALU.mult, op1=ALU.add
                                               ).then_inc(prob_ready, 1)

            def out_unit(v):
                dve.wait_ge(pv_done, v + 1)
                if v < 16:
                    dve.wait_ge(prob_ready, v + 1)
                    if v >= HEADS:
                        dve.wait_ge(o_done, v - HEADS + 1)
                    else:
                        dve.wait_ge(c_out, 4)
                for m in range(NT):
                    acc = ps[:, EX + 1, m * P:(m + 1) * P] if v < 20 else \
                        ps[:, EX + 1 - v % 2, m * P:(m + 1) * P]
                    if v < 16:
                        o = o_all[:, m, (v % HEADS) * P:(v % HEADS + 1) * P]
                        ins = nc.vector.scalar_tensor_tensor(out=o, in0=acc, scalar=coef[:, v % 4, m:m + 1],
                                                             in1=o, op0=ALU.mult, op1=ALU.add)
                    else:
                        o = o_all[:, m, (v - HEADS) * P:(v - HEADS + 1) * P]
                        ins = nc.vector.tensor_copy(o, acc)
                ins.then_inc(o_done, 1)

            def norm_heads(g):
                dve.wait_ge(b_sq, NT * 4 * (g + 1))
                r4 = rstdb[:, :, 4 * g:4 * g + 4]
                nc.vector.tensor_scalar(r4, ssqb[:, :, 4 * g:4 * g + 4], 1.0 / HD, EPS, ALU.mult, ALU.add
                                        ).then_inc(b_ms, 1)
                dve.wait_ge(b_rms, g + 1)
                step(nc.vector.reciprocal(r4, r4))
                for hd in range(4 * g, 4 * g + 4):
                    for m in range(NT):
                        o = o_all[:, m, (HEADS + hd) * P:(HEADS + hd + 1) * P]
                        ins = nc.vector.tensor_scalar(o, o, rstdb[:, m, hd:hd + 1], None, ALU.mult)
                ins.then_inc(o_ready, 1)

            def attention(t):
                if t == AT_SOFTPLUS:
                    softplus_argument()
                if t == AT_SOFTPLUS + 1:
                    softplus()
                if t == AT_LAM:
                    lambda_dots()
                if t == AT_LAM + 1:
                    lambda_value()
                if t == AT_CZ:
                    window_halves(0)
                    window_halves(1)
                if t == AT_W2:
                    dve.wait_ge(w2_done, 1)
                    nc.vector.tensor_copy(kcT[:, :, 0:NCMP],
                                          ps[:, EX, 0:2 * NCMP].rearrange("p (g n) -> p g n", g=2))
                    nc.vector.tensor_copy(vc[0:NCMP],
                                          ps[0:NCMP, EX, S:2 * S].rearrange("p (g d) -> p g d", g=2)
                                          ).then_inc(kv_cmp, 1)
                if t == AT_CSCORE + 1:
                    compressed_shift()
                if t == AT_CSCORE + 2:
                    compressed_weights()
                if t == AT_CT:
                    compressed_gate()
                if AT_CT + 1 <= t < AT_CT + 5:
                    compressed_out(t - AT_CT - 1)
                new = unit_at(t, 0)
                if new is not None and new >= 16:
                    softmin_unit(new)
                if (u := unit_at(t, 1)) is not None:
                    weights_unit(u)
                if (u := unit_at(t, 3)) is not None and u < 16:
                    out_unit(u)
                if new is not None and new < 16:
                    softmin_unit(new)
                for grp, heads in heads_at(t):
                    for hd in heads:
                        out_unit(16 + hd)
                if t in AT_NORM:
                    norm_heads(AT_NORM.index(t))
                for c in AT_OUT.get(t, ()):
                    turn_split(X["B"], 4 * c, named["out0"].hi0 - 8 + 2 * c, lambda kt: gcol[:, kt:kt + 1])

            def griffin(t):
                n, off = divmod(t - AT_GATE - 1, 4)
                if off == 0 and 0 <= n < NBLK:
                    dve.wait_ge(r_sig, n + 1)
                    x2 = xc[:, 2 * n:2 * n + 2]
                    nc.vector.tensor_tensor(x2, x2, i_t[:, n % 2], ALU.mult).then_inc(i_used, 1)
                g, off = divmod(t - AT_SQRT, 8)
                t4 = slice(4 * g, 4 * g + 4)
                if off == 0 and 0 <= g < 4:
                    dve.wait_ge(r_exp, g + 1)
                    step(nc.vector.tensor_tensor(xbT[:, t4, 0:S], decay[:, t4], decay[:, t4], ALU.mult))
                    nc.vector.scalar_tensor_tensor(out=th[:, t4], in0=xbT[:, t4, 0:S], scalar=1.0, in1=th[:, t4],
                                                   op0=ALU.add, op1=ALU.mult).then_inc(r_m, 1)
                g, off = divmod(t - AT_SCAN, 8)
                t4 = slice(4 * g, 4 * g + 4)
                if off == 0 and 0 <= g < 4:
                    dve.wait_ge(r_sqrt, g + 1)
                    dve.wait_ge(i_used, 2 * g + 2)
                    step(nc.vector.tensor_tensor(xc[:, t4], xbT[:, t4, 0:S], xc[:, t4], ALU.mult))
                    for f in range(4 * g, 4 * g + 4):
                        ins = nc.vector.tensor_tensor_scan(xbT[:, f, 0:S], decay[:, f], xc[:, f], 0.0,
                                                           ALU.mult, ALU.add)
                    ins.then_inc(r_scan, 1)
                if t in AT_PROD:
                    g = AT_PROD[t]
                    t4 = slice(4 * g, 4 * g + 4)
                    dve.wait_ge(r_scan, g + 1)
                    dve.wait_ge(turn_used, named["yb"].turn0 + 2 * (g + 1))
                    nc.vector.tensor_tensor(xc[:, t4], xbT[:, t4, 0:S], yT[:, t4], ALU.mult).then_inc(r_h, 1)
                if t in AT_SPLIT:
                    g = AT_SPLIT[t]
                    t4 = slice(4 * g, 4 * g + 4)
                    dve.wait_ge(r_hi, g + 1)
                    nc.vector.tensor_tensor(X["B"][1][:, t4], xc[:, t4], X["B"][0][:, t4].bitcast(F32),
                                            ALU.subtract).then_inc(r_lo, 1)

            dve.wait_ge(vec_turned, 1)
            nc.vector.tensor_copy(vecT[:, 0, 0:32], ps[:, EX, 0:32]).then_inc(vec_ready, 1)
            dve.wait_ge(vec_ready, 1)
            for c in range(4):
                turn_split(X["B"], 4 * c, 2 * c, lambda kt: gain_ap(0, kt))
                for j in (2 * c, 2 * c + 1):
                    split_slot(named["qa"], 0, 0, j)
            dve.wait_ge(vec_turned, 2)
            nc.vector.tensor_copy(vecT[:].rearrange("p a b -> p (a b)")[:, 32:3 * P],
                                  ps[:, EX + 1, 32:3 * P]).then_inc(vec_ready, 1)
            dve.wait_ge(vec_ready, 2)
            dve.wait_ge(consts, 1)
            run(dve, run_chunk, after)

        @block.tensor
        def _(pe):
            units_turned = 0
            banks_turned = 0

            def transpose4(src, t0, tiles=4):
                if units_turned:
                    pe.wait_ge(pT_ready, units_turned)
                for f in range(tiles):
                    b = f // 2
                    if f % 2 == 0 and not (isinstance(t0, int) and t0 + b < 2):
                        pe.wait_ge(turn_used, t0 + (b - 1))
                    for m in range(NT):
                        bank = (t0 + b) % 2 if isinstance(t0, int) else b
                        o = ps[:, TP + bank, (f % 2) * S + m * P:(f % 2) * S + (m + 1) * P]
                        ins = nc.tensor.transpose(o, src(m, f), ident[:])
                    if f % 2 == 1:
                        ins.then_inc(turned, 1)

            def multiply_slot(q, i, r, j):
                t = slot_no(q, i, r, j)
                s = ring_place(t, j)
                k0, nk, c0, w = slot_shape(q, r, j)
                pe.wait_ge(lo_ready, t + 1)
                if j == 0:
                    pre = two_before(q, i, r)
                    if pre:
                        e, n = evac_no(*pre)
                        pe.wait_ge(evac[e], n)
                ple_p = is_proj(q, j)
                if ple_p:
                    pe.wait_ge(p_ready, 1)
                    if 2 * i + r:
                        pe.wait_ge(evac["v"], evac_no(q, i, r)[1] - 1)
                    layer = int(q.name[3])
                    xh, xl = pT_hi[:, layer], pT_lo[:, layer]
                else:
                    xh, xl = X[q.src]
                if q.first_turn and isinstance(i, int) and i == 0 and r == 0 and not ple_p:
                    if q.name == "out1":
                        pe.wait_ge(r_lo, j // 2 + 1)
                    else:
                        pe.wait_ge(turn_used, src_turn0(q) + bank_of_ktile(q, j) + 1)
                nkt = 2 if ple_p else (KF if q.src == "H" else KD)
                if q.kinds[r].name == "gates":
                    o = ps[0:NGATE, 2 * r, 0:S]
                    for k in range(k0, k0 + nk):
                        wk = slice((k - k0) * w, (k - k0 + 1) * w)
                        nc.tensor.matmul(o, w_hi[:, s, wk], xh[:, k], start=(k == 0), stop=False)
                        nc.tensor.matmul(o, w_lo[:, s, wk], xh[:, k], start=False, stop=False)
                        ins = nc.tensor.matmul(o, w_hi[:, s, wk], xl[:, k], start=False, stop=(k == nkt - 1))
                    ins.then_inc(w_used, 1)
                    return
                for m in range(NT):
                    o = ps[:, EX + m if ple_p else 2 * r + m, c0:c0 + w]
                    for k in range(k0, k0 + nk):
                        tok = slice(m * P, (m + 1) * P)
                        wk = slice((k - k0) * w, (k - k0 + 1) * w)
                        nc.tensor.matmul(o, xh[:, k, tok], w_hi[:, s, wk], start=(k == 0), stop=False)
                        nc.tensor.matmul(o, xh[:, k, tok], w_lo[:, s, wk], start=False, stop=False)
                        ins = nc.tensor.matmul(o, xl[:, k, tok], w_hi[:, s, wk], start=False,
                                               stop=(k == nkt - 1))
                ins.then_inc(w_used, 1)

            def turn(q, i, r):
                nonlocal banks_turned
                k = q.kinds[r]
                if not k.banks:
                    return
                e, n = evac_no(q, i, r)
                pe.wait_ge(evac[e], n)
                t0 = turn_no(q, i, r)
                banks_turned = t0 + k.banks
                if k.name == "gates":
                    for m in range(NT):
                        pe.wait_ge(turn_used, t0 + m - 1)
                        nc.tensor.transpose(ps[:, TP + (t0 + m) % 2, 0:NGATE], stage[0:NGATE, 0, m * P:(m + 1) * P],
                                            ident[0:NGATE, 0:NGATE]).then_inc(turned, 1)
                elif k.name in ("resid", "ple"):
                    c = 2 * i + r
                    transpose4(lambda m, f: h[:, m, c * CW + f * P:c * CW + (f + 1) * P], t0)
                else:
                    transpose4(lambda m, f: stage[:, m, f * P:(f + 1) * P], t0, tiles=2 * k.banks)

            def run_chunk(q, i, r, prev):
                for j in range(0 if prev else 6, q.slots[r]):
                    multiply_slot(q, i, r, j)
                    if prev and j == 3:
                        turn(*prev)
                    if q.norm == 0 or q.name == "out0":
                        attention(slot_no(q, i, r, j))
                    if q.norm == 3 or q.name == "out1":
                        griffin(slot_no(q, i, r, j) - named["xb"].slot0)
                    if q.name == "out0" and i == 1 and r == 1 and j == 5:
                        pe.wait_ge(p_in, 32)
                        pe.wait_ge(o_done, 24)
                        for layer in range(2):
                            for k in range(2):
                                for m in range(NT):
                                    ins = nc.tensor.transpose(
                                        ps[:, EX + layer, k * S + m * P:k * S + (m + 1) * P],
                                        p_tok[:, layer, m, k * P:(k + 1) * P], ident[:])
                        ins.then_inc(p_turned, 1)

            def after(prev):
                turn(*prev)

            def compress(kind, part):
                pe.wait_ge(w1_in[kind], 16)
                pe.wait_ge(cz_ready, kind + 1)
                for l in range(8 * part, 8 * part + 8):
                    x30 = cz[kind][:, l // CSTR].rearrange("p g (n l) -> p g n l", l=CSTR)[:, :, :, l % CSTR]
                    ins = nc.tensor.matmul(ps[:, EX + kind, 0:2 * NCMP].rearrange("p (g n) -> p g n", g=2),
                                           w1[kind][:, l], x30, start=(l == 0), stop=(l == 2 * CSTR - 1))
                if part == 3:
                    ins.then_inc(z_done, 1)

            def compress_out():
                pe.wait_ge(w2_in, 32)
                pe.wait_ge(gelu_done, 2)
                nc.tensor.matmul(ps[:, EX, 0:2 * NCMP], w2[:, 0], gz[:, 0, 0:2 * NCMP], start=True, stop=True)
                for g in range(2):
                    ins = nc.tensor.matmul(ps[0:NCMP, EX, S + g * HD:S + (g + 1) * HD],
                                           gz[:, 1, g * NCMP:(g + 1) * NCMP], w2[:, 1], start=True, stop=True)
                ins.then_inc(w2_done, 1)

            def compressed_scores(m):
                pe.wait_ge(kv_cmp, 1)
                for hd in range(HEADS):
                    mh = HEADS * m + hd
                    ins = nc.tensor.matmul(ps[:, EX + 1, 16 * mh:16 * mh + NCMP], qaT[:, hd, m * P:(m + 1) * P],
                                           kcT[:, hd // KVG, 0:NCMP], start=True, stop=True)
                if m == NT - 1:
                    ins.then_inc(c_scored, 1)

            def compressed_turn(b):
                pe.wait_ge(c_prob, 1)
                if b:
                    pe.wait_ge(c_Tr, b)
                for a in range(4):
                    ins = nc.tensor.matmul(ps[0:NCMP, EX, a * P:(a + 1) * P], sc_s[:, 4 * b + a, 0:NCMP],
                                           ident[:], start=True, stop=True)
                ins.then_inc(c_T, 1)

            def compressed_value(b):
                pe.wait_ge(c_Tr, b + 1)
                if b:
                    pe.wait_ge(c_out, b)
                for a in range(4):
                    g = ((4 * b + a) % HEADS) // KVG
                    ins = nc.tensor.matmul(ps[:, EX + 1, a * P:(a + 1) * P], pc_T[0:NCMP, b % 2, a],
                                           vc[0:NCMP, g], start=True, stop=True)
                ins.then_inc(c_pv, 1)

            def score_unit(u, part):
                if u < 16 and part == 0:
                    return
                if u >= 16 and part == 1:
                    pe.wait_ge(map0_scored, u - 15)
                elif u:
                    pe.wait_ge(softmin, u)
                else:
                    pe.wait_ge(c_Tr, 4)
                if u in (0, 16, 24):
                    pe.wait_ge(turn_used, banks_turned)
                for n, cols in enumerate(unit_parts(u)):
                    if u >= 16 and n != part:
                        continue
                    m = n if u < 16 else u % NT
                    if u < 16:
                        q_t, k_t = qaT[:, u % HEADS], kT[:, u // HEADS, (u % HEADS) // KVG]
                    else:
                        rows = slice(DQK * n, DQK * (n + 1))
                        q_t, k_t = qbT[rows, (u - 16) // NT], kbT[rows, (u - 16) // NT]
                    ins = nc.tensor.matmul(ps[:, EX, cols], q_t[:, m * P:(m + 1) * P], k_t[:, 0:(m + 1) * P],
                                           start=True, stop=True)
                ins.then_inc(scored if part else map0_scored, 1)

            def turn_unit(u):
                nonlocal units_turned
                units_turned += 1
                pe.wait_ge(prob_ready, u + 1)
                pe.wait_ge(turn_used, banks_turned)
                if u >= 2:
                    pe.wait_ge(pT_ready, u - 1)
                for b in range(3 if u < 16 else u % NT + 1):
                    ins = nc.tensor.transpose(ps[:, TP + u % 2, b * P:(b + 1) * P],
                                              prob[:, u % 2, b * P:(b + 1) * P], ident[:])
                ins.then_inc(pT_made, 1)

            def value_unit(v):
                bank = EX + 1 if v < 20 else EX + 1 - v % 2
                if v < 16:
                    pe.wait_ge(pT_ready, v + 1)
                    c = ((v % HEADS) // KVG) * HD
                    val = [vtok[:, v // HEADS, m, c:c + HD] for m in range(NT)]
                    pt = probT[:, v % 2]
                else:
                    pe.wait_ge(pT_ready, 16 + NT * (v - 15))
                    val = [vb_tok[:, m, (v - 16) * P:(v - 15) * P] for m in range(NT)]
                    pt = probTd[:, v - 16]
                    pe.wait_ge(evac["v"], named["vb"].v0["v"] + (v - 16) // 4 + 1)
                if v == 0:
                    pe.wait_ge(c_out, 4)
                elif v <= 20:
                    pe.wait_ge(o_done, v)
                else:
                    pe.wait_ge(o_done, v - 1)
                o = ps[:, bank, :]
                nc.tensor.matmul(o[:, 0:P], pt[:, 0:P], val[0], start=True, stop=True)
                nc.tensor.matmul(o[:, P:S], pt[:, P:2 * P], val[0], start=True, stop=False)
                nc.tensor.matmul(o[:, P:S], pt[:, 2 * P:3 * P], val[1], start=False, stop=True
                                 ).then_inc(pv_done, 1)

            def attention(t):
                for kind in range(2):
                    if AT_Z[kind] <= t < AT_Z[kind] + 4:
                        compress(kind, t - AT_Z[kind])
                if t == AT_W2:
                    compress_out()
                if AT_CSCORE <= t < AT_CSCORE + NT:
                    compressed_scores(t - AT_CSCORE)
                if AT_CT + 1 <= t < AT_CT + 5:
                    compressed_value(t - AT_CT - 1)
                if AT_CT <= t < AT_CT + 4:
                    compressed_turn(t - AT_CT)
                if (u := unit_at(t, 0)) is not None:
                    score_unit(u, 0)
                if (u := unit_at(t, 3)) is not None and u < 16:
                    value_unit(u)
                if (u := unit_at(t, 2)) is not None:
                    turn_unit(u)
                if (u := unit_at(t, 0)) is not None:
                    score_unit(u, 1)
                for grp, heads in heads_at(t):
                    for hd in heads:
                        value_unit(16 + hd)
                for c in AT_OUT.get(t, ()):
                    if c >= 2:
                        pe.wait_ge(o_ready, c - 1)
                    pe.wait_ge(o_done, 16)
                    transpose4(lambda m, f: o_all[:, m, c * CW + f * P:c * CW + (f + 1) * P],
                               named["out0"].turn0 - 8 + 2 * c)

            def griffin(t):
                n, off = divmod(t - AT_GATE, 4)
                if off or not 0 <= n < NBLK:
                    return
                pe.wait_ge(lru_in, 32)
                pe.wait_ge(conv_step, 1 + 4 * (n // 2 + 1))
                if n:
                    pe.wait_ge(r_sig, n)
                else:
                    pe.wait_ge(evac["v"], named["xb"].v0["v"])
                for g in range(2):
                    for e in range(2):
                        for k in range(2):
                            ins = nc.tensor.matmul(ps[:, EX + g, e * S:(e + 1) * S],
                                                   lru_w[:, g, n, k, e * P:(e + 1) * P], xc[:, 2 * n + k],
                                                   start=(k == 0), stop=(k == 1))
                ins.then_inc(r_mm, 1)

            pe.wait_ge(ident_ready, 1)
            pe.wait_ge(gmix_in, 16)
            nc.tensor.transpose(ps[:, EX, 0:32], gmix[0:32], ident[0:32, 0:32]).then_inc(vec_turned, 1)
            for c in range(4):
                pe.wait_ge(x_in[c], 16)
                transpose4(lambda m, f: h[:, m, c * CW + f * P:c * CW + (f + 1) * P], 2 * c)
                if c:
                    multiply_slot(named["qa"], 0, 0, 2 * c - 2)
                    multiply_slot(named["qa"], 0, 0, 2 * c - 1)
            pe.wait_ge(vec_in, 16 * 10)
            for a in range(3):
                ins = nc.tensor.transpose(ps[:, EX + 1, a * P:(a + 1) * P], vrow[:, a], ident[:])
            ins.then_inc(vec_turned, 1)
            run(pe, run_chunk, after)


def unit_parts(u):
    if u < 16:
        return slice(0, P), slice(P, 3 * P)
    n = P * (u % NT + 1)
    return slice(0, n), slice(n, 2 * n)


def heads_at(t):
    if AT_VALUE[0] <= t < AT_VALUE[0] + 4:
        return ((0, (t - AT_VALUE[0],)),)
    if AT_VALUE[1] <= t < AT_VALUE[1] + 2:
        h0 = 4 + 2 * (t - AT_VALUE[1])
        return ((1, (h0, h0 + 1)),)
    return ()


def dma_no(t, s):
    return (t - s) * (16 // NRING) + 16


def src_turn0(q):
    if q.name == "qa":
        return 0
    if q.name == "out0":
        return q.turn0 - 8
    b = q.before
    return q.turn0 - b.per_turn * b.pairs


_INS = ["x", "p", "g_mix", "g_ffn", "g_ple", "g_final", "w_in_attn", "cmp_pe_k", "cmp_w1_k", "cmp_w2_k",
        "cmp_pe_v", "cmp_w1_v", "cmp_w2_v", "diff_lq1", "diff_lk1", "diff_lq2", "diff_lk2", "diff_subln",
        "w_out_attn", "w_in_rec", "conv_w", "conv_b", "lru_wa", "lru_ba", "lru_wx", "lru_bx",
        "lru_lambda", "w_out_rec", "w_ffn_gate", "w_ffn_up", "w_ffn_down", "w_ple_proj", "w_ple_gate"]
_OUTS = [((1, 256, 2048), "float32")]


def kernel(**inputs):
    import numpy as _np
    import concourse.bacc as _bacc
    from concourse import mybir as _mybir
    from concourse.bass_utils import run_bass_kernel_spmd as _run

    nc = _bacc.Bacc("TRN2", target_bir_lowering=False, num_devices=1)
    arrays, args = {}, []
    for name in _INS:
        a = _np.ascontiguousarray(inputs[name])
        arrays[f"in_{name}_dram"] = a
        args.append(nc.dram_tensor(f"in_{name}_dram", a.shape, _mybir.dt.from_np(a.dtype), kind="ExternalInput").ap())
    for i, (shape, dtype) in enumerate(_OUTS):
        dt = _mybir.dt.from_np(_np.dtype(dtype))
        args.append(nc.dram_tensor(f"out_{i}_dram", shape, dt, kind="ExternalOutput").ap())
    trunk(nc, *args)
    r = _run(nc, [arrays], core_ids=[0])
    got = tuple(r.results[0][f"out_{i}_dram"] for i in range(len(_OUTS)))
    return got[0]
```
